# Optimizing a Trainium2 kernel written in Bass

```python
import math
import jax
import jax.numpy as jnp
from jax import lax
import numpy as np
import jax, jax.numpy as jnp

D_MODEL = 2048
BATCH = 1
SEQ = 256
DEPTH = 1

CHUNK = 64
Q_BLOCK = 128
HEAD_DIM = 64
N_HEADS_DIFF = D_MODEL // (4 * HEAD_DIM)
N_HEADS_SB = D_MODEL // (4 * HEAD_DIM)
N_HEADS_CH = D_MODEL // (4 * HEAD_DIM)
DIFF_WIDTH = N_HEADS_DIFF * 2 * HEAD_DIM
SB_WIDTH = N_HEADS_SB * HEAD_DIM
CH_WIDTH = N_HEADS_CH * HEAD_DIM
MIX_WIDTH = DIFF_WIDTH + SB_WIDTH + CH_WIDTH
QKV_WIDTH = 3 * MIX_WIDTH
LEFT_CHUNKS = 8
BAND = (LEFT_CHUNKS + 1) * CHUNK
MAX_REL = 128
N_REL = (CHUNK - 1) + MAX_REL + 1
D_FF = 5632
CONV_WIDTH = 3
NORM_EPS = 1e-6
SUBLN_EPS = 1e-5


def rmsnorm(x, g, eps=NORM_EPS):
    xf = x.astype(jnp.float32)
    y = xf * lax.rsqrt(jnp.mean(xf * xf, axis=-1, keepdims=True) + eps)
    return (y * g.astype(jnp.float32)).astype(x.dtype)

def alibi_slopes(n):
    return 2.0 ** (-8.0 * jnp.arange(1, n + 1, dtype=jnp.float32) / n)

def to_query_blocks(t):
    b, h, s = t.shape[:3]
    t = t.reshape((b, h, s // Q_BLOCK, Q_BLOCK) + t.shape[3:])
    return jnp.moveaxis(t, 2, 0)

def from_query_blocks(o):
    nb, b, h, qb, dv = o.shape
    return o.transpose(1, 0, 3, 2, 4).reshape(b, nb * qb, h * dv)

def split_columns(qkv):
    widths = [DIFF_WIDTH] * 3 + [SB_WIDTH] * 3 + [CH_WIDTH] * 3
    outs, start = [], 0
    for w in widths:
        outs.append(qkv[..., start:start + w])
        start += w
    return outs

def diff_attention(q, k, v, lam, lam_init, subln_g):
    b, s, _ = q.shape
    h = N_HEADS_DIFF
    q = q.reshape(b, s, h, 2, HEAD_DIM).transpose(0, 2, 1, 3, 4)
    k = k.reshape(b, s, h, 2, HEAD_DIM).transpose(0, 2, 1, 3, 4)
    v = v.reshape(b, s, h, 2 * HEAD_DIM).transpose(0, 2, 1, 3)
    slopes = alibi_slopes(h)
    k_pos = jnp.arange(s)
    k_chunk = k_pos // CHUNK
    scale = HEAD_DIM ** -0.5

    def block(args):
        q_blk, i = args
        q_pos = i * Q_BLOCK + jnp.arange(Q_BLOCK)
        sc = jnp.einsum('bhqcd,bhkcd->bhcqk', q_blk, k).astype(jnp.float32) * scale
        dist = jnp.abs(q_pos[:, None] - k_pos[None, :]).astype(jnp.float32)
        bias = -slopes[:, None, None] * dist
        allowed = k_chunk[None, :] <= (q_pos // CHUNK)[:, None]
        sc = jnp.where(allowed, sc + bias[None, :, None], -jnp.inf)
        p = jax.nn.softmax(sc, axis=-1)
        w = (p[:, :, 0] - lam * p[:, :, 1]).astype(v.dtype)
        return jnp.einsum('bhqk,bhkv->bhqv', w, v)

    o = lax.map(block, (to_query_blocks(q), jnp.arange(s // Q_BLOCK)))
    o = rmsnorm(o, subln_g, SUBLN_EPS) * (1.0 - lam_init)
    return from_query_blocks(o)

def stick_breaking_attention(q, k, v, head_g):
    b, s, _ = q.shape
    h = N_HEADS_SB
    q = q.reshape(b, s, h, HEAD_DIM).transpose(0, 2, 1, 3)
    k = k.reshape(b, s, h, HEAD_DIM).transpose(0, 2, 1, 3)
    v = v.reshape(b, s, h, HEAD_DIM).transpose(0, 2, 1, 3)
    k_pos = jnp.arange(s)
    scale = HEAD_DIM ** -0.5

    def block(args):
        q_blk, i = args
        q_pos = i * Q_BLOCK + jnp.arange(Q_BLOCK)
        z = jnp.einsum('bhqd,bhkd->bhqk', q_blk, k).astype(jnp.float32) * scale
        causal = k_pos[None, :] < q_pos[:, None]
        log_1m_beta = jnp.where(causal, -jax.nn.softplus(z), 0.0)
        suffix = lax.cumsum(log_1m_beta, axis=3, reverse=True) - log_1m_beta
        log_a = jax.nn.log_sigmoid(z) + suffix
        a = jnp.where(causal, jnp.exp(log_a), 0.0).astype(v.dtype)
        return jnp.einsum('bhqk,bhkd->bhqd', a, v)

    o = lax.map(block, (to_query_blocks(q), jnp.arange(s // Q_BLOCK)))
    o = rmsnorm(o, head_g[:, None, :])
    return from_query_blocks(o)

def chunk_band_attention(q, k, v, rel_table, head_g):
    b, s, _ = q.shape
    h = N_HEADS_CH
    nc = s // CHUNK
    pad = LEFT_CHUNKS * CHUNK
    q = q.reshape(b, s, h, HEAD_DIM).transpose(0, 2, 1, 3)
    k = k.reshape(b, s, h, HEAD_DIM).transpose(0, 2, 1, 3)
    v = v.reshape(b, s, h, HEAD_DIM).transpose(0, 2, 1, 3)
    qc = q.reshape(b, h, nc, CHUNK, HEAD_DIM)

    def band(t):
        tp = jnp.pad(t, ((0, 0), (0, 0), (pad, 0), (0, 0)))
        tp = tp.reshape(b, h, nc + LEFT_CHUNKS, CHUNK, HEAD_DIM)
        return jnp.concatenate([tp[:, :, o:o + nc] for o in range(LEFT_CHUNKS + 1)], axis=3)

    kb, vb = band(k), band(v)
    sc = jnp.einsum('bhcqd,bhckd->bhcqk', qc, kb).astype(jnp.float32) * HEAD_DIM ** -0.5
    q_loc = jnp.arange(CHUNK)
    k_loc = jnp.arange(BAND) - pad
    rel_idx = jnp.clip(q_loc[:, None] - k_loc[None, :], -(CHUNK - 1), MAX_REL) + (CHUNK - 1)
    bias = rel_table[:, rel_idx].astype(jnp.float32)
    valid = (jnp.arange(nc)[:, None] * CHUNK + k_loc[None, :]) >= 0
    sc = jnp.where(valid[:, None, :], sc + bias[:, None], -jnp.inf)
    p = jax.nn.softmax(sc, axis=-1).astype(vb.dtype)
    o = jnp.einsum('bhcqk,bhckd->bhcqd', p, vb).reshape(b, h, s, HEAD_DIM)
    o = rmsnorm(o, head_g[:, None, :])
    return o.transpose(0, 2, 1, 3).reshape(b, s, h * HEAD_DIM)

def causal_dwconv(hid, w, bias):
    s = hid.shape[1]
    hp = jnp.pad(hid, ((0, 0), (CONV_WIDTH - 1, 0), (0, 0)))
    out = bias
    for j in range(CONV_WIDTH):
        out = out + hp[:, j:j + s] * w[j]
    return out

def first_inputs(seed: int = 0) -> dict:
    key = jax.random.key(seed)
    ks = jax.random.split(key, 20)

    def nrm(k, shape, scale):
        return jax.random.normal(k, shape, jnp.float32) * scale

    def gain(k, shape):
        return 1.0 + nrm(k, shape, 0.05)

    return {
        'x': nrm(ks[0], (BATCH, SEQ, D_MODEL), 1.0),
        'attn_norm': gain(ks[1], (DEPTH, D_MODEL)),
        'w_qkv': nrm(ks[2], (DEPTH, D_MODEL, QKV_WIDTH), D_MODEL ** -0.5),
        'lambda_q1': nrm(ks[3], (DEPTH, HEAD_DIM), 0.1),
        'lambda_k1': nrm(ks[4], (DEPTH, HEAD_DIM), 0.1),
        'lambda_q2': nrm(ks[5], (DEPTH, HEAD_DIM), 0.1),
        'lambda_k2': nrm(ks[6], (DEPTH, HEAD_DIM), 0.1),
        'diff_subln': gain(ks[7], (DEPTH, 2 * HEAD_DIM)),
        'sb_norm': gain(ks[8], (DEPTH, N_HEADS_SB, HEAD_DIM)),
        'rel_bias': nrm(ks[9], (DEPTH, N_HEADS_CH, N_REL), 0.2),
        'ch_norm': gain(ks[10], (DEPTH, N_HEADS_CH, HEAD_DIM)),
        'w_o': nrm(ks[11], (DEPTH, MIX_WIDTH, D_MODEL), MIX_WIDTH ** -0.5),
        'ffn_norm': gain(ks[12], (DEPTH, D_MODEL)),
        'w_gate': nrm(ks[13], (DEPTH, D_MODEL, D_FF), D_MODEL ** -0.5),
        'w_up': nrm(ks[14], (DEPTH, D_MODEL, D_FF), D_MODEL ** -0.5),
        'conv_w': nrm(ks[15], (DEPTH, CONV_WIDTH, D_FF), CONV_WIDTH ** -0.5),
        'conv_b': nrm(ks[16], (DEPTH, D_FF), 0.02),
        'w_down': nrm(ks[17], (DEPTH, D_FF, D_MODEL), D_FF ** -0.5),
        'final_norm': gain(ks[18], (D_MODEL,)),
    }

def first_block(x, attn_norm, w_qkv, lambda_q1, lambda_k1, lambda_q2, lambda_k2,
              diff_subln, sb_norm, rel_bias, ch_norm, w_o, ffn_norm, w_gate, w_up,
              conv_w, conv_b, w_down, final_norm):
    for l in range(DEPTH):
        lam_init = 0.8 - 0.6 * math.exp(-0.3 * l)
        h = rmsnorm(x, attn_norm[l])
        qkv = jnp.einsum('bsd,de->bse', h, w_qkv[l])
        q_a, k_a, v_a, q_b, k_b, v_b, q_c, k_c, v_c = split_columns(qkv)
        lam = (jnp.exp(jnp.sum(lambda_q1[l] * lambda_k1[l]).astype(jnp.float32))
               - jnp.exp(jnp.sum(lambda_q2[l] * lambda_k2[l]).astype(jnp.float32))
               + lam_init)
        y_a = diff_attention(q_a, k_a, v_a, lam, lam_init, diff_subln[l])
        y_b = stick_breaking_attention(q_b, k_b, v_b, sb_norm[l])
        y_c = chunk_band_attention(q_c, k_c, v_c, rel_bias[l], ch_norm[l])
        y = jnp.concatenate([y_a, y_b, y_c], axis=-1)
        x = x + jnp.einsum('bse,ed->bsd', y, w_o[l])
        h = rmsnorm(x, ffn_norm[l])
        g = causal_dwconv(jnp.einsum('bsd,df->bsf', h, w_gate[l]), conv_w[l], conv_b[l])
        u = jnp.einsum('bsd,df->bsf', h, w_up[l])
        x = x + jnp.einsum('bsf,fd->bsd', jax.nn.silu(g) * u, w_down[l])
    return rmsnorm(x, final_norm)


ROPE_THETA = 500000.0
N_MEM = 256
EPS = 1e-6

MLA_HEADS = 8
MLA_NOPE = 128
MLA_ROPE = 64
MLA_V = 128
MLA_Q_LORA = 512
MLA_KV_LORA = 256
DSA_HEADS = 8
DSA_HEAD_DIM = 128
DSA_ROT = DSA_HEAD_DIM // 4
IDX_HEADS = 16
IDX_DIM = 64
IDX_ROT = IDX_DIM // 4
TOPK_MAX = 256
X_HEADS = 4
X_HEAD_DIM = 128
D_FF_2 = 4 * D_MODEL

MIX_WIDTH_2 = MLA_HEADS * MLA_V + DSA_HEADS * DSA_HEAD_DIM
IN_SPLITS = (
    MLA_Q_LORA,
    MLA_KV_LORA,
    MLA_ROPE,
    DSA_HEADS * DSA_HEAD_DIM,
    DSA_HEADS * DSA_HEAD_DIM,
    DSA_HEADS * DSA_HEAD_DIM,
    IDX_HEADS * IDX_DIM,
    IDX_DIM,
    IDX_HEADS,
)
D_IN = int(sum(IN_SPLITS))


def rmsnorm_2(x, g):
    xf = x.astype(jnp.float32)
    y = xf * lax.rsqrt(jnp.mean(xf * xf, axis=-1, keepdims=True) + EPS)
    return (y * g.astype(jnp.float32)).astype(x.dtype)

def rope(x, pos, rot_dim):
    half = rot_dim // 2
    inv_freq = ROPE_THETA ** (-jnp.arange(half, dtype=jnp.float32) / half)
    ang = pos.astype(jnp.float32)[..., None] * inv_freq
    ang = ang.reshape(ang.shape[:2] + (1,) * (x.ndim - 3) + (half,))
    cos, sin = jnp.cos(ang), jnp.sin(ang)
    xf = x.astype(jnp.float32)
    x1, x2, rest = xf[..., :half], xf[..., half:rot_dim], xf[..., rot_dim:]
    out = jnp.concatenate([x1 * cos - x2 * sin, x2 * cos + x1 * sin, rest], axis=-1)
    return out.astype(x.dtype)

def to_blocks(a):
    b, s = a.shape[:2]
    a = a.reshape((b, s // Q_BLOCK, Q_BLOCK) + a.shape[2:])
    return jnp.moveaxis(a, 1, 0)

def from_blocks(a):
    a = jnp.moveaxis(a, 0, 1)
    return a.reshape((a.shape[0], a.shape[1] * a.shape[2]) + a.shape[3:])

def query_chunks(i):
    return (i * Q_BLOCK + jnp.arange(Q_BLOCK)) // CHUNK

def mla_mixer(c_q, c_kv, k_rope, pos, g_cq, g_ckv, w_qb, w_kvb):
    b, s, _ = c_q.shape
    q = (rmsnorm_2(c_q, g_cq) @ w_qb).reshape(b, s, MLA_HEADS, MLA_NOPE + MLA_ROPE)
    q_nope = q[..., :MLA_NOPE]
    q_rope = rope(q[..., MLA_NOPE:], pos, MLA_ROPE)
    kv = (rmsnorm_2(c_kv, g_ckv) @ w_kvb).reshape(b, s, MLA_HEADS, MLA_NOPE + MLA_V)
    k_nope, v = kv[..., :MLA_NOPE], kv[..., MLA_NOPE:]
    k_rope = rope(k_rope, pos, MLA_ROPE)
    scale = (MLA_NOPE + MLA_ROPE) ** -0.5
    key_chunk = jnp.arange(s) // CHUNK

    def block(args):
        i, qn, qr = args
        sc = (jnp.einsum('bqhd,bkhd->bhqk', qn, k_nope)
              + jnp.einsum('bqhr,bkr->bhqk', qr, k_rope)).astype(jnp.float32) * scale
        allowed = key_chunk[None, :] <= query_chunks(i)[:, None]
        sc = jnp.where(allowed[None, None], sc, -jnp.inf)
        p = jax.nn.softmax(sc, axis=-1).astype(v.dtype)
        return jnp.einsum('bhqk,bkhd->bqhd', p, v)

    o = lax.map(block, (jnp.arange(s // Q_BLOCK), to_blocks(q_nope), to_blocks(q_rope)))
    return from_blocks(o).reshape(b, s, MLA_HEADS * MLA_V)

def dsa_mixer(q, k, v, q_idx, k_idx, w_idx, pos):
    b, s, _ = q.shape
    q = rope(q.reshape(b, s, DSA_HEADS, DSA_HEAD_DIM), pos, DSA_ROT)
    k = rope(k.reshape(b, s, DSA_HEADS, DSA_HEAD_DIM), pos, DSA_ROT)
    v = v.reshape(b, s, DSA_HEADS, DSA_HEAD_DIM)
    q_idx = rope(q_idx.reshape(b, s, IDX_HEADS, IDX_DIM), pos, IDX_ROT)
    k_idx = rope(k_idx, pos, IDX_ROT)
    w_idx = w_idx * (IDX_HEADS ** -0.5)
    n_sel = min(TOPK_MAX, s // 4)
    key_chunk = jnp.arange(s) // CHUNK
    gather = jax.vmap(lambda arr, idx: arr[idx])

    def block(args):
        i, qb, qib, wb = args
        qc = query_chunks(i)
        logits = jax.nn.relu(jnp.einsum('bqhd,bkd->bqhk', qib, k_idx).astype(jnp.float32) * (IDX_DIM ** -0.5))
        score = jnp.einsum('bqhk,bqh->bqk', logits, wb.astype(jnp.float32))
        allowed = key_chunk[None, :] <= qc[:, None]
        score = jnp.where(allowed[None], score, -jnp.inf)
        _, sel = lax.top_k(score, n_sel)
        sel_ok = (sel // CHUNK) <= qc[None, :, None]
        k_sel = gather(k, sel)
        v_sel = gather(v, sel)
        sc = jnp.einsum('bqhd,bqnhd->bhqn', qb, k_sel).astype(jnp.float32) * (DSA_HEAD_DIM ** -0.5)
        sc = jnp.where(sel_ok[:, None], sc, -jnp.inf)
        p = jax.nn.softmax(sc, axis=-1).astype(v.dtype)
        return jnp.einsum('bhqn,bqnhd->bqhd', p, v_sel)

    o = lax.map(block, (jnp.arange(s // Q_BLOCK), to_blocks(q), to_blocks(q_idx), to_blocks(w_idx)))
    return from_blocks(o).reshape(b, s, DSA_HEADS * DSA_HEAD_DIM)

def memory_cross_attention(h, mem_n, wq, wk, wv, wo):
    b, s, _ = h.shape
    m = mem_n.shape[1]
    q = (h @ wq).reshape(b, s, X_HEADS, X_HEAD_DIM)
    k = (mem_n @ wk).reshape(b, m, X_HEADS, X_HEAD_DIM)
    v = (mem_n @ wv).reshape(b, m, X_HEADS, X_HEAD_DIM)
    sc = jnp.einsum('bshd,bmhd->bhsm', q, k).astype(jnp.float32) * (X_HEAD_DIM ** -0.5)
    p = jax.nn.softmax(sc, axis=-1).astype(v.dtype)
    o = jnp.einsum('bhsm,bmhd->bshd', p, v).reshape(b, s, X_HEADS * X_HEAD_DIM)
    return o @ wo

def second_inputs(seed: int = 0) -> dict:
    key = jax.random.key(seed)
    ks = jax.random.split(key, 24)
    f32 = jnp.float32

    def w(k, shape, fan_in):
        return jax.random.normal(k, (DEPTH,) + shape, f32) * (fan_in ** -0.5)

    def gain(k, n):
        return 1.0 + 0.02 * jax.random.normal(k, (DEPTH, n), f32)

    x = jax.random.normal(ks[0], (BATCH, SEQ, D_MODEL), f32)
    mem = jax.random.normal(ks[1], (BATCH, N_MEM, D_MODEL), f32)
    offset = jax.random.randint(ks[2], (BATCH, 1), 0, 16, dtype=jnp.int32) * CHUNK
    positions = (offset + jnp.arange(SEQ, dtype=jnp.int32)[None, :]).astype(jnp.int32)
    return {
        "x": x,
        "mem": mem,
        "positions": positions,
        "g_mix": gain(ks[3], D_MODEL),
        "w_in": w(ks[4], (D_MODEL, D_IN), D_MODEL),
        "g_cq": gain(ks[5], MLA_Q_LORA),
        "g_ckv": gain(ks[6], MLA_KV_LORA),
        "w_qb": w(ks[7], (MLA_Q_LORA, MLA_HEADS * (MLA_NOPE + MLA_ROPE)), MLA_Q_LORA),
        "w_kvb": w(ks[8], (MLA_KV_LORA, MLA_HEADS * (MLA_NOPE + MLA_V)), MLA_KV_LORA),
        "w_out": w(ks[9], (MIX_WIDTH_2, D_MODEL), MIX_WIDTH_2),
        "g_cross": gain(ks[10], D_MODEL),
        "g_mem": gain(ks[11], D_MODEL),
        "w_q_cross": w(ks[12], (D_MODEL, X_HEADS * X_HEAD_DIM), D_MODEL),
        "w_k_cross": w(ks[13], (D_MODEL, X_HEADS * X_HEAD_DIM), D_MODEL),
        "w_v_cross": w(ks[14], (D_MODEL, X_HEADS * X_HEAD_DIM), D_MODEL),
        "w_o_cross": w(ks[15], (X_HEADS * X_HEAD_DIM, D_MODEL), X_HEADS * X_HEAD_DIM),
        "g_mlp": gain(ks[16], D_MODEL),
        "w_up": w(ks[17], (D_MODEL, D_FF_2), D_MODEL),
        "w_down": w(ks[18], (D_FF_2, D_MODEL), D_FF_2),
        "g_final": 1.0 + 0.02 * jax.random.normal(ks[19], (D_MODEL,), f32),
    }

def second_block(x, mem, positions, g_mix, w_in, g_cq, g_ckv, w_qb, w_kvb, w_out,
              g_cross, g_mem, w_q_cross, w_k_cross, w_v_cross, w_o_cross,
              g_mlp, w_up, w_down, g_final):
    offsets = np.cumsum(np.array(IN_SPLITS))[:-1].tolist()
    for l in range(DEPTH):
        h = rmsnorm_2(x, g_mix[l])
        c_q, c_kv, k_rope, q_d, k_d, v_d, q_idx, k_idx, w_idx = jnp.split(h @ w_in[l], offsets, axis=-1)
        a = mla_mixer(c_q, c_kv, k_rope, positions, g_cq[l], g_ckv[l], w_qb[l], w_kvb[l])
        bb = dsa_mixer(q_d, k_d, v_d, q_idx, k_idx, w_idx, positions)
        x = x + jnp.concatenate([a, bb], axis=-1) @ w_out[l]
        hc = rmsnorm_2(x, g_cross[l])
        mem_n = rmsnorm_2(mem, g_mem[l])
        x = x + memory_cross_attention(hc, mem_n, w_q_cross[l], w_k_cross[l], w_v_cross[l], w_o_cross[l])
        hm = rmsnorm_2(x, g_mlp[l])
        x = x + jnp.square(jax.nn.relu(hm @ w_up[l])) @ w_down[l]
    return rmsnorm_2(x, g_final)


def setup_inputs(seed=0):
    out = dict(first_inputs(seed))
    for name, value in second_inputs(seed + 1).items():
        if name != "x":
            out[name + "_2"] = value
    return out


def reference(
    x, attn_norm, w_qkv, lambda_q1, lambda_k1, lambda_q2, lambda_k2, diff_subln, sb_norm,
    rel_bias, ch_norm, w_o, ffn_norm, w_gate, w_up, conv_w, conv_b, w_down, final_norm, mem_2,
    positions_2, g_mix_2, w_in_2, g_cq_2, g_ckv_2, w_qb_2, w_kvb_2, w_out_2, g_cross_2, g_mem_2,
    w_q_cross_2, w_k_cross_2, w_v_cross_2, w_o_cross_2, g_mlp_2, w_up_2, w_down_2, g_final_2,
):
    x = first_block(
        x, attn_norm, w_qkv, lambda_q1, lambda_k1, lambda_q2, lambda_k2, diff_subln, sb_norm,
        rel_bias, ch_norm, w_o, ffn_norm, w_gate, w_up, conv_w, conv_b, w_down, final_norm,
    )
    return second_block(
        x, mem_2, positions_2, g_mix_2, w_in_2, g_cq_2, g_ckv_2, w_qb_2, w_kvb_2, w_out_2,
        g_cross_2, g_mem_2, w_q_cross_2, w_k_cross_2, w_v_cross_2, w_o_cross_2, g_mlp_2, w_up_2,
        w_down_2, g_final_2,
    )


_drawn_inputs = setup_inputs


def setup_inputs(seed=0):
    import zlib

    import numpy as np

    out = dict(_drawn_inputs(seed))
    spreads = {}
    factors = {'lambda_q2': 8.0,
     'conv_b': 3.6,
     'g_mix_2': 2.753,
     'g_cq_2': 8.0,
     'g_ckv_2': 8.0,
     'g_cross_2': 8.0,
     'g_mem_2': 8.0,
     'g_mlp_2': 9.619,
     'g_final_2': 7.873}
    for name, (base, spread) in spreads.items():
        noise = np.random.default_rng([zlib.crc32(name.encode()), seed]).standard_normal(out[name].shape)
        drawn = base * np.exp(spread * noise) if base else spread * noise
        out[name] = jnp.asarray(drawn.astype(out[name].dtype))
    for name, factor in factors.items():
        out[name] = (out[name] * factor).astype(out[name].dtype)
    return out
```

```python
from contextlib import ExitStack

import numpy as np
import concourse.bass as bass
from concourse import mybir

F32 = mybir.dt.float32
F32R = mybir.dt.float32r
I32 = mybir.dt.int32
ALU = mybir.AluOpType
ACT = mybir.ActivationFunctionType
AX_X = mybir.AxisListType.X

P = 128
TOK = 256
TT = TOK // P
D = 2048
DK = D // P
CHUNK = 64
F1 = 5632
F2 = 8192
HD = 64
NH = 8
MIX = 2048
N_REL = 192
IDX_HEADS = 16
TOPK = 64
NEG = -1.0e30
TAKEN = -3.0e38
PHASE = 16
TURNED_COLS = 256
STRAIGHT_COLS = 512
UNIT = 1024
RAW_SLOTS = 6
SPLIT_SLOTS = 4
EXPS = "natural_log_exp_and_others"

C_Q, C_KV, K_ROPE, Q_D, K_D, V_D, Q_IDX, K_IDX, W_IDX = 0, 512, 768, 832, 1856, 2880, 3904, 4928, 4992
TAIL = 256 + 64 + 64 + 16

CONSTS = [("ident", P), ("flip", P), ("after", P), ("causal", P), ("ones", P),
          ("mask", TOK), ("dist", TOK), ("freq", 32), ("half", 1), ("eighth", 1), ("less_eighth", 1)]
GAINS = [("attn", 16), ("y1", 16), ("ffn", 16), ("conv0", 44), ("conv1", 44), ("conv2", 44), ("convb", 44),
         ("mix", 16), ("cq", 4), ("ckv", 2), ("cross", 16), ("mem", 16), ("mlp", 16)]


def columns_of(table):
    at, out = 0, {}
    for name, width in table:
        out[name] = (at, at + width)
        at += width
    return out, at


class Engine:

    def __init__(self, semaphore):
        self.semaphore, self.count, self.program, self.reached = semaphore, 0, [], {}

    def wait(self, *marks):
        for mark in flat(marks):
            semaphore, value = mark
            if self.reached.get(semaphore.name, 0) < value:
                self.reached[semaphore.name] = value
                self.program.append(lambda e, s=semaphore, v=value: e.wait_ge(s, v))

    def do(self, issue, *marks):
        self.wait(*marks)
        self.count += 1
        self.program.append(lambda e: issue(e).then_inc(self.semaphore, 1))
        return (self.semaphore, self.count)

    def run(self, e):
        for step in self.program:
            step(e)


def flat(marks):
    for m in marks:
        if m is None:
            continue
        if isinstance(m, list):
            yield from flat(m)
        else:
            yield m


class Banks:

    def __init__(self, banks):
        self.banks, self.free, self.at = banks, [None] * len(banks), 0

    def take(self):
        n = self.at % len(self.banks)
        self.at += 1
        return n, self.banks[n]


class Slots:

    def __init__(self, views):
        self.views, self.free = views, [None] * len(views)

    def of(self, i):
        return i % len(self.views), self.views[i % len(self.views)]


def build_program(nc, dram, out_dram):
    const_at, n_const = columns_of(CONSTS)
    gain_at, n_gain = columns_of(GAINS)

    ctx = ExitStack()
    with ctx:
        def sbuf(name, shape, dt=F32, scope=ctx):
            return scope.enter_context(nc.sbuf_tensor(name, shape, dt))

        raw_w = sbuf("raw_w", [P, RAW_SLOTS, UNIT])
        hi_w = sbuf("hi_w", [P, SPLIT_SLOTS, UNIT], F32R)
        lo_w = sbuf("lo_w", [P, SPLIT_SLOTS, UNIT], F32R)
        x = sbuf("x", [P, TT, D])
        xT_hi = sbuf("xT_hi", [P, DK, TOK], F32R)
        xT_lo = sbuf("xT_lo", [P, DK, TOK], F32R)
        consts = sbuf("consts", [P, n_const])
        gains = sbuf("gains", [P, n_gain])
        stats = sbuf("stats", [P, 192])
        banks = [ctx.enter_context(nc.psum_tensor(f"bank{i}", [P, 512], F32)) for i in range(8)]

        pe = Engine(ctx.enter_context(nc.semaphore("pe_done")))
        act = Engine(ctx.enter_context(nc.semaphore("act_done")))
        dve = Engine(ctx.enter_context(nc.semaphore("dve_done")))
        weights_in = Engine(None)
        others_in = Engine(None)
        raw_landed = [ctx.enter_context(nc.semaphore(f"raw_landed{i}")) for i in range(RAW_SLOTS)]

        def const(name):
            a, b = const_at[name]
            return consts[:, a:b]

        def gain(name, k):
            a = gain_at[name][0]
            return gains[:, a + k:a + k + 1]

        def load(queue, dst, src, name, *marks):
            landed = ctx.enter_context(nc.semaphore(name))
            queue.wait(*marks)
            queue.program.append(lambda e: e.dma_start(dst, src).then_inc(landed, 16))
            return (landed, 16)

        gemm_banks = Banks(banks[0:4])
        work_banks = Banks(banks[4:8])

        x_in = load(others_in, x[:, :, :], dram["x"].rearrange("(t p) d -> p t d", p=P), "x_landed")
        consts_in = load(others_in, consts[:, :], dram["consts"], "consts_landed")
        gains_in = load(others_in, gains[:, :], dram["gains"], "gains_landed")

        def units_turned(name, cols, kts):
            w, per = dram[name], min(4, kts)
            return [(name, w[g, u].rearrange("p k c -> p (k c)"))
                    for g in range(cols // TURNED_COLS) for u in range(kts // per)]

        def units_straight(name, chunks, kts, k0=0):
            w = dram[name]
            return [(name, w[c, k0 // 2 + u].rearrange("p k c -> p (k c)"))
                    for c in range(chunks) for u in range(kts // 2)]

        plan = units_turned("w_qk", 4096, DK) + units_straight("w_v", 4, DK) + units_straight("w_o", 4, DK)
        phases1 = [(a, min(a + PHASE, F1 // P)) for a in range(0, F1 // P, PHASE)]
        phases2 = [(a, min(a + PHASE, F2 // P)) for a in range(0, F2 // P, PHASE)]

        def ffn_plan(phases, ups, down):
            out = []
            for n, (a, b) in enumerate(phases):
                for pair in range(a // 2, b // 2):
                    for name in ups:
                        out += [(name, dram[name][pair, u].rearrange("p k c -> p (k c)")) for u in range(4)]
                if n:
                    out += units_straight(down, 4, phases[n - 1][1] - phases[n - 1][0], phases[n - 1][0])
            return out + units_straight(down, 4, phases[-1][1] - phases[-1][0], phases[-1][0])

        plan += ffn_plan(phases1, ["w_gate", "w_up1"], "w_down1")
        plan += units_straight("w_tail", 1, DK) + units_straight("w_in", 9, DK)
        plan += units_turned("w_qnope", 1024, 4) + units_straight("w_qrope", 1, 4)
        plan += units_turned("w_knope", 1024, 2) + units_straight("w_vmla", 2, 2)
        plan += units_straight("w_out", 4, DK)
        plan += units_turned("w_kx", 512, DK) + units_straight("w_vx", 1, DK) + units_turned("w_qx", 512, DK)
        plan += units_straight("w_ox", 4, 4)
        plan += ffn_plan(phases2, ["w_up2"], "w_down2")

        class WeightStream:

            def __init__(self):
                self.loaded = self.split_up_to = self.at = 0
                self.split_done = {}
                self.used = {}
                for _ in range(RAW_SLOTS):
                    self.load()
                for _ in range(SPLIT_SLOTS - 1):
                    self.split()

            def load(self):
                u = self.loaded
                if u >= len(plan):
                    return
                self.loaded += 1
                slot, src = u % RAW_SLOTS, plan[u][1]
                weights_in.wait(self.split_done.get(u - RAW_SLOTS))
                weights_in.program.append(
                    lambda e: e.dma_start(raw_w[:, slot, 0:src.shape[1]], src).then_inc(raw_landed[slot], 16))

            def split(self):
                u = self.split_up_to
                if u >= len(plan):
                    return
                self.split_up_to += 1
                n = plan[u][1].shape[1]
                raw = raw_w[:, u % RAW_SLOTS, 0:n]
                hi, lo = hi_w[:, u % SPLIT_SLOTS, 0:n], lo_w[:, u % SPLIT_SLOTS, 0:n]
                landed = (raw_landed[u % RAW_SLOTS], 16 * (u // RAW_SLOTS + 1))
                free = self.used.get(u - SPLIT_SLOTS)
                hi_done = act.do(lambda e: e.activation(hi, raw, ACT.Copy), landed, free)
                lo_done = dve.do(lambda e: e.tensor_tensor(lo, raw, hi.bitcast(F32), ALU.subtract), hi_done)
                self.split_done[u] = [lo_done, hi_done]
                self.load()

            def take(self, name):
                assert plan[self.at][0] == name, (plan[self.at][0], name)
                self.split()
                u, n = self.at, plan[self.at][1].shape[1]
                return hi_w[:, u % SPLIT_SLOTS, 0:n], lo_w[:, u % SPLIT_SLOTS, 0:n], self.split_done[u][0]

            def release(self, mark):
                self.used[self.at] = mark
                self.at += 1

        stream = WeightStream()

        def turned(name, cols, kts, in_hi, in_lo, in_ready, evict, group0=0):
            per = min(4, kts)
            for g in range(group0, group0 + cols // TURNED_COLS):
                n, bank = gemm_banks.take()
                done = None
                for u in range(kts // per):
                    w_hi, w_lo, w_ready = stream.take(name)

                    def issue(e, u=u, w_hi=w_hi, w_lo=w_lo, bank=bank):
                        for c in range(2):
                            o = bank[:, c * TOK:(c + 1) * TOK]
                            for k in range(per):
                                kt = u * per + k
                                cols_k = slice(k * TURNED_COLS + c * P, k * TURNED_COLS + (c + 1) * P)
                                passes = [(w_hi, in_hi), (w_hi, in_lo), (w_lo, in_hi)]
                                for i, (w, v) in enumerate(passes):
                                    last = e.matmul(o, w[:, cols_k], v[:, kt, :],
                                                    start=(kt == 0 and c == 0 and i == 0),
                                                    stop=(kt == kts - 1 and i == 2), skip_group_check=True)
                        return last

                    ready = [in_ready[u * per + k] for k in range(per)]
                    done = pe.do(issue, w_ready, ready, gemm_banks.free[n] if u == 0 else None)
                    stream.release(done)
                gemm_banks.free[n] = evict(g, bank, done)

        def straight(name, chunks, kts, in_hi, in_lo, in_ready, evict, width=STRAIGHT_COLS, k0=0):
            for c in range(chunks):
                pair = [gemm_banks.take() for _ in range(TT)]
                done = None
                for u in range(kts // 2):
                    w_hi, w_lo, w_ready = stream.take(name)

                    def issue(e, u=u, w_hi=w_hi, w_lo=w_lo, pair=pair):
                        for t in range(TT):
                            for k in range(2):
                                kt = u * 2 + k
                                cols_k = slice(k * width, (k + 1) * width)
                                rows = slice(t * P, (t + 1) * P)
                                passes = [(in_hi, w_hi), (in_hi, w_lo), (in_lo, w_hi)]
                                for i, (v, w) in enumerate(passes):
                                    last = e.matmul(pair[t][1][:, 0:width], v[:, k0 + kt, rows], w[:, cols_k],
                                                    start=(kt == 0 and i == 0),
                                                    stop=(kt == kts - 1 and i == 2))
                        return last

                    ready = [in_ready[k0 + u * 2 + k] for k in range(2)]
                    free = [gemm_banks.free[n] for n, _ in pair] if u == 0 else None
                    done = pe.do(issue, w_ready, ready, free)
                    stream.release(done)
                for t, (n, bank) in enumerate(pair):
                    gemm_banks.free[n] = evict(c, t, bank, done)

        def inverse_rms(parts, ss, width, ready):
            r, t = stats[:, 64:64 + width], stats[:, 128:128 + width]
            a = [dve.do(lambda e, view=view, n=n, eps=eps: e.tensor_scalar(view, view, 1.0 / n, eps,
                                                                           ALU.mult, ALU.add), ready)
                 for view, n, eps in parts]
            b = act.do(lambda e: e.activation(r, ss, ACT.Sqrt), a)
            b = dve.do(lambda e: e.reciprocal(r, r), b)
            c = dve.do(lambda e: e.tensor_tensor(t, r, r, ALU.mult), b)
            c = dve.do(lambda e: e.tensor_tensor(t, t, ss, ALU.mult), c)
            c = dve.do(lambda e: e.tensor_scalar(t, t, -0.5, 1.5, ALU.mult, ALU.add), c)
            return dve.do(lambda e: e.tensor_tensor(ss, r, t, ALU.mult), c)

        def fine_exp(quarters, rest, out, ready, out_free=None):
            a = act.do(lambda e: e.activation(out, quarters, ACT.Exp, bias=const("eighth"), scale=0.25),
                       ready, out_free)
            b = act.do(lambda e: e.activation(rest, rest, ACT.Exp, bias=const("less_eighth"), scale=0.25))
            return [a, b]

        def rms_scaled(src, dst, n, ready, dst_free, stat):
            marks = []
            for t in range(TT):
                ss = stats[:, stat + t:stat + t + 1]
                marks.append(act.do(lambda e, t=t, ss=ss: e.activation(dst[:, t, :], src[:, t, :], ACT.Square,
                                                                       accum_out=ss), ready, dst_free))
            ss = stats[:, stat:stat + TT]
            scale = inverse_rms([(ss, n, 1e-6)], ss, TT, marks)
            return [dve.do(lambda e, t=t: e.tensor_scalar(dst[:, t, :], src[:, t, :],
                                                          stats[:, stat + t:stat + t + 1], None, ALU.mult),
                           scale) for t in range(TT)]

        def turn_and_split(src, n_kt, gain_name, dst_hi, dst_lo, ready, dst_free, kt0=0):
            done = [None] * (kt0 + n_kt)
            for pair in range(n_kt // 2):
                n, bank = work_banks.take()

                def issue(e, pair=pair, bank=bank):
                    for k in range(2):
                        for t in range(TT):
                            kt = pair * 2 + k
                            last = e.transpose(bank[:, k * TOK + t * P:k * TOK + (t + 1) * P],
                                               src[:, t, kt * P:(kt + 1) * P], const("ident"))
                    return last

                turned_mark = pe.do(issue, ready, work_banks.free[n], consts_in)
                his = []
                for k in range(2):
                    kt = pair * 2 + k
                    half, hi = bank[:, k * TOK:(k + 1) * TOK], dst_hi[:, kt0 + kt, :]
                    scale = gain(gain_name, kt) if gain_name else 1.0
                    his.append(act.do(lambda e, hi=hi, half=half, scale=scale:
                                      e.activation(hi, half, ACT.Copy, scale=scale),
                                      turned_mark, dst_free, gains_in))
                for k in range(2):
                    kt = pair * 2 + k
                    half, hi, lo = bank[:, k * TOK:(k + 1) * TOK], dst_hi[:, kt0 + kt, :], dst_lo[:, kt0 + kt, :]
                    scale = gain(gain_name, kt) if gain_name else 1.0
                    done[kt0 + kt] = dve.do(lambda e, hi=hi, half=half, lo=lo, scale=scale:
                                            e.scalar_tensor_tensor(lo, half, scale, hi.bitcast(F32),
                                                                   ALU.mult, ALU.subtract),
                                            his, dst_free, gains_in)
                work_banks.free[n] = done[kt0 + pair * 2 + 1]
            return done

        def add_to_x(x_ready):
            def evict(c, t, bank, mark):
                cols = slice(c * STRAIGHT_COLS, (c + 1) * STRAIGHT_COLS)
                done = dve.do(lambda e: e.tensor_tensor(x[:, t, cols], bank[:, :], x[:, t, cols], ALU.add),
                              mark, x_ready[:])
                x_ready.append(done)
                return done
            return evict

        def pipeline(items, stages):
            for s in range(len(items) + len(stages) - 1):
                for k in reversed(range(len(stages))):
                    if 0 <= s - k < len(items):
                        stages[k](items[s - k], s - k)

        def softmax_buffers(scope, prefix, wide):
            b = {}
            for name, depth, width in (("s", 3, wide), ("p", 3, wide), ("w", 3, TOK), ("pT", 3, TOK)):
                if name == "w" and wide == TOK:
                    continue
                t = sbuf(prefix + name, [P, depth, width], F32, scope)
                b[name] = Slots([t[:, i, :] for i in range(depth)])
            small = sbuf(prefix + "small", [P, 4, 8], F32, scope)
            b["small"] = Slots([small[:, i, :] for i in range(4)])
            return b

        def weighted_values(item, i, weights, weights_ready, b, scale, scale_ready):
            kts = item["W"] // P
            n, bank = work_banks.take()

            def turn(e):
                for k in range(kts):
                    last = e.transpose(bank[:, k * P:(k + 1) * P], weights[:, k * P:(k + 1) * P], const("ident"))
                return last

            mark = pe.do(turn, weights_ready, work_banks.free[n])
            slot, pT = b["pT"].of(i)
            copied = act.do(lambda e: e.activation(pT[:, 0:kts * P], bank[:, 0:kts * P], ACT.Copy),
                            mark, b["pT"].free[slot])
            work_banks.free[n] = copied
            item["pT"], item["pT_ready"], item["pT_slot"] = pT, copied, slot
            return mark

        def values_stage(b):
            def stage(item, i):
                kts, pT = item["W"] // P, item["pT"]
                n, bank = work_banks.take()
                wide = item["width"]

                def issue(e):
                    for k in range(kts):
                        last = e.matmul(bank[:, 0:wide], pT[:, k * P:(k + 1) * P], item["v"](k),
                                        start=(k == 0), stop=(k == kts - 1))
                    return last

                mark = pe.do(issue, item["pT_ready"], item["v_ready"], work_banks.free[n])
                b["pT"].free[item["pT_slot"]] = mark
                scale = item["scale_out"]
                done = act.do(lambda e: e.activation(item["out"], bank[:, 0:wide], ACT.Copy, scale=scale),
                              mark, item["scale_ready"], item.get("out_free"))
                if "ss" in item:
                    slot, junk = b["s"].of(i)
                    junk_free = b["s"].free[slot]
                    done = act.do(lambda e: e.activation(junk[:, 0:wide], bank[:, 0:wide], ACT.Square,
                                                         scale=scale, accum_out=item["ss"]), junk_free)
                    b["s"].free[slot] = [b["s"].free[slot], done]
                b["small"].free[item["small_slot"]] = done
                work_banks.free[n] = done
                item["done"] = done
            return stage

        def softmax_stages(b):
            def scores(item, i):
                n, bank = work_banks.take()
                mark = pe.do(lambda e: item["scores"](e, bank), item["ready"], work_banks.free[n])
                item["bank"], item["bank_n"], item["mark"] = bank, n, mark

            def soft(item, i):
                W, bank = item["W"], item["bank"]
                slot, s = b["s"].of(i)
                p_slot, p = b["p"].of(i)
                m_slot, small = b["small"].of(i)
                free = b["s"].free[slot]
                if item["scale"] == 1.0:
                    a = dve.do(lambda e: e.tensor_tensor(s[:, 0:W], bank[:, 0:W], item["mask"], ALU.add),
                               item["mark"], item["mask_ready"], free)
                elif item["mask"] is None:
                    a = dve.do(lambda e: e.tensor_scalar(s[:, 0:W], bank[:, 0:W], item["scale"], None, ALU.mult),
                               item["mark"], free)
                else:
                    a = dve.do(lambda e: e.scalar_tensor_tensor(s[:, 0:W], bank[:, 0:W], item["scale"],
                                                                item["mask"], ALU.mult, ALU.add),
                               item["mark"], item["mask_ready"], free)
                work_banks.free[item["bank_n"]] = a
                m = dve.do(lambda e: e.tensor_reduce(small[:, 0:1], s[:, 0:W], AX_X, ALU.max, negate=True),
                           a, b["small"].free[m_slot])
                if item.get("times4"):
                    quarters = p.bitcast(I32)
                    q = dve.do(lambda e: e.tensor_scalar(quarters[:, 0:W], s[:, 0:W], small[:, 0:1], -0.5,
                                                         ALU.add, ALU.add), m, b["p"].free[p_slot])
                    q = dve.do(lambda e: e.scalar_tensor_tensor(s[:, 0:W], s[:, 0:W], small[:, 0:1],
                                                                quarters[:, 0:W], ALU.add, ALU.subtract), q)
                    q = fine_exp(quarters[:, 0:W], s[:, 0:W], p[:, 0:W], q)
                    ex = dve.do(lambda e: e.tensor_tensor_reduce(p[:, 0:W], p[:, 0:W], s[:, 0:W], 1.0, 0.0,
                                                                 ALU.mult, ALU.add, small[:, 1:2]), q)
                else:
                    ex = act.do(lambda e: e.activation(p[:, 0:W], s[:, 0:W], ACT.Exp, bias=small[:, 0:1],
                                                       accum_out=small[:, 1:2]), m, b["p"].free[p_slot])
                b["s"].free[slot] = ex
                item["p"], item["p_slot"], item["p_ready"] = p, p_slot, ex
                item["scale_out"] = small[:, 2:3]
                item["small_slot"] = m_slot
                item["scale_ready"] = dve.do(lambda e: e.reciprocal(small[:, 2:3], small[:, 1:2]), ex)

            def turn(item, i):
                mark = weighted_values(item, i, item["p"], item["p_ready"], b, None, None)
                b["p"].free[item["p_slot"]] = mark

            return [scores, soft, turn, values_stage(b)]

        scope = ExitStack()
        qkT = sbuf("qkT", [P, 32, TOK], F32, scope)
        v1 = sbuf("v1", [P, TT, D], F32, scope)
        y1 = sbuf("y1", [P, TT, D], F32, scope)
        rel = sbuf("rel", [P, NH, TOK], F32, scope)
        lams = sbuf("lams", [P, 4, HD], F32, scope)
        b1 = softmax_buffers(scope, "a1_", 2 * TOK)
        Q_SCALE = HD ** -0.5

        ext = nc.dram_tensor("rel_ext", (NH, 384), F32, kind="Internal").ap()
        ext_sb = v1[0:NH, 1, 0:384]
        table_in = load(others_in, ext_sb[:, 127:319], dram["rel_rev"], "rel_table_landed")
        far = dve.do(lambda e: e.tensor_copy(ext_sb[:, 0:127], ext_sb[:, 127:128].to_broadcast([NH, 127])), table_in)
        near = dve.do(lambda e: e.tensor_copy(ext_sb[:, 319:384], ext_sb[:, 318:319].to_broadcast([NH, 65])))
        ext_done = load(others_in, ext, ext_sb, "rel_ext_landed", near)
        hankel_src = bass.AP(tensor=ext.tensor, offset=0, ap=[[1, P], [384, NH], [1, TOK]])
        hankel = v1[:, 0, :].rearrange("p (h k) -> p h k", h=NH)
        hankel_in = load(others_in, hankel, hankel_src, "hankel_landed", ext_done)
        lams_in = load(others_in, lams[:, :, :], bass.AP(tensor=dram["lambdas"].tensor, offset=0,
                                                         ap=[[0, P], [HD, 4], [1, HD]]), "lams_landed")

        h_ready = rms_scaled(x, y1, D, x_in, None, 0)
        h_in = turn_and_split(y1, DK, "attn", xT_hi, xT_lo, h_ready, None)

        dots = [dve.do(lambda e, j=j: e.tensor_tensor_reduce(lams[:, 2 * j, :], lams[:, 2 * j, :], lams[:, 2 * j + 1, :],
                                                             1.0, 0.0, ALU.mult, ALU.add, stats[:, 8 + j:9 + j]),
                       lams_in) for j in range(2)]
        lam_x, lam_n = stats[:, 8:10], stats[:, 12:14]
        m = dve.do(lambda e: e.tensor_scalar(lam_n.bitcast(I32), lam_x, 4.0, -0.5, ALU.mult, ALU.add), dots)
        m = dve.do(lambda e: e.scalar_tensor_tensor(lam_x, lam_x, 4.0, lam_n.bitcast(I32), ALU.mult, ALU.subtract), m)
        lam_e = fine_exp(lam_n.bitcast(I32), lam_x, lam_n, [m, consts_in])
        m = dve.do(lambda e: e.tensor_tensor(lam_x, lam_x, lam_n, ALU.mult), lam_e)
        lam_d = dve.do(lambda e: e.tensor_tensor(stats[:, 10:11], stats[:, 9:10], stats[:, 8:9], ALU.subtract), m)
        neg_lam = stats[:, 11:12]
        neg_lam_ready = dve.do(lambda e: e.tensor_scalar(neg_lam, stats[:, 10:11], -0.2, None, ALU.add), lam_d)

        rel_ready = []
        for h in range(NH):
            n, bank = work_banks.take()
            mark = pe.do(lambda e, h=h, bank=bank: e.matmul(bank[:, 0:TOK], const("flip"), hankel[:, h, :],
                                                            start=True, stop=True),
                         hankel_in, consts_in, work_banks.free[n])
            done = dve.do(lambda e, h=h, bank=bank: e.scalar_tensor_tensor(
                rel[:, h, :], bank[:, 0:TOK], 4.0, const("mask"), ALU.mult, ALU.add), mark)
            work_banks.free[n] = done
            rel_ready.append(done)
        hankel_read = mark

        qk_ready = {}

        def evict_qk(g, bank, mark):
            tile0 = 2 * g
            scale = 1.0
            if tile0 < 8 or 24 <= tile0 < 28:
                scale = 4 * Q_SCALE
            elif 16 <= tile0 < 20:
                scale = Q_SCALE
            done = act.do(lambda e: e.activation(qkT[:, tile0:tile0 + 2, :],
                                                 bank[:, :].rearrange("p (c t) -> p c t", c=2), ACT.Copy,
                                                 scale=scale), mark)
            qk_ready[tile0] = qk_ready[tile0 + 1] = done
            return done

        turned("w_qk", 4096, DK, xT_hi, xT_lo, h_in, evict_qk)

        v_ready = {}

        def evict_v(c, t, bank, mark):
            done = act.do(lambda e: e.activation(v1[:, t, c * 512:(c + 1) * 512], bank[:, :], ACT.Copy),
                          mark, hankel_read)
            v_ready[c, t] = done
            return done

        straight("w_v", 4, DK, xT_hi, xT_lo, h_in, evict_v)
        xT_read = stream.used[stream.at - 1]

        ss1 = stats[:, 16:64]
        act.program.append(lambda e: e.preload_act_table_set(EXPS))

        def token_tile(t):
            return (P, P) if t == 0 else (TOK, 0)

        def diff_scores(item, i):
            t, h, W = item["t"], item["h"], item["W"]
            item["banks"] = []
            for c in range(2):
                n, bank = work_banks.take()
                rows = slice(c * 64, (c + 1) * 64)
                mark = pe.do(lambda e, rows=rows, bank=bank: e.matmul(
                    bank[:, 0:W], qkT[rows, h, t * P:(t + 1) * P], qkT[rows, 8 + h, 0:W], start=True, stop=True),
                    qk_ready[h], qk_ready[8 + h], work_banks.free[n])
                item["banks"].append((n, bank, mark))

        def diff_soft(item, i):
            h, W, m0 = item["h"], item["W"], item["m0"]
            slot, s = b1["s"].of(i)
            p_slot, p = b1["p"].of(i)
            w_slot, w = b1["w"].of(i)
            m_slot, small = b1["small"].of(i)
            slope = 4 * 2.0 ** -(h + 1)
            biased = []
            for c, (n, bank, mark) in enumerate(item["banks"]):
                a = dve.do(lambda e, c=c, bank=bank: e.scalar_tensor_tensor(
                    s[:, c * W:(c + 1) * W], const("dist")[:, m0:m0 + W], slope, bank[:, 0:W], ALU.mult, ALU.add),
                    mark, b1["s"].free[slot])
                work_banks.free[n] = a
                biased.append(a)
            s3 = s[:, 0:2 * W].rearrange("p (c k) -> p c k", c=2)
            m = dve.do(lambda e: e.tensor_reduce(small[:, 0:2], s3, AX_X, ALU.max, negate=True),
                       biased, b1["small"].free[m_slot])
            quarters = p.bitcast(I32)
            rests = []
            for c in range(2):
                part = slice(c * W, (c + 1) * W)
                q = dve.do(lambda e, part=part, c=c: e.tensor_scalar(quarters[:, part], s[:, part], small[:, c:c + 1],
                                                                     -0.5, ALU.add, ALU.add), m, b1["p"].free[p_slot])
                rests.append(dve.do(lambda e, part=part, c=c: e.scalar_tensor_tensor(
                    s[:, part], s[:, part], small[:, c:c + 1], quarters[:, part], ALU.add, ALU.subtract), q))
            ex = fine_exp(quarters[:, 0:2 * W], s[:, 0:2 * W], p[:, 0:2 * W], rests)
            exps = [dve.do(lambda e, part=slice(c * W, (c + 1) * W), c=c: e.tensor_tensor_reduce(
                p[:, part], p[:, part], s[:, part], 1.0, 0.0, ALU.mult, ALU.add, small[:, 2 + c:3 + c]), ex)
                for c in range(2)]
            b1["s"].free[slot] = exps[-1]
            r = dve.do(lambda e: e.reciprocal(small[:, 4:6], small[:, 2:4]), exps)
            lr = dve.do(lambda e: e.tensor_scalar(small[:, 5:6], small[:, 5:6], neg_lam, None, ALU.mult),
                        r, neg_lam_ready)
            w0 = dve.do(lambda e: e.tensor_scalar(w[:, 0:W], p[:, 0:W], small[:, 4:5], None, ALU.mult),
                        r, b1["w"].free[w_slot])
            item["w"] = w
            item["w_slot"] = w_slot
            item["w_ready"] = dve.do(lambda e: e.scalar_tensor_tensor(
                w[:, 0:W], p[:, W:2 * W], small[:, 5:6], w[:, 0:W], ALU.mult, ALU.add), w0, lr)
            b1["p"].free[p_slot] = item["w_ready"]
            item["scale_out"], item["scale_ready"], item["small_slot"] = 1.0, None, m_slot

        def diff_turn(item, i):
            mark = weighted_values(item, i, item["w"], item["w_ready"], b1, None, None)
            b1["w"].free[item["w_slot"]] = mark

        diff_items = []
        for h in range(NH):
            for t in range(TT):
                W, m0 = token_tile(t)
                diff_items.append(dict(
                    t=t, h=h, W=W, m0=m0, width=2 * HD, out=y1[:, t, h * P:(h + 1) * P],
                    ss=ss1[:, t * 24 + h:t * 24 + h + 1], v=lambda k, h=h: v1[:, k, h * P:(h + 1) * P],
                    v_ready=[v_ready[h // 4, k] for k in range(TT)], out_free=h_in))
        pipeline(diff_items, [diff_scores, diff_soft, diff_turn, values_stage(b1)])

        SBW = 384
        half_tanh = qkT[:, 0:12, :].rearrange("p a t -> p (a t)")
        diff_read = diff_items[-1]["banks"][1][2]
        sb_items = [dict(h=h, tile=h // 2, rows=slice(64 * (h % 2), 64 * (h % 2) + 64), c0=1024 + h * HD)
                    for h in range(NH)]

        def sb_scores(item, i):
            tile, rows = item["tile"], item["rows"]
            n, bank = work_banks.take()

            def issue(e):
                e.matmul(bank[:, 0:TOK], qkT[rows, 20 + tile, 0:P], qkT[rows, 16 + tile, :], start=True, stop=True)
                return e.matmul(bank[:, TOK:SBW], qkT[rows, 20 + tile, P:TOK], qkT[rows, 16 + tile, P:TOK],
                                start=True, stop=True)

            item["z"] = (n, bank, pe.do(issue, qk_ready[20 + tile], qk_ready[16 + tile], work_banks.free[n]))

        def sb_tanh(item, i):
            n, z, mark = item["z"]
            item["tanh"] = half_tanh[:, i * SBW:(i + 1) * SBW]
            item["tanh_ready"] = act.do(lambda e: e.activation(item["tanh"], z[:, 0:SBW], ACT.Tanh, scale=0.5),
                                        mark, diff_read)
            work_banks.free[n] = item["tanh_ready"]

        pipeline(sb_items, [sb_scores, sb_tanh])
        act.program.append(lambda e: e.preload_act_table_set(EXPS))

        band_items = []
        for h in range(NH):
            for t in range(TT):
                W, m0 = token_tile(t)
                tile, rows = h // 2, slice(64 * (h % 2), 64 * (h % 2) + 64)
                c0 = 1536 + h * HD
                band_items.append(dict(
                    W=W, width=HD, scale=1.0, times4=True, mask=rel[:, h, m0:m0 + W], mask_ready=rel_ready[h],
                    scores=lambda e, bank, t=t, W=W, tile=tile, rows=rows: e.matmul(
                        bank[:, 0:W], qkT[rows, 24 + tile, t * P:(t + 1) * P], qkT[rows, 28 + tile, 0:W],
                        start=True, stop=True),
                    ready=[qk_ready[24 + tile], qk_ready[28 + tile]],
                    v=lambda k, c0=c0: v1[:, k, c0:c0 + HD], v_ready=[v_ready[3, k] for k in range(TT)],
                    out=y1[:, t, c0:c0 + HD], ss=ss1[:, t * 24 + 16 + h:t * 24 + 17 + h]))
        pipeline(band_items, softmax_stages(b1))

        def sb_softplus(item, i):
            n, z, mark = item["z"]
            slot, l = b1["s"].of(i)
            p_slot, d = b1["p"].of(i)
            l, d = l[:, 0:SBW], d[:, 0:SBW]
            th = item["tanh"]
            a = act.do(lambda e: e.activation(l, th, ACT.Abs), item["tanh_ready"], b1["s"].free[slot])
            a = act.do(lambda e: e.activation(l, l, ACT.Ln, bias=const("half"), scale=0.5), a)
            a = dve.do(lambda e: e.scalar_tensor_tensor(l, z[:, 0:SBW], 0.0, l, ALU.max, ALU.subtract), a, mark)
            item["d_ready"] = dve.do(lambda e: e.tensor_tensor(d, z[:, 0:SBW], l, ALU.subtract),
                                     a, b1["p"].free[p_slot])
            work_banks.free[n] = item["d_ready"]
            diagonal = l.rearrange("p (b q) -> p b q", b=3)[:, 0:3:2, :]
            item["l_ready"] = dve.do(lambda e: e.tensor_tensor(
                diagonal, diagonal, const("causal").unsqueeze(1).to_broadcast([P, 2, P]), ALU.mult),
                item["d_ready"])
            item["l"], item["d"], item["slot"], item["p_slot"] = l, d, slot, p_slot

        def sb_suffix(item, i):
            l, d = item["l"], item["d"]
            n, bank = work_banks.take()

            def issue(e):
                e.matmul(bank[:, 0:TOK], const("after"), l[:, 0:TOK], start=True, stop=True, skip_group_check=True)
                e.matmul(bank[:, P:TOK], const("ones"), l[:, TOK:SBW], start=False, stop=True,
                         skip_group_check=True)
                return e.matmul(bank[:, TOK:SBW], const("after"), l[:, TOK:SBW], start=False, stop=True,
                                skip_group_check=True)

            mark = pe.do(issue, item["l_ready"], work_banks.free[n])
            a = dve.do(lambda e: e.tensor_tensor(d, d, bank[:, 0:SBW], ALU.subtract), mark, item["d_ready"])
            work_banks.free[n] = a
            quarters = l.bitcast(I32)
            a = dve.do(lambda e: e.tensor_scalar(quarters, d, 4.0, -0.5, ALU.mult, ALU.add), a)
            a = dve.do(lambda e: e.scalar_tensor_tensor(d, d, 4.0, quarters, ALU.mult, ALU.subtract), a)
            a = fine_exp(quarters, d, l, a)
            a = dve.do(lambda e: e.tensor_tensor(d, d, l, ALU.mult), a)
            b1["s"].free[item["slot"]] = a
            diagonal = d.rearrange("p (b q) -> p b q", b=3)[:, 0:3:2, :]
            item["a_ready"] = dve.do(lambda e: e.tensor_tensor(
                diagonal, diagonal, const("causal").unsqueeze(1).to_broadcast([P, 2, P]), ALU.mult), a)

        def sb_values(item, i):
            d, c0 = item["d"], item["c0"]
            n, bank = work_banks.take()

            def issue(e):
                e.matmul(bank[:, 0:HD], d[:, 0:P], v1[:, 0, c0:c0 + HD], start=True, stop=True)
                e.matmul(bank[:, HD:2 * HD], d[:, P:TOK], v1[:, 0, c0:c0 + HD], start=True, stop=False)
                return e.matmul(bank[:, HD:2 * HD], d[:, TOK:SBW], v1[:, 1, c0:c0 + HD], start=False, stop=True)

            mark = pe.do(issue, item["a_ready"], [v_ready[2, k] for k in range(TT)], work_banks.free[n])
            slot, junk = b1["w"].of(i)
            done = act.do(lambda e: e.activation(y1[:, :, c0:c0 + HD],
                                                 bank[:, 0:2 * HD].rearrange("p (t c) -> p t c", t=2), ACT.Copy), mark)
            for t in range(TT):
                col = t * 24 + 8 + item["h"]
                done = act.do(lambda e, t=t, col=col: e.activation(
                    junk[:, 0:HD], bank[:, t * HD:(t + 1) * HD], ACT.Square, accum_out=ss1[:, col:col + 1]),
                    b1["w"].free[slot], done)
            b1["w"].free[slot] = done
            b1["p"].free[item["p_slot"]] = mark
            work_banks.free[n] = done
            item["done"] = done

        pipeline(sb_items, [sb_scores, sb_softplus, sb_suffix, sb_values])

        ss3 = ss1.rearrange("p (t h) -> p t h", t=TT)
        all_done = [sb_items[-1]["done"], band_items[-1]["done"], diff_items[-1]["done"]]
        a = inverse_rms([(ss3[:, :, 0:8], 2 * HD, 1e-5), (ss3[:, :, 8:24], HD, 1e-6)], ss1, 48, all_done)
        c = dve.do(lambda e: e.tensor_scalar(ss3[:, :, 0:8], ss3[:, :, 0:8], 0.8, None, ALU.mult), a)
        y_ready = []
        for t in range(TT):
            for lo_h, hi_h, c0, w in ((0, 8, 0, 2 * HD), (8, 24, 1024, HD)):
                view = y1[:, t, c0:c0 + 1024].rearrange("p (h c) -> p h c", c=w)
                scale = ss3[:, t, lo_h:hi_h].unsqueeze(2).to_broadcast([P, hi_h - lo_h, w])
                y_ready.append(dve.do(lambda e, view=view, scale=scale: e.tensor_tensor(view, view, scale, ALU.mult),
                                      c))
        y_in = turn_and_split(y1, DK, "y1", xT_hi, xT_lo, y_ready, xT_read)
        x_ready = []
        straight("w_o", 4, DK, xT_hi, xT_lo, y_in, add_to_x(x_ready))
        xT_read = stream.used[stream.at - 1]
        scope.close()
        block_free = [y_in, xT_read, sb_items[-1]["done"], c]

        def mlp(phases, gate, up, down, x_ready, gain_name, dst_free, xT_read, scope, tag):
            act_hi = sbuf(f"act_hi{tag}", [P, 2, PHASE, TOK], F32R, scope)
            act_lo = sbuf(f"act_lo{tag}", [P, 2, PHASE, TOK], F32R, scope)
            h_nat = sbuf(f"h_nat{tag}", [P, TT, D], F32, scope)
            conv = sbuf(f"conv{tag}", [P, 2, 2, TOK], F32, scope)
            prod = sbuf(f"prod{tag}", [P, 2, 2, TOK], F32, scope)
            prod_free = [None, None]
            h_done = rms_scaled(x, h_nat, D, x_ready[:], dst_free, 0)
            h_in = turn_and_split(h_nat, DK, gain_name, xT_hi, xT_lo, h_done, xT_read)
            acts_ready = {}
            down_read = {}

            def split_act(pair, src, ready):
                n, a = pair // (PHASE // 2), 2 * pair % PHASE
                hi, lo = act_hi[:, n % 2, a:a + 2, :], act_lo[:, n % 2, a:a + 2, :]
                free = down_read.get(n - 2)
                h = act.do(lambda e: e.activation(hi, src, ACT.Copy), ready, free)
                l = dve.do(lambda e: e.tensor_tensor(lo, src, hi.bitcast(F32), ALU.subtract), h, free)
                acts_ready[n, a] = acts_ready[n, a + 1] = [h, l]
                return [h, l]

            def gate_pair(pair):
                slot = pair % 2
                cv, pr = conv[:, slot], prod[:, slot]
                state = {}

                def evict_gate(g, bank, mark):
                    gates = bank[:, :].rearrange("p (c t) -> p c t", c=2)
                    first = [act.do(lambda e, c=c: e.activation(
                        cv[:, c, :], gates[:, c, :], ACT.Identity, bias=gain("convb", 2 * pair + c),
                        scale=gain("conv2", 2 * pair + c)), mark, prod_free[slot]) for c in range(2)]
                    last = []
                    for shift, tap in ((1, "conv1"), (2, "conv0")):
                        last = [dve.do(lambda e, c=c, shift=shift, tap=tap: e.scalar_tensor_tensor(
                            cv[:, c, shift:TOK], gates[:, c, 0:TOK - shift], gain(tap, 2 * pair + c),
                            cv[:, c, shift:TOK], ALU.mult, ALU.add), first, last) for c in range(2)]
                    th = act.do(lambda e: e.activation(pr, cv, ACT.Tanh, scale=0.5), last, prod_free[slot])
                    state["silu2"] = dve.do(lambda e: e.scalar_tensor_tensor(pr, pr, 1.0, cv, ALU.add, ALU.mult), th)
                    return last[-1]

                def evict_up(g, bank, mark):
                    ups = bank[:, :].rearrange("p (c t) -> p c t", c=2)
                    m = dve.do(lambda e: e.scalar_tensor_tensor(pr, pr, 0.5, ups, ALU.mult, ALU.mult),
                               state["silu2"], mark)
                    prod_free[slot] = split_act(pair, pr, m)
                    return m

                turned(gate, TURNED_COLS, DK, xT_hi, xT_lo, h_in, evict_gate, pair)
                turned(up, TURNED_COLS, DK, xT_hi, xT_lo, h_in, evict_up, pair)

            def square_pair(pair):
                slot = pair % 2
                cv, pr = conv[:, slot], prod[:, slot]

                def evict(g, bank, mark):
                    r = act.do(lambda e: e.activation(cv, bank[:, :].rearrange("p (c t) -> p c t", c=2), ACT.Relu),
                               mark, prod_free[slot])
                    m = dve.do(lambda e: e.tensor_tensor(pr, cv, cv, ALU.mult), r, prod_free[slot])
                    prod_free[slot] = split_act(pair, pr, m)
                    return r

                turned(up, TURNED_COLS, DK, xT_hi, xT_lo, h_in, evict, pair)

            def down_phase(n):
                a, b = phases[n]
                ready = [acts_ready[n, k] for k in range(b - a)]
                straight(down, 4, b - a, act_hi[:, n % 2], act_lo[:, n % 2], ready, add_to_x(x_ready))
                down_read[n] = stream.used[stream.at - 1]

            for n, (a, b) in enumerate(phases):
                for pair in range(a // 2, b // 2):
                    (gate_pair if gate else square_pair)(pair)
                if n:
                    down_phase(n - 1)
            down_phase(len(phases) - 1)
            return [h_in, x_ready, down_read[len(phases) - 1], prod_free]

        scope = ExitStack()
        block_free = mlp(phases1, "w_gate", "w_up1", "w_down1", x_ready, "ffn", block_free, xT_read, scope, "1")
        xT_read = stream.used[stream.at - 1]
        scope.close()

        scope = ExitStack()
        mixed = sbuf("mixed", [P, TT, MIX], F32, scope)
        q_idxT = sbuf("q_idxT", [P, 8, TOK], F32, scope)
        k_idxT = sbuf("k_idxT", [P, TOK], F32, scope)
        q_dT = sbuf("q_dT", [P, 8, TOK], F32, scope)
        k_dT = sbuf("k_dT", [P, 8, TOK], F32, scope)
        v_d = sbuf("v_d", [P, TT, 1024], F32, scope)
        tail = sbuf("tail", [P, TT, TAIL], F32, scope)
        c_q = sbuf("c_q", [P, TT, 512], F32, scope)
        staging = [sbuf(f"staging{i}", [P, TT, 1024], F32, scope) for i in range(2)]
        k_dup = sbuf("k_dup", [P, TT, P], F32, scope)
        cos = sbuf("cos", [P, TT, 32], F32, scope)
        sin = sbuf("sin", [P, TT, 32], F32, scope)
        angle = sbuf("angle", [P, TT, 32], F32, scope)
        rope_tmp = [sbuf(f"rope_tmp{i}", [P, 512], F32, scope) for i in range(3)]
        pos = sbuf("pos", [P, TT], I32, scope)
        posf = sbuf("posf", [P, TT], F32, scope)
        index = sbuf("index", [P, 384], F32, scope)
        top8 = sbuf("top8", [P, TT, 8], F32, scope)
        krT = sbuf("krT", [P, TOK], F32, scope)
        b2 = softmax_buffers(scope, "a2_", TOK)

        pos_in = load(others_in, pos[:, :], dram["positions"], "pos_landed", block_free)

        TWO_PI = (6.28125, 1.9350051879882812e-03, 3.0198694e-07)
        ROUND = 12582912.0
        a = dve.do(lambda e: e.tensor_copy(posf[:, :], pos[:, :]), pos_in, block_free)
        ang_ready = [dve.do(lambda e, t=t: e.tensor_scalar(angle[:, t, :], const("freq"), posf[:, t:t + 1], None,
                                                           ALU.mult), a) for t in range(TT)]
        trig_ready = []
        for dst, quarter in ((sin, 0.0), (cos, 0.25)):
            turns = rope_tmp[0][:, 0:64].rearrange("p (t f) -> p t f", t=TT)
            m = dve.do(lambda e, quarter=quarter: e.tensor_scalar(turns, angle[:, :, :], 0.15915494309189535, quarter,
                                                                  ALU.mult, ALU.add), ang_ready, trig_ready)
            m = dve.do(lambda e: e.tensor_scalar(turns, turns, ROUND, None, ALU.add), m)
            m = dve.do(lambda e: e.tensor_scalar(turns, turns, -ROUND, None, ALU.add), m)
            src = angle[:, :, :]
            for part in TWO_PI:
                m = dve.do(lambda e, src=src, part=part, dst=dst: e.scalar_tensor_tensor(
                    dst[:, :, :], turns, -part, src, ALU.mult, ALU.add), m)
                src = dst[:, :, :]
            if quarter:
                m = dve.do(lambda e: e.tensor_scalar(dst[:, :, :], dst[:, :, :], 1.5707963267948966, None, ALU.add), m)
            m = dve.do(lambda e, dst=dst: e.tensor_scalar(dst[:, :, :], dst[:, :, :], 3.1415925, -3.1415925,
                                                          ALU.min, ALU.max), m)
            trig_ready.append(act.do(lambda e, dst=dst: e.activation(dst[:, :, :], dst[:, :, :], ACT.Sin), m))

        def rope(view, heads, half, ready):
            step = 32 // half
            x1, x2 = view[:, :, :, 0:half], view[:, :, :, half:2 * half]
            shape = [P, TT, heads, half]
            co = cos[:, :, 0:32:step].unsqueeze(2).to_broadcast(shape)
            si = sin[:, :, 0:32:step].unsqueeze(2).to_broadcast(shape)
            t1, t2, t3 = (r[:, 0:TT * heads * half].rearrange("p (t h f) -> p t h f", t=TT, h=heads)
                          for r in rope_tmp)
            before = [rope.done, trig_ready, ready]
            a = dve.do(lambda e: e.tensor_tensor(t1, x1, co, ALU.mult), before)
            b = dve.do(lambda e: e.tensor_tensor(t2, x2, si, ALU.mult))
            c = dve.do(lambda e: e.tensor_tensor(t3, x1, si, ALU.mult))
            d = dve.do(lambda e: e.tensor_tensor(x2, x2, co, ALU.mult), b)
            a = dve.do(lambda e: e.tensor_tensor(x1, t1, t2, ALU.subtract), c)
            rope.done = dve.do(lambda e: e.tensor_tensor(x2, x2, t3, ALU.add), d)
            return [a, rope.done]

        rope.done = trig_ready

        def turn_tiles(src, tiles, dst, ready, scale=1.0, free=None):
            marks = {}
            for pair in range((tiles + 1) // 2):
                n, bank = work_banks.take()
                here = range(2 * pair, min(2 * pair + 2, tiles))

                def issue(e, bank=bank, here=here):
                    for j, tile in enumerate(here):
                        for t in range(TT):
                            last = e.transpose(bank[:, j * TOK + t * P:j * TOK + (t + 1) * P],
                                               src[:, t, tile * P:(tile + 1) * P], const("ident"))
                    return last

                mark = pe.do(issue, ready, work_banks.free[n])
                w = len(here)
                done = act.do(lambda e, bank=bank, here=here, w=w: e.activation(
                    dst[:, here[0]:here[0] + w, :], bank[:, 0:w * TOK].rearrange("p (c t) -> p c t", c=w),
                    ACT.Copy, scale=scale), mark, free)
                work_banks.free[n] = done
                for tile in here:
                    marks[tile] = done
            turn_tiles.read = mark
            return marks

        g_end = v_d[:, :, :].rearrange("p t c -> p (t c)")
        g_end_in = load(others_in, g_end, bass.AP(tensor=dram["final_gain_1"].tensor, offset=0, ap=[[0, P], [1, D]]),
                        "final_gain_1_landed", block_free)
        normed = rms_scaled(x, mixed, D, x_ready[:], block_free, 0)
        x_ready = [dve.do(lambda e, t=t: e.tensor_tensor(x[:, t, :], mixed[:, t, :], g_end, ALU.mult),
                          normed, g_end_in) for t in range(TT)]
        g_end_read = x_ready[:]
        h_done = rms_scaled(x, mixed, D, x_ready[:], x_ready[:], 0)
        h_in = turn_and_split(mixed, DK, "mix", xT_hi, xT_lo, h_done, xT_read)

        def copy_out(dst, marks, free=None):
            def evict(c, t, bank, mark):
                view = dst(c, t)
                done = act.do(lambda e: e.activation(view, bank[:, 0:view.shape[1]], ACT.Copy), mark, free)
                marks.append(done)
                return done
            return evict

        tail_done = []
        straight("w_tail", 1, DK, xT_hi, xT_lo, h_in, copy_out(lambda c, t: tail[:, t, :], tail_done, block_free),
                 width=TAIL)
        k_r, k_i, w_i = (tail[:, :, a:b] for a, b in ((256, 320), (320, 384), (384, 400)))

        def rope_key(src, half, dst, free):
            done = rope(src.unsqueeze(2), 1, half, tail_done)
            cp = [dve.do(lambda e, j=j: e.tensor_copy(k_dup[:, :, j * 64:(j + 1) * 64], src), done, free)
                  for j in range(2)]
            marks = turn_tiles(k_dup, 1, dst[:, :].unsqueeze(1), cp)
            return marks[0], turn_tiles.read

        k_idx_ready, k_dup_read = rope_key(k_i, 8, k_idxT, None)
        kr_ready, _ = rope_key(k_r, 32, krT, k_dup_read)
        w_idx_ready = dve.do(lambda e: e.tensor_scalar(w_i, w_i, IDX_HEADS ** -0.5, None, ALU.mult), tail_done)

        def staged(chunk0):
            pass

        def project(buf, marks, free):
            straight("w_in", 2, DK, xT_hi, xT_lo, h_in,
                     copy_out(lambda c, t: buf[:, t, c * 512:(c + 1) * 512], marks, free))

        m_qi = []
        project(staging[0], m_qi, block_free)
        r = rope(staging[0][:, :, :].rearrange("p t (h d) -> p t h d", d=64), IDX_HEADS, 8, m_qi)
        q_idx_ready = turn_tiles(staging[0], 8, q_idxT, r)
        staging0_free = turn_tiles.read
        m_qd = []
        project(staging[1], m_qd, block_free)
        r = rope(staging[1][:, :, :].rearrange("p t (h d) -> p t h d", d=P), 8, 16, m_qd)
        q_d_ready = turn_tiles(staging[1], 8, q_dT, r)
        staging1_free = turn_tiles.read

        index_of = (index[:, 0:P], index[:, P:384])
        relus = Slots([rope_tmp[i][:, 0:TOK] for i in range(3)])
        index_ready = []
        for t in range(TT):
            W, m0 = token_tile(t)
            index_ready.append(dve.do(lambda e, t=t, m0=m0, W=W: e.tensor_copy(index_of[t], const("mask")[:, m0:m0 + W]),
                                      block_free))
        mask_marks = index_ready
        index_ready = [None, None]
        idx_items = [dict(h=h, t=t) for h in range(IDX_HEADS) for t in range(TT)]
        relus.free = [rope.done] * 3

        def idx_scores(item, i):
            h, t = item["h"], item["t"]
            W, _ = token_tile(t)
            rows = slice(64 * (h % 2), 64 * (h % 2) + 64)
            n, bank = work_banks.take()
            mark = pe.do(lambda e: e.matmul(bank[:, 0:W], q_idxT[rows, h // 2, t * P:(t + 1) * P], k_idxT[rows, 0:W],
                                            start=True, stop=True),
                         q_idx_ready[h // 2], k_idx_ready, work_banks.free[n])
            slot, r = relus.of(i)
            relu = act.do(lambda e: e.activation(r[:, 0:W], bank[:, 0:W], ACT.Relu, scale=64 ** -0.5),
                          mark, relus.free[slot])
            work_banks.free[n] = relu
            item["r"], item["relu"], item["slot"] = r, relu, slot

        def idx_add(item, i):
            h, t, r = item["h"], item["t"], item["r"]
            W, _ = token_tile(t)
            w = tail[:, t, 384 + h:385 + h]
            if h == 0:
                a = dve.do(lambda e: e.tensor_scalar(index_of[t], r[:, 0:W], w, None, ALU.mult),
                           item["relu"], w_idx_ready, mask_marks)
            else:
                a = dve.do(lambda e: e.scalar_tensor_tensor(index_of[t], r[:, 0:W], w, index_of[t],
                                                            ALU.mult, ALU.add), item["relu"], index_ready[t])
            index_ready[t] = a
            relus.free[item["slot"]] = a

        pipeline(idx_items, [idx_scores, idx_add])

        for t in range(TT):
            W, m0 = token_tile(t)
            index_ready[t] = dve.do(lambda e, t=t, m0=m0, W=W: e.tensor_tensor(
                index_of[t], index_of[t], const("mask")[:, m0:m0 + W], ALU.add), index_ready[t])
        for _ in range(TOPK // 8):
            best = [dve.do(lambda e, t=t: e.max(top8[:, t, :], index_of[t]), index_ready[t]) for t in range(TT)]
            index_ready = [dve.do(lambda e, t=t: e.match_replace(index_of[t], top8[:, t, :], index_of[t], TAKEN),
                                  best[t]) for t in range(TT)]
        select_ready = [dve.do(lambda e, t=t: e.tensor_scalar(index_of[t], index_of[t], TAKEN / 2, NEG,
                                                              ALU.is_ge, ALU.mult), index_ready[t])
                        for t in range(TT)]

        m_kd = []
        project(staging[0], m_kd, staging0_free)
        r = rope(staging[0][:, :, :].rearrange("p t (h d) -> p t h d", d=P), 8, 16, [m_kd, index_ready])
        k_d_ready = turn_tiles(staging[0], 8, k_dT, r)
        staging0_free = turn_tiles.read
        m_vd = []
        project(v_d, m_vd, [block_free, g_end_read])
        m_cq = []
        straight("w_in", 1, DK, xT_hi, xT_lo, h_in, copy_out(lambda c, t: c_q[:, t, :], m_cq, block_free))
        xT_read = stream.used[stream.at - 1]
        act.program.append(lambda e: e.preload_act_table_set(EXPS))

        dsa_items = []
        for h in range(NH):
            for t in range(TT):
                W, _ = token_tile(t)
                dsa_items.append(dict(
                    W=W, width=P, scale=P ** -0.5, mask=index_of[t], mask_ready=select_ready[t],
                    scores=lambda e, bank, t=t, W=W, h=h: e.matmul(
                        bank[:, 0:W], q_dT[:, h, t * P:(t + 1) * P], k_dT[:, h, 0:W], start=True, stop=True),
                    ready=[q_d_ready[h], k_d_ready[h]],
                    v=lambda k, h=h: v_d[:, k, h * P:(h + 1) * P], v_ready=m_vd,
                    out=mixed[:, t, 1024 + h * P:1024 + (h + 1) * P], out_free=h_in))
        pipeline(dsa_items, softmax_stages(b2))

        c_kv = tail[:, :, 0:256]
        n_cq = rms_scaled(c_q, staging[1][:, :, 0:512], 512, m_cq, staging1_free, 2)
        cq_in = turn_and_split(staging[1][:, :, 0:512], 4, "cq", xT_hi, xT_lo, n_cq, xT_read)
        n_ckv = rms_scaled(c_kv, staging[1][:, :, 512:768], 256, tail_done, staging1_free, 4)
        ckv_in = turn_and_split(staging[1][:, :, 512:768], 2, "ckv", xT_hi, xT_lo, n_ckv, xT_read, 4)

        q_nT = staging[0][:, :, :].rearrange("p t (a c) -> p (t a) c", c=TOK)
        k_nT = q_idxT
        q_ready2, k_ready2 = {}, {}

        def evict_tiles(dst, marks, free):
            def evict(g, bank, mark):
                done = act.do(lambda e: e.activation(dst[:, 2 * g:2 * g + 2, :],
                                                     bank[:, :].rearrange("p (c t) -> p c t", c=2), ACT.Copy),
                              mark, free)
                marks[2 * g] = marks[2 * g + 1] = done
                return done
            return evict

        turned("w_qnope", 1024, 4, xT_hi, xT_lo, cq_in, evict_tiles(q_nT, q_ready2, staging0_free))
        q_rope = c_q
        m_qr = []
        straight("w_qrope", 1, 4, xT_hi, xT_lo, cq_in, copy_out(lambda c, t: q_rope[:, t, :], m_qr, [n_cq]))
        r = rope(q_rope[:, :, :].rearrange("p t (h d) -> p t h d", d=64), 8, 32, m_qr)
        q_rT = sbuf("q_rT", [P, 4, TOK], F32, scope)
        q_r_ready = turn_tiles(q_rope, 4, q_rT, r, free=block_free)
        idx_read = [idx_items[-1]["relu"], idx_items[-2]["relu"]]
        ckv_hi, ckv_lo = xT_hi[:, 4:6, :], xT_lo[:, 4:6, :]
        turned("w_knope", 1024, 2, ckv_hi, ckv_lo, ckv_in[4:6], evict_tiles(k_nT, k_ready2, idx_read))
        v_m = staging[1]
        m_vm = []
        straight("w_vmla", 2, 2, ckv_hi, ckv_lo, ckv_in[4:6],
                 copy_out(lambda c, t: v_m[:, t, c * 512:(c + 1) * 512], m_vm, [cq_in, ckv_in]))
        xT_read = stream.used[stream.at - 1]

        mla_items = []
        for h in range(NH):
            for t in range(TT):
                W, m0 = token_tile(t)
                rows = slice(64 * (h % 2), 64 * (h % 2) + 64)

                def scores(e, bank, t=t, W=W, h=h, rows=rows):
                    e.matmul(bank[:, 0:W], q_nT[:, h, t * P:(t + 1) * P], k_nT[:, h, 0:W], start=True, stop=False)
                    return e.matmul(bank[:, 0:W], q_rT[rows, h // 2, t * P:(t + 1) * P], krT[rows, 0:W],
                                    start=False, stop=True)

                mla_items.append(dict(
                    W=W, width=P, scale=192 ** -0.5, mask=const("mask")[:, m0:m0 + W], mask_ready=None,
                    scores=scores, ready=[q_ready2[h], k_ready2[h], q_r_ready[h // 2], kr_ready],
                    v=lambda k, h=h: v_m[:, k, h * P:(h + 1) * P], v_ready=m_vm,
                    out=mixed[:, t, h * P:(h + 1) * P], out_free=h_in))
        pipeline(mla_items, softmax_stages(b2))
        mixed_ready = [mla_items[-1]["done"], dsa_items[-1]["done"]]
        m_in = turn_and_split(mixed, DK, None, xT_hi, xT_lo, mixed_ready, xT_read)
        straight("w_out", 4, DK, xT_hi, xT_lo, m_in, add_to_x(x_ready))
        xT_read = stream.used[stream.at - 1]
        block_free = [m_in, xT_read, select_ready, x_ready]
        scope.close()

        scope = ExitStack()
        mT_hi = sbuf("mT_hi", [P, DK, TOK], F32R, scope)
        mT_lo = sbuf("mT_lo", [P, DK, TOK], F32R, scope)
        mem = sbuf("mem", [P, TT, D], F32, scope)
        kxT = sbuf("kxT", [P, 4, TOK], F32, scope)
        qxT = sbuf("qxT", [P, 4, TOK], F32, scope)
        v_x = sbuf("v_x", [P, TT, 512], F32, scope)
        o_x = sbuf("o_x", [P, TT, 512], F32, scope)
        h_x = sbuf("h_x", [P, TT, D], F32, scope)
        b3 = softmax_buffers(scope, "a3_", TOK)
        mem_in = load(others_in, mem[:, :, :], dram["mem"].rearrange("(t p) d -> p t d", p=P), "mem_landed",
                      block_free)
        n_mem = rms_scaled(mem, h_x, D, mem_in, block_free, 2)
        mem_T = turn_and_split(h_x, DK, "mem", mT_hi, mT_lo, n_mem, block_free)
        kx_ready, qx_ready, vx_ready = {}, {}, []
        turned("w_kx", 512, DK, mT_hi, mT_lo, mem_T, evict_tiles(kxT, kx_ready, block_free))
        straight("w_vx", 1, DK, mT_hi, mT_lo, mem_T, copy_out(lambda c, t: v_x[:, t, :], vx_ready, block_free))
        h_done = rms_scaled(x, h_x, D, x_ready[:], mem_T, 0)
        h_in = turn_and_split(h_x, DK, "cross", xT_hi, xT_lo, h_done, xT_read)
        turned("w_qx", 512, DK, xT_hi, xT_lo, h_in, evict_tiles(qxT, qx_ready, block_free))
        xT_read = stream.used[stream.at - 1]
        act.program.append(lambda e: e.preload_act_table_set(EXPS))
        x_items = []
        for h in range(4):
            for t in range(TT):
                x_items.append(dict(
                    W=TOK, width=P, scale=P ** -0.5, mask=None, mask_ready=None,
                    scores=lambda e, bank, t=t, h=h: e.matmul(
                        bank[:, 0:TOK], qxT[:, h, t * P:(t + 1) * P], kxT[:, h, :], start=True, stop=True),
                    ready=[qx_ready[h], kx_ready[h]],
                    v=lambda k, h=h: v_x[:, k, h * P:(h + 1) * P], v_ready=vx_ready,
                    out=o_x[:, t, h * P:(h + 1) * P], out_free=block_free))
        pipeline(x_items, softmax_stages(b3))
        o_in = turn_and_split(o_x, 4, None, xT_hi, xT_lo, x_items[-1]["done"], xT_read)
        straight("w_ox", 4, 4, xT_hi, xT_lo, o_in, add_to_x(x_ready))
        xT_read = stream.used[stream.at - 1]
        block_free = [o_in, xT_read, x_ready, x_items[-1]["done"]]
        scope.close()

        scope = ExitStack()
        block_free = mlp(phases2, None, "w_up2", "w_down2", x_ready, "mlp", block_free, xT_read, scope, "2")
        scope.close()

        assert stream.at == len(plan)
        scope = ExitStack()
        g_final = sbuf("g_final", [P, D], F32, scope)
        result = sbuf("result", [P, TT, D], F32, scope)
        g_in = load(others_in, g_final[:, :], bass.AP(tensor=dram["final_gain"].tensor, offset=0, ap=[[0, P], [1, D]]),
                    "final_gain_landed", block_free)
        norm = rms_scaled(x, result, D, x_ready[:], block_free, 0)
        stored = ctx.enter_context(nc.semaphore("stored"))
        for t in range(TT):
            done = dve.do(lambda e, t=t: e.tensor_tensor(result[:, t, :], result[:, t, :], g_final[:, :], ALU.mult),
                          norm[t], g_in)
            others_in.wait(done)
            others_in.program.append(lambda e, t=t: e.dma_start(out_dram[t * P:(t + 1) * P, :], result[:, t, :])
                                     .then_inc(stored, 16))
        others_in.wait((stored, 16 * TT))
        scope.close()

        block = ctx.enter_context(nc.Block())

        @block.sync
        def _(e):
            weights_in.run(e)

        @block.gpsimd
        def _(e):
            others_in.run(e)

        @block.scalar
        def _(e):
            act.run(e)

        @block.vector
        def _(e):
            dve.run(e)

        @block.tensor
        def _(e):
            pe.run(e)


def lay_turned(w):
    k, c = w.shape
    per = min(4, k // P)
    return np.ascontiguousarray(w.reshape(k // P // per, per, P, c // TURNED_COLS, TURNED_COLS).transpose(3, 0, 2, 1, 4))


def lay_straight(w, width=STRAIGHT_COLS):
    k, c = w.shape
    return np.ascontiguousarray(w.reshape(k // P // 2, 2, P, c // width, width).transpose(3, 0, 2, 1, 4))


def lay_gain(g):
    return g.reshape(-1, P).T


def constants():
    i = np.arange(P)
    q = P + i[:, None]
    k = np.arange(TOK)[None, :]
    mask = np.where(k // CHUNK <= q // CHUNK, 0.0, NEG)
    parts = {
        "ident": np.eye(P), "flip": np.eye(P)[::-1],
        "after": i[:, None] > i[None, :],
        "causal": i[:, None] < i[None, :],
        "ones": np.ones((P, P)),
        "mask": mask,
        "dist": np.where(mask == 0.0, -np.abs(q - k), NEG),
        "half": np.full((P, 1), 0.5), "eighth": np.full((P, 1), 0.125), "less_eighth": np.full((P, 1), -0.125),
        "freq": np.broadcast_to(np.float32(500000.0) ** (-np.arange(32, dtype=np.float32) / np.float32(32)), (P, 32)),
    }
    return np.ascontiguousarray(np.concatenate([parts[n].astype(np.float32) for n, _ in CONSTS], axis=1))


def kernel(**inputs):
    import concourse.bacc as bacc
    from concourse.bass_utils import run_bass_kernel_spmd

    i = {k: np.asarray(v) for k, v in inputs.items()}
    qkv, w_in = i["w_qkv"][0], i["w_in_2"][0]
    qb = i["w_qb_2"][0].reshape(512, 8, 192)
    kvb = i["w_kvb_2"][0].reshape(256, 8, 256)
    gains = {
        "attn": i["attn_norm"][0], "ffn": i["ffn_norm"][0],
        "y1": np.concatenate([np.tile(i["diff_subln"][0], NH), i["sb_norm"][0].ravel(), i["ch_norm"][0].ravel()]),
        "conv0": i["conv_w"][0, 0], "conv1": i["conv_w"][0, 1], "conv2": i["conv_w"][0, 2], "convb": i["conv_b"][0],
        "mix": i["g_mix_2"][0], "cq": i["g_cq_2"][0], "ckv": i["g_ckv_2"][0], "cross": i["g_cross_2"][0],
        "mem": i["g_mem_2"][0], "mlp": i["g_mlp_2"][0],
    }
    arrays = {
        "x": i["x"][0], "mem": i["mem_2"][0],
        "consts": constants(),
        "gains": np.concatenate([lay_gain(gains[n]) for n, _ in GAINS], axis=1),
        "lambdas": np.concatenate([i["lambda_q1"], i["lambda_k1"], i["lambda_q2"], i["lambda_k2"]]),
        "rel_rev": i["rel_bias"][0][:, ::-1],
        "positions": i["positions_2"][0].reshape(TT, P).T,
        "final_gain_1": i["final_norm"], "final_gain": i["g_final_2"],
        "w_qk": lay_turned(np.concatenate([qkv[:, 0:2048], qkv[:, 3072:4096], qkv[:, 4608:5632]], axis=1)),
        "w_v": lay_straight(np.concatenate([qkv[:, 2048:3072], qkv[:, 4096:4608], qkv[:, 5632:6144]], axis=1)),
        "w_o": lay_straight(i["w_o"][0]),
        "w_gate": lay_turned(i["w_gate"][0]), "w_up1": lay_turned(i["w_up"][0]),
        "w_down1": lay_straight(i["w_down"][0]),
        "w_tail": lay_straight(np.concatenate([w_in[:, C_KV:Q_D], w_in[:, K_IDX:]], axis=1), TAIL),
        "w_in": lay_straight(np.concatenate([w_in[:, Q_IDX:K_IDX], w_in[:, Q_D:Q_IDX], w_in[:, C_Q:C_KV]], axis=1)),
        "w_qnope": lay_turned(qb[:, :, 0:P].reshape(512, 1024)),
        "w_qrope": lay_straight(qb[:, :, P:].reshape(512, 512)),
        "w_knope": lay_turned(kvb[:, :, 0:P].reshape(256, 1024)),
        "w_vmla": lay_straight(kvb[:, :, P:].reshape(256, 1024)),
        "w_out": lay_straight(i["w_out_2"][0]),
        "w_qx": lay_turned(i["w_q_cross_2"][0]), "w_kx": lay_turned(i["w_k_cross_2"][0]),
        "w_vx": lay_straight(i["w_v_cross_2"][0]), "w_ox": lay_straight(i["w_o_cross_2"][0]),
        "w_up2": lay_turned(i["w_up_2"][0]), "w_down2": lay_straight(i["w_down_2"][0]),
    }
    nc = bacc.Bacc("TRN2", target_bir_lowering=False, num_devices=1)
    arrays = {f"in_{n}": np.ascontiguousarray(a) for n, a in arrays.items()}
    dram = {n[3:]: nc.dram_tensor(n, a.shape, mybir.dt.from_np(a.dtype), kind="ExternalInput").ap()
            for n, a in arrays.items()}
    out = nc.dram_tensor("out", (TOK, D), F32, kind="ExternalOutput").ap()
    build_program(nc, dram, out)
    r = run_bass_kernel_spmd(nc, [arrays], core_ids=[0])
    return r.results[0]["out"].reshape(1, TOK, D)
```

```python
from contextlib import ExitStack

import numpy as np
import concourse.bass as bass
from concourse import mybir

F32 = mybir.dt.float32
F32R = mybir.dt.float32r
I32 = mybir.dt.int32
ALU = mybir.AluOpType
ACT = mybir.ActivationFunctionType
AX_X = mybir.AxisListType.X

P = 128
TOK = 256
TT = TOK // P
D = 2048
DK = D // P
CHUNK = 64
F1 = 5632
F2 = 8192
HD = 64
NH = 8
MIX = 2048
N_REL = 192
IDX_HEADS = 16
TOPK = 64
NEG = -1.0e30
TAKEN = -3.0e38
PHASE = 16
TURNED_COLS = 256
STRAIGHT_COLS = 512
UNIT = 1024
RAW_SLOTS = 4
SPLIT_SLOTS = 4
EXPS = "natural_log_exp_and_others"

C_Q, C_KV, K_ROPE, Q_D, K_D, V_D, Q_IDX, K_IDX, W_IDX = 0, 512, 768, 832, 1856, 2880, 3904, 4928, 4992
TAIL = 256 + 64 + 64 + 16

CONSTS = [("ident", P), ("flip", P), ("after", P), ("causal", P), ("ones", P),
          ("mask", TOK), ("blocked", TOK), ("dist", TOK), ("freq", 32), ("half", 1), ("eighth", 1), ("less_eighth", 1)]
GAINS = [("attn", 16), ("y1", 16), ("ffn", 16), ("conv0", 44), ("conv1", 44), ("conv2", 44), ("convb", 44),
         ("mix", 16), ("cq", 4), ("ckv", 2), ("cross", 16), ("mem", 16), ("mlp", 16)]


def columns_of(table):
    at, out = 0, {}
    for name, width in table:
        out[name] = (at, at + width)
        at += width
    return out, at


class Engine:

    def __init__(self, semaphore):
        self.semaphore, self.count, self.program, self.reached = semaphore, 0, [], {}

    def wait(self, *marks):
        for mark in flat(marks):
            semaphore, value = mark
            if self.reached.get(semaphore.name, 0) < value:
                self.reached[semaphore.name] = value
                self.program.append(lambda e, s=semaphore, v=value: e.wait_ge(s, v))

    def do(self, issue, *marks):
        self.wait(*marks)
        self.count += 1
        self.program.append(lambda e: issue(e).then_inc(self.semaphore, 1))
        return (self.semaphore, self.count)

    def run(self, e):
        for step in self.program:
            step(e)


def flat(marks):
    for m in marks:
        if m is None:
            continue
        if isinstance(m, list):
            yield from flat(m)
        else:
            yield m


class Banks:

    def __init__(self, banks):
        self.banks, self.free, self.at = banks, [None] * len(banks), 0

    def take(self):
        n = self.at % len(self.banks)
        self.at += 1
        return n, self.banks[n]


class Slots:

    def __init__(self, views):
        self.views, self.free = views, [None] * len(views)

    def of(self, i):
        return i % len(self.views), self.views[i % len(self.views)]


def build_program(nc, dram, out_dram):
    const_at, n_const = columns_of(CONSTS)
    gain_at, n_gain = columns_of(GAINS)

    ctx = ExitStack()
    with ctx:
        def sbuf(name, shape, dt=F32, scope=ctx):
            return scope.enter_context(nc.sbuf_tensor(name, shape, dt))

        raw_w = sbuf("raw_w", [P, RAW_SLOTS, UNIT])
        hi_w = sbuf("hi_w", [P, SPLIT_SLOTS, UNIT], F32R)
        lo_w = sbuf("lo_w", [P, SPLIT_SLOTS, UNIT], F32R)
        x = sbuf("x", [P, TT, D])
        xT_hi = sbuf("xT_hi", [P, DK, TOK], F32R)
        xT_lo = sbuf("xT_lo", [P, DK, TOK], F32R)
        consts = sbuf("consts", [P, n_const])
        gains = sbuf("gains", [P, n_gain])
        stats = sbuf("stats", [P, 192])
        banks = [ctx.enter_context(nc.psum_tensor(f"bank{i}", [P, 512], F32)) for i in range(8)]

        pe = Engine(ctx.enter_context(nc.semaphore("pe_done")))
        act = Engine(ctx.enter_context(nc.semaphore("act_done")))
        dve = Engine(ctx.enter_context(nc.semaphore("dve_done")))
        weights_in = Engine(None)
        others_in = Engine(None)
        raw_landed = [ctx.enter_context(nc.semaphore(f"raw_landed{i}")) for i in range(RAW_SLOTS)]

        def const(name):
            a, b = const_at[name]
            return consts[:, a:b]

        def gain(name, k):
            a = gain_at[name][0]
            return gains[:, a + k:a + k + 1]

        def load(queue, dst, src, name, *marks):
            landed = ctx.enter_context(nc.semaphore(name))
            queue.wait(*marks)
            queue.program.append(lambda e: e.dma_start(dst, src).then_inc(landed, 16))
            return (landed, 16)

        gemm_banks = Banks(banks[0:4])
        work_banks = Banks(banks[4:8])

        x_in = load(others_in, x[:, :, :], dram["x"].rearrange("(t p) d -> p t d", p=P), "x_landed")
        consts_in = load(others_in, consts[:, :], dram["consts"], "consts_landed")
        gains_in = load(others_in, gains[:, :], dram["gains"], "gains_landed")

        def units_turned(name, groups, kts):
            per = min(4, kts)
            return [(name, g, u) for g in groups for u in range(kts // per)]

        def units_straight(name, chunks, kts, k0=0):
            return [(name, c, k0 // 2 + u) for c in chunks for u in range(kts // 2)]

        phases1 = [(a, min(a + PHASE, F1 // P)) for a in range(0, F1 // P, PHASE)]
        phases2 = [(a, min(a + PHASE, F2 // P)) for a in range(0, F2 // P, PHASE)]

        def mlp_units(phases, ups, down):
            out = []
            for n, (a, b) in enumerate(phases):
                for pair in range(a // 2, b // 2):
                    for name in ups:
                        out += units_turned(name, [pair], DK)
                if n:
                    out += units_straight(down, range(4), phases[n - 1][1] - phases[n - 1][0], phases[n - 1][0])
            return out + units_straight(down, range(4), phases[-1][1] - phases[-1][0], phases[-1][0])

        QKV_ORDER = [("w_qk", [0, 1, 4, 5]), ("w_v", [0]), ("w_qk", [2, 3, 6, 7]), ("w_v", [1]),
                     ("w_qk", [8, 9, 10, 11]), ("w_v", [2]), ("w_qk", [12, 13, 14, 15]), ("w_v", [3])]
        plan = []
        for name, parts in QKV_ORDER:
            plan += (units_turned if name == "w_qk" else units_straight)(name, parts, DK)
        plan += units_straight("w_o", range(4), 12) + units_straight("w_o", range(4), 4, 12)
        plan += mlp_units(phases1, ["w_gate", "w_up1"], "w_down1")
        plan += units_straight("w_tail", [0], DK) + units_straight("w_in", [8, 0, 1], DK)
        plan += units_turned("w_qnope", range(4), 4) + units_straight("w_qrope", [0], 4)
        plan += units_turned("w_knope", range(4), 2) + units_straight("w_vmla", range(2), 2)
        plan += units_straight("w_in", range(2, 8), DK)
        plan += units_straight("w_out", range(4), 8) + units_straight("w_out", range(4), 8, 8)
        plan += units_turned("w_kx", range(2), DK) + units_turned("w_qx", range(2), DK)
        plan += units_straight("w_vx", [0], DK) + units_straight("w_ox", range(4), 4)
        plan += mlp_units(phases2, ["w_up2"], "w_down2")

        def unit_source(u):
            name, part, k = plan[u]
            return dram[name][part, k].rearrange("p k c -> p (k c)")

        class WeightStream:

            def __init__(self):
                self.loaded = self.split_up_to = self.at = 0
                self.split_done = {}
                self.used = {}
                for _ in range(RAW_SLOTS):
                    self.load()
                for _ in range(SPLIT_SLOTS - 1):
                    self.split()

            def load(self):
                u = self.loaded
                if u >= len(plan):
                    return
                self.loaded += 1
                slot, src = u % RAW_SLOTS, unit_source(u)
                weights_in.wait(self.split_done.get(u - RAW_SLOTS))
                weights_in.program.append(
                    lambda e: e.dma_start(raw_w[:, slot, 0:src.shape[1]], src).then_inc(raw_landed[slot], 16))

            def split(self):
                u = self.split_up_to
                if u >= len(plan):
                    return
                self.split_up_to += 1
                n = unit_source(u).shape[1]
                raw = raw_w[:, u % RAW_SLOTS, 0:n]
                hi, lo = hi_w[:, u % SPLIT_SLOTS, 0:n], lo_w[:, u % SPLIT_SLOTS, 0:n]
                landed = (raw_landed[u % RAW_SLOTS], 16 * (u // RAW_SLOTS + 1))
                free = self.used.get(u - SPLIT_SLOTS)
                hi_done = act.do(lambda e: e.activation(hi, raw, ACT.Copy), landed, free)
                lo_done = dve.do(lambda e: e.tensor_tensor(lo, raw, hi.bitcast(F32), ALU.subtract), hi_done)
                self.split_done[u] = [lo_done, hi_done]
                self.load()

            def take(self, name, part, k):
                assert plan[self.at] == (name, part, k), (plan[self.at], name, part, k)
                self.split()
                u, n = self.at, unit_source(self.at).shape[1]
                return hi_w[:, u % SPLIT_SLOTS, 0:n], lo_w[:, u % SPLIT_SLOTS, 0:n], self.split_done[u][0]

            def release(self, mark):
                self.used[self.at] = mark
                self.at += 1

        stream = WeightStream()

        def turned(name, groups, kts, in_hi, in_lo, in_ready, evict):
            per = min(4, kts)
            for g in groups:
                n, bank = gemm_banks.take()
                done = None
                for u in range(kts // per):
                    w_hi, w_lo, w_ready = stream.take(name, g, u)

                    def issue(e, u=u, w_hi=w_hi, w_lo=w_lo, bank=bank):
                        for c in range(2):
                            o = bank[:, c * TOK:(c + 1) * TOK]
                            for k in range(per):
                                kt = u * per + k
                                cols_k = slice(k * TURNED_COLS + c * P, k * TURNED_COLS + (c + 1) * P)
                                passes = [(w_hi, in_hi), (w_hi, in_lo), (w_lo, in_hi)]
                                for i, (w, v) in enumerate(passes):
                                    last = e.matmul(o, w[:, cols_k], v[:, kt, :],
                                                    start=(kt == 0 and c == 0 and i == 0),
                                                    stop=(kt == kts - 1 and i == 2), skip_group_check=True)
                        return last

                    ready = [in_ready[u * per + k] for k in range(per)]
                    done = pe.do(issue, w_ready, ready, gemm_banks.free[n] if u == 0 else None)
                    stream.release(done)
                    if u < kts // per - 1:
                        yield
                gemm_banks.free[n] = evict(g, bank, done)
                yield

        def straight(name, chunks, kts, in_hi, in_lo, in_ready, evict, width=STRAIGHT_COLS, k0=0, in0=None):
            in0 = k0 if in0 is None else in0
            for c in chunks:
                pair = [gemm_banks.take() for _ in range(TT)]
                done = None
                for u in range(kts // 2):
                    w_hi, w_lo, w_ready = stream.take(name, c, k0 // 2 + u)

                    def issue(e, u=u, w_hi=w_hi, w_lo=w_lo, pair=pair):
                        for t in range(TT):
                            for k in range(2):
                                kt = u * 2 + k
                                cols_k = slice(k * width, (k + 1) * width)
                                rows = slice(t * P, (t + 1) * P)
                                passes = [(in_hi, w_hi), (in_hi, w_lo), (in_lo, w_hi)]
                                for i, (v, w) in enumerate(passes):
                                    last = e.matmul(pair[t][1][:, 0:width], v[:, in0 + kt, rows], w[:, cols_k],
                                                    start=(kt == 0 and i == 0),
                                                    stop=(kt == kts - 1 and i == 2))
                        return last

                    ready = [in_ready[in0 + u * 2 + k] for k in range(2)]
                    free = [gemm_banks.free[n] for n, _ in pair] if u == 0 else None
                    done = pe.do(issue, w_ready, ready, free)
                    stream.release(done)
                    if u < kts // 2 - 1:
                        yield
                for t, (n, bank) in enumerate(pair):
                    gemm_banks.free[n] = evict(c, t, bank, done)
                yield

        class Filler:

            def __init__(self, *products):
                self.left = (None for product in products for _ in product)

            def advance(self, units):
                for _ in range(units):
                    next(self.left, None)

            def until(self, have):
                while not have():
                    next(self.left)

            def finish(self):
                for _ in self.left:
                    pass

        def run(product):
            for _ in product:
                pass

        def inverse_rms(parts, ss, width, ready):
            r, t = stats[:, 64:64 + width], stats[:, 128:128 + width]
            a = [dve.do(lambda e, view=view, n=n, eps=eps: e.tensor_scalar(view, view, 1.0 / n, eps,
                                                                           ALU.mult, ALU.add), ready)
                 for view, n, eps in parts]
            b = act.do(lambda e: e.activation(r, ss, ACT.Sqrt), a)
            b = dve.do(lambda e: e.reciprocal(r, r), b)
            c = dve.do(lambda e: e.tensor_tensor(t, r, r, ALU.mult), b)
            c = dve.do(lambda e: e.tensor_tensor(t, t, ss, ALU.mult), c)
            c = dve.do(lambda e: e.tensor_scalar(t, t, -0.5, 1.5, ALU.mult, ALU.add), c)
            return dve.do(lambda e: e.tensor_tensor(ss, r, t, ALU.mult), c)

        def fine_exp(quarters, rest, out, ready, out_free=None):
            a = act.do(lambda e: e.activation(out, quarters, ACT.Exp, bias=const("eighth"), scale=0.25),
                       ready, out_free)
            b = act.do(lambda e: e.activation(rest, rest, ACT.Exp, bias=const("less_eighth"), scale=0.25))
            return [a, b]

        def rms_scaled(src, dst, n, ready, dst_free, stat):
            marks = []
            for t in range(TT):
                ss = stats[:, stat + t:stat + t + 1]
                marks.append(act.do(lambda e, t=t, ss=ss: e.activation(dst[:, t, :], src[:, t, :], ACT.Square,
                                                                       accum_out=ss), ready, dst_free))
            ss = stats[:, stat:stat + TT]
            scale = inverse_rms([(ss, n, 1e-6)], ss, TT, marks)
            return [dve.do(lambda e, t=t: e.tensor_scalar(dst[:, t, :], src[:, t, :],
                                                          stats[:, stat + t:stat + t + 1], None, ALU.mult),
                           scale) for t in range(TT)]

        def turn_and_split(src, n_kt, gain_name, dst_hi, dst_lo, ready, dst_free, kt0=0, src0=None):
            src0 = kt0 if src0 is None else src0
            done = [None] * (kt0 + n_kt)
            for pair in range(n_kt // 2):
                n, bank = work_banks.take()

                def issue(e, pair=pair, bank=bank):
                    for k in range(2):
                        for t in range(TT):
                            kt = src0 + pair * 2 + k
                            last = e.transpose(bank[:, k * TOK + t * P:k * TOK + (t + 1) * P],
                                               src[:, t, kt * P:(kt + 1) * P], const("ident"))
                    return last

                turned_mark = pe.do(issue, ready, work_banks.free[n], consts_in)
                his = []
                for k in range(2):
                    kt = pair * 2 + k
                    half, hi = bank[:, k * TOK:(k + 1) * TOK], dst_hi[:, kt0 + kt, :]
                    scale = gain(gain_name, src0 + kt) if gain_name else 1.0
                    his.append(act.do(lambda e, hi=hi, half=half, scale=scale:
                                      e.activation(hi, half, ACT.Copy, scale=scale),
                                      turned_mark, dst_free, gains_in))
                for k in range(2):
                    kt = pair * 2 + k
                    half, hi, lo = bank[:, k * TOK:(k + 1) * TOK], dst_hi[:, kt0 + kt, :], dst_lo[:, kt0 + kt, :]
                    scale = gain(gain_name, src0 + kt) if gain_name else 1.0
                    done[kt0 + kt] = dve.do(lambda e, hi=hi, half=half, lo=lo, scale=scale:
                                            e.scalar_tensor_tensor(lo, half, scale, hi.bitcast(F32),
                                                                   ALU.mult, ALU.subtract),
                                            his, dst_free, gains_in)
                work_banks.free[n] = done[kt0 + pair * 2 + 1]
            return done

        def add_to_x(x_ready):
            def evict(c, t, bank, mark):
                cols = slice(c * STRAIGHT_COLS, (c + 1) * STRAIGHT_COLS)
                done = dve.do(lambda e: e.tensor_tensor(x[:, t, cols], bank[:, :], x[:, t, cols], ALU.add),
                              mark, x_ready[:])
                x_ready.append(done)
                return done
            return evict

        FILL = None

        def pipeline(items, stages, filler=None, rate=0.0):
            due = 0.0
            for s in range(len(items) + max(stage[0] for stage in stages if stage)):
                for stage in stages:
                    if stage is FILL:
                        due += rate
                        if filler and due >= 1:
                            filler.advance(int(due))
                            due -= int(due)
                    elif 0 <= s - stage[0] < len(items):
                        stage[1](items[s - stage[0]], s - stage[0])

        def softmax_buffers(scope, prefix, wide):
            b = {}
            for name, depth, width in (("s", 3, wide), ("p", 3, wide), ("pT", 2, TOK)):
                t = sbuf(prefix + name, [P, depth, width], F32, scope)
                b[name] = Slots([t[:, i, :] for i in range(depth)])
            small = sbuf(prefix + "small", [P, 4, 8], F32, scope)
            b["small"] = Slots([small[:, i, :] for i in range(4)])
            return b

        def turn_stage(b):
            def stage(item, i):
                kts, weights = item["W"] // P, item["p"]
                n, bank = work_banks.take()

                def turn(e):
                    for k in range(kts):
                        last = e.transpose(bank[:, k * P:(k + 1) * P], weights[:, k * P:(k + 1) * P], const("ident"))
                    return last

                mark = pe.do(turn, item["p_ready"], work_banks.free[n])
                b["p"].free[item["p_slot"]] = mark
                slot, pT = b["pT"].of(i)
                copied = act.do(lambda e: e.activation(pT[:, 0:kts * P], bank[:, 0:kts * P], ACT.Copy),
                                mark, b["pT"].free[slot])
                work_banks.free[n] = copied
                item["pT"], item["pT_ready"], item["pT_slot"] = pT, copied, slot
            return stage

        def values_stage(b):
            def stage(item, i):
                kts, pT = item["W"] // P, item["pT"]
                n, bank = work_banks.take()
                wide = item["width"]

                def issue(e):
                    for k in range(kts):
                        last = e.matmul(bank[:, 0:wide], pT[:, k * P:(k + 1) * P], item["v"](k),
                                        start=(k == 0), stop=(k == kts - 1))
                    return last

                mark = pe.do(issue, item["pT_ready"], item["v_ready"](), work_banks.free[n])
                b["pT"].free[item["pT_slot"]] = mark
                scale = item["scale_out"]
                done = act.do(lambda e: e.activation(item["out"], bank[:, 0:wide], ACT.Copy, scale=scale),
                              mark, item["scale_ready"], item.get("out_free"))
                if "ss" in item:
                    slot, junk = b["s"].of(i)
                    junk_free = b["s"].free[slot]
                    done = act.do(lambda e: e.activation(junk[:, 0:wide], bank[:, 0:wide], ACT.Square,
                                                         scale=scale, accum_out=item["ss"]), junk_free)
                    b["s"].free[slot] = [b["s"].free[slot], done]
                b["small"].free[item["small_slot"]] = done
                work_banks.free[n] = done
                item["done"] = done
            return stage

        def softmax_stages(b, values=None):
            def scores(item, i):
                n, bank = work_banks.take()
                mark = pe.do(lambda e: item["scores"](e, bank), item["ready"](), work_banks.free[n])
                item["bank"], item["bank_n"], item["mark"] = bank, n, mark

            def soft(item, i):
                W, bank = item["W"], item["bank"]
                slot, s = b["s"].of(i)
                p_slot, p = b["p"].of(i)
                m_slot, small = b["small"].of(i)
                free = [b["s"].free[slot], b["small"].free[m_slot]]
                if item["kind"] == "fine":
                    m = dve.do(lambda e: e.tensor_tensor_reduce(s[:, 0:W], bank[:, 0:W], item["mask"], 1.0, TAKEN,
                                                                ALU.add, ALU.max, small[:, 0:1]),
                               item["mark"], item["mask_ready"], free)
                    work_banks.free[item["bank_n"]] = m
                    quarters = p.bitcast(I32)
                    q = dve.do(lambda e: e.tensor_scalar(quarters[:, 0:W], s[:, 0:W], small[:, 0:1], -0.5,
                                                         ALU.subtract, ALU.add), m, b["p"].free[p_slot])
                    q = dve.do(lambda e: e.scalar_tensor_tensor(s[:, 0:W], s[:, 0:W], small[:, 0:1],
                                                                quarters[:, 0:W], ALU.subtract, ALU.subtract), q)
                    ex = q
                elif item["kind"] == "masked":
                    m = dve.do(lambda e: e.tensor_tensor_reduce(s[:, 0:W], bank[:, 0:W], item["mask"], 1.0, -TAKEN,
                                                                ALU.add, ALU.min, small[:, 0:1]),
                               item["mark"], item["mask_ready"], free)
                    work_banks.free[item["bank_n"]] = m
                    ex = act.do(lambda e: e.activation(p[:, 0:W], s[:, 0:W], ACT.Exp, bias=small[:, 0:1], scale=-1.0,
                                                       accum_out=small[:, 1:2]), m, b["p"].free[p_slot])
                else:
                    m = dve.do(lambda e: e.tensor_reduce(small[:, 0:1], bank[:, 0:W], AX_X, ALU.max, negate=True),
                               item["mark"], free)
                    ex = act.do(lambda e: e.activation(p[:, 0:W], bank[:, 0:W], ACT.Exp, bias=small[:, 0:1],
                                                       accum_out=small[:, 1:2]), m, b["p"].free[p_slot])
                    work_banks.free[item["bank_n"]] = ex
                b["s"].free[slot] = ex
                item["s"], item["s_slot"] = s, slot
                item["p"], item["p_slot"], item["p_ready"] = p, p_slot, ex
                item["small"], item["small_slot"] = small, m_slot

            def fine(item, i):
                W, s, p = item["W"], item["s"], item["p"]
                if item["kind"] == "fine":
                    item["p_ready"] = fine_exp(p.bitcast(I32)[:, 0:W], s[:, 0:W], p[:, 0:W], item["p_ready"])

            def total(item, i):
                W, s, p, small = item["W"], item["s"], item["p"], item["small"]
                if item["kind"] == "fine":
                    item["p_ready"] = b["s"].free[item["s_slot"]] = dve.do(lambda e: e.tensor_tensor_reduce(
                        p[:, 0:W], p[:, 0:W], s[:, 0:W], 1.0, 0.0, ALU.mult, ALU.add, small[:, 1:2]),
                        item["p_ready"])
                item["scale_out"] = small[:, 2:3]
                item["scale_ready"] = dve.do(lambda e: e.reciprocal(small[:, 2:3], small[:, 1:2]), item["p_ready"])

            return [(4, values or values_stage(b)), (3, turn_stage(b)), (2, fine), (1, soft), (2, total), FILL, (0, scores)]

        scope = ExitStack()
        qkT = sbuf("qkT", [P, 32, TOK], F32, scope)
        v1 = sbuf("v1", [P, TT, D], F32, scope)
        y1 = sbuf("y1", [P, TT, D], F32, scope)
        rel = sbuf("rel", [P, NH, TOK], F32, scope)
        lams = sbuf("lams", [P, 4, HD], F32, scope)
        b1 = softmax_buffers(scope, "a1_", 2 * TOK)
        Q_SCALE = HD ** -0.5

        ext = nc.dram_tensor("rel_ext", (NH, 384), F32, kind="Internal").ap()
        ext_sb = v1[0:NH, 1, 0:384]
        table_in = load(others_in, ext_sb[:, 127:319], dram["rel_rev"], "rel_table_landed")
        far = dve.do(lambda e: e.tensor_copy(ext_sb[:, 0:127], ext_sb[:, 127:128].to_broadcast([NH, 127])), table_in)
        near = dve.do(lambda e: e.tensor_copy(ext_sb[:, 319:384], ext_sb[:, 318:319].to_broadcast([NH, 65])))
        ext_done = load(others_in, ext, ext_sb, "rel_ext_landed", near)
        hankel_src = bass.AP(tensor=ext.tensor, offset=0, ap=[[1, P], [384, NH], [1, TOK]])
        hankel = v1[:, 0, :].rearrange("p (h k) -> p h k", h=NH)
        hankel_in = load(others_in, hankel, hankel_src, "hankel_landed", ext_done)
        lams_in = load(others_in, lams[:, :, :], bass.AP(tensor=dram["lambdas"].tensor, offset=0,
                                                         ap=[[0, P], [HD, 4], [1, HD]]), "lams_landed")

        h_ready = rms_scaled(x, y1, D, x_in, None, 0)
        h_in = turn_and_split(y1, DK, "attn", xT_hi, xT_lo, h_ready, None)

        dots = [dve.do(lambda e, j=j: e.tensor_tensor_reduce(lams[:, 2 * j, :], lams[:, 2 * j, :], lams[:, 2 * j + 1, :],
                                                             1.0, 0.0, ALU.mult, ALU.add, stats[:, 8 + j:9 + j]),
                       lams_in) for j in range(2)]
        lam_x, lam_n = stats[:, 8:10], stats[:, 12:14]
        m = dve.do(lambda e: e.tensor_scalar(lam_n.bitcast(I32), lam_x, 4.0, -0.5, ALU.mult, ALU.add), dots)
        m = dve.do(lambda e: e.scalar_tensor_tensor(lam_x, lam_x, 4.0, lam_n.bitcast(I32), ALU.mult, ALU.subtract), m)
        lam_e = fine_exp(lam_n.bitcast(I32), lam_x, lam_n, [m, consts_in])
        m = dve.do(lambda e: e.tensor_tensor(lam_x, lam_x, lam_n, ALU.mult), lam_e)
        lam_d = dve.do(lambda e: e.tensor_tensor(stats[:, 10:11], stats[:, 9:10], stats[:, 8:9], ALU.subtract), m)
        neg_lam = stats[:, 11:12]
        neg_lam_ready = dve.do(lambda e: e.tensor_scalar(neg_lam, stats[:, 10:11], -0.2, None, ALU.add), lam_d)

        rel_ready = []
        for h in range(NH):
            n, bank = work_banks.take()
            mark = pe.do(lambda e, h=h, bank=bank: e.matmul(bank[:, 0:TOK], const("flip"), hankel[:, h, :],
                                                            start=True, stop=True),
                         hankel_in, consts_in, work_banks.free[n])
            done = dve.do(lambda e, h=h, bank=bank: e.scalar_tensor_tensor(
                rel[:, h, :], bank[:, 0:TOK], 4.0, const("mask"), ALU.mult, ALU.add), mark)
            work_banks.free[n] = done
            rel_ready.append(done)
        hankel_read = mark

        qk_ready = {}

        def evict_qk(g, bank, mark):
            tile0 = 2 * g
            scale = 1.0
            if tile0 < 8 or 24 <= tile0 < 28:
                scale = 4 * Q_SCALE
            elif 16 <= tile0 < 20:
                scale = Q_SCALE
            done = act.do(lambda e: e.activation(qkT[:, tile0:tile0 + 2, :],
                                                 bank[:, :].rearrange("p (c t) -> p c t", c=2), ACT.Copy,
                                                 scale=scale), mark)
            qk_ready[tile0] = qk_ready[tile0 + 1] = done
            return done

        v_ready = {}

        def evict_v(c, t, bank, mark):
            done = act.do(lambda e: e.activation(v1[:, t, c * 512:(c + 1) * 512], bank[:, :], ACT.Copy),
                          mark, hankel_read)
            v_ready[c, t] = done
            return done

        qkv = Filler(*(
            turned(name, parts, DK, xT_hi, xT_lo, h_in, evict_qk) if name == "w_qk" else
            straight(name, parts, DK, xT_hi, xT_lo, h_in, evict_v) for name, parts in QKV_ORDER))

        ss1 = stats[:, 16:64]

        def head_ss(branch, t, h):
            col = 16 * branch + 8 * t + h
            return ss1[:, col:col + 1]

        act.program.append(lambda e: e.preload_act_table_set(EXPS))

        def token_tile(t):
            return (P, P) if t == 0 else (TOK, 0)

        scaled_dist = sbuf("scaled_dist", [P, 2, TOK], F32, scope)
        dists = Slots([scaled_dist[:, j, :] for j in range(2)])
        dists.ready = [None, None]

        def diff_scores(item, i):
            t, h, W = item["t"], item["h"], item["W"]
            item["banks"] = []
            n_dist, dist = dists.of(h)
            if t == 0:
                dists.ready[n_dist] = act.do(
                    lambda e: e.activation(dist, const("dist"), ACT.Copy, scale=4 * 2.0 ** -(h + 1)),
                    consts_in, dists.free[n_dist])
            qkv.until(lambda: h in qk_ready and 8 + h in qk_ready)
            for c in range(2):
                n, bank = work_banks.take()
                rows = slice(c * 64, (c + 1) * 64)
                mark = pe.do(lambda e, rows=rows, bank=bank: e.matmul(
                    bank[:, 0:W], qkT[rows, h, t * P:(t + 1) * P], qkT[rows, 8 + h, 0:W], start=True, stop=True),
                    qk_ready[h], qk_ready[8 + h], work_banks.free[n])
                item["banks"].append((n, bank, mark))

        def diff_soft(item, i):
            h, W, m0 = item["h"], item["W"], item["m0"]
            slot, s = b1["s"].of(i)
            p_slot, p = b1["p"].of(i)
            m_slot, small = b1["small"].of(i)
            n_dist, dist = dists.of(h)
            maxima = []
            for c, (n, bank, mark) in enumerate(item["banks"]):
                a = dve.do(lambda e, c=c, bank=bank: e.tensor_tensor_reduce(
                    s[:, c * W:(c + 1) * W], bank[:, 0:W], dist[:, m0:m0 + W], 1.0, TAKEN,
                    ALU.add, ALU.max, small[:, c:c + 1]),
                    mark, dists.ready[n_dist], b1["s"].free[slot], b1["small"].free[m_slot])
                work_banks.free[n] = a
                maxima.append(a)
            dists.free[n_dist] = a
            quarters = p.bitcast(I32)
            rests = []
            for c in range(2):
                part = slice(c * W, (c + 1) * W)
                q = dve.do(lambda e, part=part, c=c: e.tensor_scalar(quarters[:, part], s[:, part], small[:, c:c + 1],
                                                                     -0.5, ALU.subtract, ALU.add),
                           maxima[c], b1["p"].free[p_slot])
                rests.append(dve.do(lambda e, part=part, c=c: e.scalar_tensor_tensor(
                    s[:, part], s[:, part], small[:, c:c + 1], quarters[:, part], ALU.subtract, ALU.subtract), q))
            item.update(s=s, s_slot=slot, p=p, p_slot=p_slot, small=small, small_slot=m_slot, rests=rests)

        def diff_exp(item, i):
            W, s, p = item["W"], item["s"], item["p"]
            item["exps"] = fine_exp(p.bitcast(I32)[:, 0:2 * W], s[:, 0:2 * W], p[:, 0:2 * W], item["rests"])

        def diff_combine(item, i):
            W, s, p, small = item["W"], item["s"], item["p"], item["small"]
            exps = [dve.do(lambda e, part=slice(c * W, (c + 1) * W), c=c: e.tensor_tensor_reduce(
                p[:, part], p[:, part], s[:, part], 1.0, 0.0, ALU.mult, ALU.add, small[:, 2 + c:3 + c]), item["exps"])
                for c in range(2)]
            b1["s"].free[item["s_slot"]] = exps[-1]
            r = dve.do(lambda e: e.reciprocal(small[:, 4:6], small[:, 2:4]), exps)
            ratio = dve.do(lambda e: e.scalar_tensor_tensor(small[:, 6:7], small[:, 5:6], neg_lam, small[:, 2:3],
                                                            ALU.mult, ALU.mult), r, neg_lam_ready)
            item["p_ready"] = dve.do(lambda e: e.scalar_tensor_tensor(
                p[:, 0:W], p[:, W:2 * W], small[:, 6:7], p[:, 0:W], ALU.mult, ALU.add), ratio)
            item["scale_out"], item["scale_ready"] = small[:, 4:5], r

        def diff_v_ready(h):
            qkv.until(lambda: (h // 4, 1) in v_ready)
            return [v_ready[h // 4, k] for k in range(TT)]

        diff_items = []
        for h in range(NH):
            for t in range(TT):
                W, m0 = token_tile(t)
                diff_items.append(dict(
                    t=t, h=h, W=W, m0=m0, width=2 * HD, out=y1[:, t, h * P:(h + 1) * P],
                    ss=head_ss(0, t, h), v=lambda k, h=h: v1[:, k, h * P:(h + 1) * P],
                    v_ready=lambda h=h: diff_v_ready(h), out_free=h_in))
        qkv.until(lambda: (0, 1) in v_ready)
        pipeline(diff_items, [(4, values_stage(b1)), (3, turn_stage(b1)), (2, diff_exp), (1, diff_soft), (2, diff_combine), FILL,
                              (0, diff_scores)], qkv, 2)

        def head_norm(branches, ready):
            cols = slice(16 * branches[0], 16 * branches[-1] + 16)
            dims = {0: (2 * HD, 1e-5), 1: (HD, 1e-6), 2: (HD, 1e-6)}
            parts = [(ss1[:, 16 * b:16 * b + 16], *dims[b]) for b in branches]
            a = inverse_rms(parts, ss1[:, cols], 16 * len(branches), ready)
            if 0 in branches:
                a = dve.do(lambda e: e.tensor_scalar(ss1[:, 0:16], ss1[:, 0:16], 0.8, None, ALU.mult), a)
            marks = []
            for b in branches:
                c0, w = (0, 2 * HD) if b == 0 else (1024 + 512 * (b - 1), HD)
                for t in range(TT):
                    view = y1[:, t, c0:c0 + 8 * w].rearrange("p (h c) -> p h c", c=w)
                    scale = ss1[:, 16 * b + 8 * t:16 * b + 8 * t + 8].unsqueeze(2).to_broadcast([P, 8, w])
                    marks.append(dve.do(lambda e, view=view, scale=scale: e.tensor_tensor(view, view, scale,
                                                                                          ALU.mult), a))
            return marks

        early_diff = head_norm([0], diff_items[-1]["done"])

        SBW = 384
        half_tanh = qkT[:, 0:12, :].rearrange("p a t -> p (a t)")
        diff_read = diff_items[-1]["banks"][1][2]
        sb_items = [dict(h=h, tile=h // 2, rows=slice(64 * (h % 2), 64 * (h % 2) + 64), c0=1024 + h * HD)
                    for h in range(NH)]

        def sb_scores(item, i):
            tile, rows = item["tile"], item["rows"]
            n, bank = work_banks.take()

            def issue(e):
                e.matmul(bank[:, 0:TOK], qkT[rows, 20 + tile, 0:P], qkT[rows, 16 + tile, :], start=True, stop=True)
                return e.matmul(bank[:, TOK:SBW], qkT[rows, 20 + tile, P:TOK], qkT[rows, 16 + tile, P:TOK],
                                start=True, stop=True)

            qkv.until(lambda: 20 + tile in qk_ready and 16 + tile in qk_ready)
            item["z"] = (n, bank, pe.do(issue, qk_ready[20 + tile], qk_ready[16 + tile], work_banks.free[n]))

        def sb_tanh(item, i):
            n, z, mark = item["z"]
            item["tanh"] = half_tanh[:, i * SBW:(i + 1) * SBW]
            item["tanh_ready"] = act.do(lambda e: e.activation(item["tanh"], z[:, 0:SBW], ACT.Tanh, scale=0.5),
                                        mark, diff_read)
            work_banks.free[n] = item["tanh_ready"]

        pipeline(sb_items, [(1, sb_tanh), FILL, (0, sb_scores)], qkv, .5)
        act.program.append(lambda e: e.preload_act_table_set(EXPS))

        def sb_softplus(item, i):
            n, z, mark = item["z"]
            slot, l = b1["s"].of(i)
            p_slot, d = b1["p"].of(i)
            l, d = l[:, 0:SBW], d[:, 0:SBW]
            th = item["tanh"]
            a = act.do(lambda e: e.activation(l, th, ACT.Abs), item["tanh_ready"], b1["s"].free[slot])
            a = act.do(lambda e: e.activation(l, l, ACT.Ln, bias=const("half"), scale=0.5), a)
            a = dve.do(lambda e: e.scalar_tensor_tensor(l, z[:, 0:SBW], 0.0, l, ALU.max, ALU.subtract), a, mark)
            item["d_ready"] = dve.do(lambda e: e.tensor_tensor(d, z[:, 0:SBW], l, ALU.subtract),
                                     a, b1["p"].free[p_slot])
            work_banks.free[n] = item["d_ready"]
            diagonal = l.rearrange("p (b q) -> p b q", b=3)[:, 0:3:2, :]
            item["l_ready"] = dve.do(lambda e: e.tensor_tensor(
                diagonal, diagonal, const("causal").unsqueeze(1).to_broadcast([P, 2, P]), ALU.mult),
                item["d_ready"])
            item["l"], item["d"], item["slot"], item["p_slot"] = l, d, slot, p_slot

        def sb_suffix(item, i):
            l, d = item["l"], item["d"]
            n, bank = work_banks.take()

            def issue(e):
                e.matmul(bank[:, 0:TOK], const("after"), l[:, 0:TOK], start=True, stop=True, skip_group_check=True)
                e.matmul(bank[:, P:TOK], const("ones"), l[:, TOK:SBW], start=False, stop=True,
                         skip_group_check=True)
                return e.matmul(bank[:, TOK:SBW], const("after"), l[:, TOK:SBW], start=False, stop=True,
                                skip_group_check=True)

            mark = pe.do(issue, item["l_ready"], work_banks.free[n])
            a = dve.do(lambda e: e.tensor_tensor(d, d, bank[:, 0:SBW], ALU.subtract), mark, item["d_ready"])
            work_banks.free[n] = a
            quarters = l.bitcast(I32)
            a = dve.do(lambda e: e.tensor_scalar(quarters, d, 4.0, -0.5, ALU.mult, ALU.add), a)
            a = dve.do(lambda e: e.scalar_tensor_tensor(d, d, 4.0, quarters, ALU.mult, ALU.subtract), a)
            a = fine_exp(quarters, d, l, a)
            a = dve.do(lambda e: e.tensor_tensor(d, d, l, ALU.mult), a)
            b1["s"].free[item["slot"]] = a
            diagonal = d.rearrange("p (b q) -> p b q", b=3)[:, 0:3:2, :]
            item["a_ready"] = dve.do(lambda e: e.tensor_tensor(
                diagonal, diagonal, const("causal").unsqueeze(1).to_broadcast([P, 2, P]), ALU.mult), a)

        def sb_values(item, i):
            d, c0 = item["d"], item["c0"]
            n, bank = work_banks.take()

            def issue(e):
                e.matmul(bank[:, 0:HD], d[:, 0:P], v1[:, 0, c0:c0 + HD], start=True, stop=True)
                e.matmul(bank[:, HD:2 * HD], d[:, P:TOK], v1[:, 0, c0:c0 + HD], start=True, stop=False)
                return e.matmul(bank[:, HD:2 * HD], d[:, TOK:SBW], v1[:, 1, c0:c0 + HD], start=False, stop=True)

            mark = pe.do(issue, item["a_ready"], [v_ready[2, k] for k in range(TT)], work_banks.free[n])
            slot, junk = b1["pT"].of(i)
            done = act.do(lambda e: e.activation(y1[:, :, c0:c0 + HD],
                                                 bank[:, 0:2 * HD].rearrange("p (t c) -> p t c", t=2), ACT.Copy), mark)
            for t in range(TT):
                ss = head_ss(1, t, item["h"])
                done = act.do(lambda e, t=t, ss=ss: e.activation(
                    junk[:, 0:HD], bank[:, t * HD:(t + 1) * HD], ACT.Square, accum_out=ss),
                    b1["pT"].free[slot], done)
            b1["pT"].free[slot] = done
            b1["p"].free[item["p_slot"]] = mark
            work_banks.free[n] = done
            item["done"] = done

        pipeline(sb_items, [(3, sb_values), (2, sb_suffix), (1, sb_softplus), FILL, (0, sb_scores)], qkv, 2.4)
        qkv.finish()
        xT_read = stream.used[stream.at - 1]

        y_in = turn_and_split(y1, 8, "y1", xT_hi, xT_lo, early_diff, xT_read)
        early_sb = head_norm([1], sb_items[-1]["done"])
        y_in = y_in + turn_and_split(y1, 4, "y1", xT_hi, xT_lo, early_sb, xT_read, 8)[8:]
        x_ready = []
        out_early = Filler(straight("w_o", range(4), 12, xT_hi, xT_lo, y_in, add_to_x(x_ready)))
        act.program.append(lambda e: e.preload_act_table_set(EXPS))

        band_items = []
        for h in range(NH):
            for t in range(TT):
                W, m0 = token_tile(t)
                tile, rows = h // 2, slice(64 * (h % 2), 64 * (h % 2) + 64)
                c0 = 1536 + h * HD
                band_items.append(dict(
                    W=W, width=HD, kind="fine", mask=rel[:, h, m0:m0 + W], mask_ready=rel_ready[h],
                    scores=lambda e, bank, t=t, W=W, tile=tile, rows=rows: e.matmul(
                        bank[:, 0:W], qkT[rows, 24 + tile, t * P:(t + 1) * P], qkT[rows, 28 + tile, 0:W],
                        start=True, stop=True),
                    ready=lambda tile=tile: [qk_ready[24 + tile], qk_ready[28 + tile]],
                    v=lambda k, c0=c0: v1[:, k, c0:c0 + HD], v_ready=lambda: [v_ready[3, k] for k in range(TT)],
                    out=y1[:, t, c0:c0 + HD], ss=head_ss(2, t, h)))
        pipeline(band_items, softmax_stages(b1), out_early, 1.3)
        out_early.finish()

        late = head_norm([2], band_items[-1]["done"])
        y_in2 = turn_and_split(y1, 4, "y1", xT_hi, xT_lo, late, xT_read, 12)
        run(straight("w_o", range(4), 4, xT_hi, xT_lo, y_in2, add_to_x(x_ready), k0=12))
        xT_read = stream.used[stream.at - 1]
        scope.close()
        block_free = [y_in, y_in2, late, hankel_read]

        def mlp(phases, gate, up, down, x_ready, gain_name, dst_free, xT_read, scope, tag):
            act_hi = sbuf(f"act_hi{tag}", [P, 2, PHASE, TOK], F32R, scope)
            act_lo = sbuf(f"act_lo{tag}", [P, 2, PHASE, TOK], F32R, scope)
            h_nat = sbuf(f"h_nat{tag}", [P, TT, D], F32, scope)
            conv = sbuf(f"conv{tag}", [P, 2, 2, TOK], F32, scope)
            prod = sbuf(f"prod{tag}", [P, 2, 2, TOK], F32, scope)
            prod_free = [None, None]
            h_done = rms_scaled(x, h_nat, D, x_ready[:], dst_free, 0)
            h_in = turn_and_split(h_nat, DK, gain_name, xT_hi, xT_lo, h_done, xT_read)
            acts_ready = {}
            down_read = {}

            def split_act(pair, src, ready):
                n, a = pair // (PHASE // 2), 2 * pair % PHASE
                hi, lo = act_hi[:, n % 2, a:a + 2, :], act_lo[:, n % 2, a:a + 2, :]
                free = down_read.get(n - 2)
                h = act.do(lambda e: e.activation(hi, src, ACT.Copy), ready, free)
                l = dve.do(lambda e: e.tensor_tensor(lo, src, hi.bitcast(F32), ALU.subtract), h, free)
                acts_ready[n, a] = acts_ready[n, a + 1] = [h, l]
                return [h, l]

            def gate_pair(pair):
                slot = pair % 2
                cv, pr = conv[:, slot], prod[:, slot]
                state = {}

                def evict_gate(g, bank, mark):
                    gates = bank[:, :].rearrange("p (c t) -> p c t", c=2)
                    first = [act.do(lambda e, c=c: e.activation(
                        cv[:, c, :], gates[:, c, :], ACT.Identity, bias=gain("convb", 2 * pair + c),
                        scale=gain("conv2", 2 * pair + c)), mark, prod_free[slot]) for c in range(2)]
                    last = []
                    for shift, tap in ((1, "conv1"), (2, "conv0")):
                        last = [dve.do(lambda e, c=c, shift=shift, tap=tap: e.scalar_tensor_tensor(
                            cv[:, c, shift:TOK], gates[:, c, 0:TOK - shift], gain(tap, 2 * pair + c),
                            cv[:, c, shift:TOK], ALU.mult, ALU.add), first, last) for c in range(2)]
                    th = act.do(lambda e: e.activation(pr, cv, ACT.Tanh, scale=0.5), last, prod_free[slot])
                    state["silu2"] = dve.do(lambda e: e.scalar_tensor_tensor(pr, pr, 1.0, cv, ALU.add, ALU.mult), th)
                    return last[-1]

                def evict_up(g, bank, mark):
                    ups = bank[:, :].rearrange("p (c t) -> p c t", c=2)
                    m = dve.do(lambda e: e.scalar_tensor_tensor(pr, pr, 0.5, ups, ALU.mult, ALU.mult),
                               state["silu2"], mark)
                    prod_free[slot] = split_act(pair, pr, m)
                    return m

                run(turned(gate, [pair], DK, xT_hi, xT_lo, h_in, evict_gate))
                run(turned(up, [pair], DK, xT_hi, xT_lo, h_in, evict_up))

            def square_pair(pair):
                slot = pair % 2
                cv, pr = conv[:, slot], prod[:, slot]

                def evict(g, bank, mark):
                    r = act.do(lambda e: e.activation(cv, bank[:, :].rearrange("p (c t) -> p c t", c=2), ACT.Relu),
                               mark, prod_free[slot])
                    m = dve.do(lambda e: e.tensor_tensor(pr, cv, cv, ALU.mult), r, prod_free[slot])
                    prod_free[slot] = split_act(pair, pr, m)
                    return r

                run(turned(up, [pair], DK, xT_hi, xT_lo, h_in, evict))

            def down_phase(n):
                a, b = phases[n]
                ready = [acts_ready[n, k] for k in range(b - a)]
                run(straight(down, range(4), b - a, act_hi[:, n % 2], act_lo[:, n % 2], ready, add_to_x(x_ready),
                             k0=a, in0=0))
                down_read[n] = stream.used[stream.at - 1]

            for n, (a, b) in enumerate(phases):
                for pair in range(a // 2, b // 2):
                    (gate_pair if gate else square_pair)(pair)
                if n:
                    down_phase(n - 1)
            down_phase(len(phases) - 1)
            return [h_in, x_ready, down_read[len(phases) - 1], prod_free]

        scope = ExitStack()
        block_free = mlp(phases1, "w_gate", "w_up1", "w_down1", x_ready, "ffn", block_free, xT_read, scope, "1")
        xT_read = stream.used[stream.at - 1]
        scope.close()

        scope = ExitStack()
        mixed = sbuf("mixed", [P, TT, MIX], F32, scope)
        q_idxT = sbuf("q_idxT", [P, 8, TOK], F32, scope)
        k_idxT = sbuf("k_idxT", [P, TOK], F32, scope)
        q_dT = sbuf("q_dT", [P, 8, TOK], F32, scope)
        k_dT = q_idxT
        tail = sbuf("tail", [P, TT, TAIL], F32, scope)
        c_q = sbuf("c_q", [P, TT, 512], F32, scope)
        staging = sbuf("staging", [P, TT, 1024], F32, scope)
        q_nT = sbuf("q_nT", [P, 8, TOK], F32, scope)
        k_nT = sbuf("k_nT", [P, 8, TOK], F32, scope)
        v_m = sbuf("v_m", [P, TT, 1024], F32, scope)
        q_rT = sbuf("q_rT", [P, 4, TOK], F32, scope)
        k_dup = sbuf("k_dup", [P, TT, P], F32, scope)
        cos = sbuf("cos", [P, TT, 32], F32, scope)
        sin = sbuf("sin", [P, TT, 32], F32, scope)
        angle = sbuf("angle", [P, TT, 32], F32, scope)
        rope_tmp = [sbuf(f"rope_tmp{i}", [P, TOK], F32, scope) for i in range(3)]
        pos = sbuf("pos", [P, TT], I32, scope)
        posf = sbuf("posf", [P, TT], F32, scope)
        index = sbuf("index", [P, 384], F32, scope)
        top8 = sbuf("top8", [P, TT, 8], F32, scope)
        krT = sbuf("krT", [P, TOK], F32, scope)
        b2 = softmax_buffers(scope, "a2_", TOK)
        low_rank = ExitStack()
        cT_hi = sbuf("cT_hi", [P, 6, TOK], F32R, low_rank)
        cT_lo = sbuf("cT_lo", [P, 6, TOK], F32R, low_rank)
        low_rank.close()
        v_d = sbuf("v_d", [P, TT, 1024], F32, scope)

        pos_in = load(others_in, pos[:, :], dram["positions"], "pos_landed", block_free)

        TWO_PI = (6.28125, 1.9350051879882812e-03, 3.0198694e-07)
        ROUND = 12582912.0
        a = dve.do(lambda e: e.tensor_copy(posf[:, :], pos[:, :]), pos_in, block_free)
        ang_ready = [dve.do(lambda e, t=t: e.tensor_scalar(angle[:, t, :], const("freq"), posf[:, t:t + 1], None,
                                                           ALU.mult), a) for t in range(TT)]
        trig_ready = []
        for dst, quarter in ((sin, 0.0), (cos, 0.25)):
            turns = rope_tmp[0][:, 0:64].rearrange("p (t f) -> p t f", t=TT)
            m = dve.do(lambda e, quarter=quarter: e.tensor_scalar(turns, angle[:, :, :], 0.15915494309189535, quarter,
                                                                  ALU.mult, ALU.add), ang_ready, trig_ready)
            m = dve.do(lambda e: e.tensor_scalar(turns, turns, ROUND, None, ALU.add), m)
            m = dve.do(lambda e: e.tensor_scalar(turns, turns, -ROUND, None, ALU.add), m)
            src = angle[:, :, :]
            for part in TWO_PI:
                m = dve.do(lambda e, src=src, part=part, dst=dst: e.scalar_tensor_tensor(
                    dst[:, :, :], turns, -part, src, ALU.mult, ALU.add), m)
                src = dst[:, :, :]
            if quarter:
                m = dve.do(lambda e: e.tensor_scalar(dst[:, :, :], dst[:, :, :], 1.5707963267948966, None, ALU.add), m)
            m = dve.do(lambda e, dst=dst: e.tensor_scalar(dst[:, :, :], dst[:, :, :], 3.1415925, -3.1415925,
                                                          ALU.min, ALU.max), m)
            trig_ready.append(act.do(lambda e, dst=dst: e.activation(dst[:, :, :], dst[:, :, :], ACT.Sin), m))

        def rope(view, heads, half, ready):
            step = 32 // half
            shape = [P, heads, half]
            ends = []
            t1, t2, t3 = (r[:, 0:heads * half].rearrange("p (h f) -> p h f", h=heads) for r in rope_tmp)
            for t in range(TT):
                x1, x2 = view[:, t, :, 0:half], view[:, t, :, half:2 * half]
                co = cos[:, t, 0:32:step].unsqueeze(1).to_broadcast(shape)
                si = sin[:, t, 0:32:step].unsqueeze(1).to_broadcast(shape)
                before = [rope.done, trig_ready, ready]
                a = dve.do(lambda e, x1=x1, co=co: e.tensor_tensor(t1, x1, co, ALU.mult), before)
                b = dve.do(lambda e, x2=x2, si=si: e.tensor_tensor(t2, x2, si, ALU.mult))
                c = dve.do(lambda e, x1=x1, si=si: e.tensor_tensor(t3, x1, si, ALU.mult))
                d = dve.do(lambda e, x2=x2, co=co: e.tensor_tensor(x2, x2, co, ALU.mult), b)
                a = dve.do(lambda e, x1=x1: e.tensor_tensor(x1, t1, t2, ALU.subtract), c)
                rope.done = dve.do(lambda e, x2=x2: e.tensor_tensor(x2, x2, t3, ALU.add), d)
                ends += [a, rope.done]
            return ends

        rope.done = trig_ready

        def turn_tiles(src, tiles, dst, ready, scale=1.0, free=None):
            marks = {}
            for pair in range((tiles + 1) // 2):
                n, bank = work_banks.take()
                here = range(2 * pair, min(2 * pair + 2, tiles))

                def issue(e, bank=bank, here=here):
                    for j, tile in enumerate(here):
                        for t in range(TT):
                            last = e.transpose(bank[:, j * TOK + t * P:j * TOK + (t + 1) * P],
                                               src[:, t, tile * P:(tile + 1) * P], const("ident"))
                    return last

                mark = pe.do(issue, ready, work_banks.free[n])
                w = len(here)
                done = act.do(lambda e, bank=bank, here=here, w=w: e.activation(
                    dst[:, here[0]:here[0] + w, :], bank[:, 0:w * TOK].rearrange("p (c t) -> p c t", c=w),
                    ACT.Copy, scale=scale), mark, free)
                work_banks.free[n] = done
                for tile in here:
                    marks[tile] = done
            turn_tiles.read = mark
            return marks

        g_end = staging[:, :, :].rearrange("p t c -> p (t c)")
        g_end_in = load(others_in, g_end, bass.AP(tensor=dram["final_gain_1"].tensor, offset=0, ap=[[0, P], [1, D]]),
                        "final_gain_1_landed", block_free)
        normed = rms_scaled(x, mixed, D, x_ready[:], block_free, 0)
        x_ready = [dve.do(lambda e, t=t: e.tensor_tensor(x[:, t, :], mixed[:, t, :], g_end, ALU.mult),
                          normed, g_end_in) for t in range(TT)]
        g_end_read = x_ready[:]
        h_done = rms_scaled(x, mixed, D, x_ready[:], x_ready[:], 0)
        h_in = turn_and_split(mixed, DK, "mix", xT_hi, xT_lo, h_done, xT_read)

        def copy_out(dst, marks, free=None):
            def evict(c, t, bank, mark):
                view = dst(c, t)
                done = act.do(lambda e: e.activation(view, bank[:, 0:view.shape[1]], ACT.Copy), mark, free)
                marks.append(done)
                return done
            return evict

        tail_done = []
        run(straight("w_tail", [0], DK, xT_hi, xT_lo, h_in,
                     copy_out(lambda c, t: tail[:, t, :], tail_done, block_free), width=TAIL))
        k_r, k_i, w_i = (tail[:, :, a:b] for a, b in ((256, 320), (320, 384), (384, 400)))

        def rope_key(src, half, dst, free):
            done = rope(src.unsqueeze(2), 1, half, tail_done)
            cp = [dve.do(lambda e, j=j: e.tensor_copy(k_dup[:, :, j * 64:(j + 1) * 64], src), done, free)
                  for j in range(2)]
            marks = turn_tiles(k_dup, 1, dst[:, :].unsqueeze(1), cp)
            return marks[0], turn_tiles.read

        k_idx_ready, k_dup_read = rope_key(k_i, 8, k_idxT, None)
        kr_ready, _ = rope_key(k_r, 32, krT, k_dup_read)
        w_idx_ready = dve.do(lambda e: e.tensor_scalar(w_i, w_i, IDX_HEADS ** -0.5, None, ALU.mult), tail_done)

        def project(c0, buf, marks, free):
            return straight("w_in", [c0, c0 + 1], DK, xT_hi, xT_lo, h_in,
                            copy_out(lambda c, t: buf[:, t, (c - c0) * 512:(c - c0 + 1) * 512], marks, free))

        m_cq, m_qi = [], []
        run(straight("w_in", [8], DK, xT_hi, xT_lo, h_in, copy_out(lambda c, t: c_q[:, t, :], m_cq, block_free)))
        low_q = q_nT[:, 0:4, :].rearrange("p (t a) c -> p t (a c)", t=TT)
        low_kv = k_nT[:, 0:2, :]
        n_cq = rms_scaled(c_q, low_q, 512, m_cq, block_free, 2)
        cq_in = turn_and_split(low_q, 4, "cq", cT_hi, cT_lo, n_cq, block_free)
        c_kv = tail[:, :, 0:256]
        n_ckv = rms_scaled(c_kv, low_kv, 256, tail_done, block_free, 4)
        ckv_in = turn_and_split(low_kv, 2, "ckv", cT_hi, cT_lo, n_ckv, block_free, 4, 0)

        run(project(0, staging, m_qi, [block_free, g_end_read]))
        r = rope(staging[:, :, :].rearrange("p t (h d) -> p t h d", d=64), IDX_HEADS, 8, m_qi)
        q_idx_ready = turn_tiles(staging, 8, q_idxT, r)
        staging_free = turn_tiles.read

        index_of = (index[:, 0:P], index[:, P:384])
        relus = Slots([rope_tmp[i][:, 0:TOK] for i in range(3)])
        index_ready = []
        for t in range(TT):
            W, m0 = token_tile(t)
            index_ready.append(dve.do(lambda e, t=t, m0=m0, W=W: e.tensor_copy(index_of[t], const("mask")[:, m0:m0 + W]),
                                      block_free))
        mask_marks = index_ready
        index_ready = [None, None]
        idx_items = [dict(h=h, t=t) for h in range(IDX_HEADS) for t in range(TT)]
        relus.free = [rope.done] * 3

        def idx_scores(item, i):
            h, t = item["h"], item["t"]
            W, _ = token_tile(t)
            rows = slice(64 * (h % 2), 64 * (h % 2) + 64)
            n, bank = work_banks.take()
            mark = pe.do(lambda e: e.matmul(bank[:, 0:W], q_idxT[rows, h // 2, t * P:(t + 1) * P], k_idxT[rows, 0:W],
                                            start=True, stop=True),
                         q_idx_ready[h // 2], k_idx_ready, work_banks.free[n])
            slot, r = relus.of(i)
            relu = act.do(lambda e: e.activation(r[:, 0:W], bank[:, 0:W], ACT.Relu, scale=64 ** -0.5),
                          mark, relus.free[slot])
            work_banks.free[n] = relu
            item["r"], item["relu"], item["slot"], item["mark"] = r, relu, slot, mark

        def idx_add(item, i):
            h, t, r = item["h"], item["t"], item["r"]
            W, _ = token_tile(t)
            w = tail[:, t, 384 + h:385 + h]
            if h == 0:
                a = dve.do(lambda e: e.tensor_scalar(index_of[t], r[:, 0:W], w, None, ALU.mult),
                           item["relu"], w_idx_ready, mask_marks)
            else:
                a = dve.do(lambda e: e.scalar_tensor_tensor(index_of[t], r[:, 0:W], w, index_of[t],
                                                            ALU.mult, ALU.add), item["relu"], index_ready[t])
            index_ready[t] = a
            relus.free[item["slot"]] = item["added"] = a

        q_ready2, k_ready2 = {}, {}

        def evict_tiles(dst, marks, free, scale=1.0):
            def evict(g, bank, mark):
                done = act.do(lambda e: e.activation(dst[:, 2 * g:2 * g + 2, :],
                                                     bank[:, :].rearrange("p (c t) -> p c t", c=2), ACT.Copy,
                                                     scale=scale), mark, free)
                marks[2 * g] = marks[2 * g + 1] = done
                return done
            return evict

        m_qr, m_vm = [], []
        q_rope = c_q
        ckv_hi, ckv_lo = cT_hi[:, 4:6, :], cT_lo[:, 4:6, :]
        expand = Filler(
            turned("w_qnope", range(4), 4, cT_hi, cT_lo, cq_in, evict_tiles(q_nT, q_ready2, cq_in, -192 ** -0.5)),
            straight("w_qrope", [0], 4, cT_hi, cT_lo, cq_in, copy_out(lambda c, t: q_rope[:, t, :], m_qr, n_cq)),
            turned("w_knope", range(4), 2, ckv_hi, ckv_lo, ckv_in[4:6], evict_tiles(k_nT, k_ready2, ckv_in)),
            straight("w_vmla", range(2), 2, ckv_hi, ckv_lo, ckv_in[4:6],
                     copy_out(lambda c, t: v_m[:, t, c * 512:(c + 1) * 512], m_vm, block_free)))
        pipeline(idx_items, [(1, idx_add), FILL, (0, idx_scores)], expand, 0.4)
        expand.finish()
        expanded = stream.used[stream.at - 1]
        r = rope(q_rope[:, :, :].rearrange("p t (h d) -> p t h d", d=64), 8, 32, [m_qr, idx_items[-1]["added"]])
        q_r_ready = turn_tiles(q_rope, 4, q_rT, r, -192 ** -0.5, block_free)

        for t in range(TT):
            W, m0 = token_tile(t)
            index_ready[t] = dve.do(lambda e, t=t, m0=m0, W=W: e.tensor_tensor(
                index_of[t], index_of[t], const("mask")[:, m0:m0 + W], ALU.add), index_ready[t])

        def select_round():
            best = [dve.do(lambda e, t=t: e.max(top8[:, t, :], index_of[t]), index_ready[t]) for t in range(TT)]
            for t in range(TT):
                index_ready[t] = dve.do(lambda e, t=t: e.match_replace(index_of[t], top8[:, t, :], index_of[t],
                                                                       TAKEN), best[t])

        m_qd, m_kd, m_vd = [], [], []
        rest = Filler(project(2, staging, m_qd, staging_free))
        for _ in range(TOPK // 8):
            select_round()
            rest.advance(2)
        rest.finish()
        select_ready = [dve.do(lambda e, t=t: e.tensor_scalar(index_of[t], index_of[t], TAKEN / 2, -NEG,
                                                              ALU.is_ge, ALU.mult), index_ready[t])
                        for t in range(TT)]
        r = rope(staging[:, :, :].rearrange("p t (h d) -> p t h d", d=P), 8, 16, m_qd)
        q_d_ready = turn_tiles(staging, 8, q_dT, r, -P ** -0.5)
        act.program.append(lambda e: e.preload_act_table_set(EXPS))

        rest = Filler(project(4, staging, m_kd, turn_tiles.read), project(6, v_d, m_vd, [block_free, expanded]))
        mla_items = []
        for h in range(NH):
            for t in range(TT):
                W, m0 = token_tile(t)
                rows = slice(64 * (h % 2), 64 * (h % 2) + 64)

                def scores(e, bank, t=t, W=W, h=h, rows=rows):
                    e.matmul(bank[:, 0:W], q_nT[:, h, t * P:(t + 1) * P], k_nT[:, h, 0:W], start=True, stop=False)
                    return e.matmul(bank[:, 0:W], q_rT[rows, h // 2, t * P:(t + 1) * P], krT[rows, 0:W],
                                    start=False, stop=True)

                mla_items.append(dict(
                    W=W, width=P, kind="masked", mask=const("blocked")[:, m0:m0 + W], mask_ready=None,
                    scores=scores, ready=lambda h=h: [q_ready2[h], k_ready2[h], q_r_ready[h // 2], kr_ready],
                    v=lambda k, h=h: v_m[:, k, h * P:(h + 1) * P], v_ready=lambda: m_vm,
                    out=mixed[:, t, h * P:(h + 1) * P], out_free=h_in))
        pipeline(mla_items, softmax_stages(b2), rest, 1.7)
        rest.finish()
        r = rope(staging[:, :, :].rearrange("p t (h d) -> p t h d", d=P), 8, 16, m_kd)
        k_d_ready = turn_tiles(staging, 8, k_dT, r, free=idx_items[-1]["mark"])
        xT_read = stream.used[stream.at - 1]
        m_in = turn_and_split(mixed, 8, None, xT_hi, xT_lo, mla_items[-1]["done"], xT_read)
        out_early = Filler(straight("w_out", range(4), 8, xT_hi, xT_lo, m_in, add_to_x(x_ready)))

        dsa_items = []
        for h in range(NH):
            for t in range(TT):
                W, _ = token_tile(t)
                dsa_items.append(dict(
                    W=W, width=P, kind="masked", mask=index_of[t], mask_ready=select_ready[t],
                    scores=lambda e, bank, t=t, W=W, h=h: e.matmul(
                        bank[:, 0:W], q_dT[:, h, t * P:(t + 1) * P], k_dT[:, h, 0:W], start=True, stop=True),
                    ready=lambda h=h: [q_d_ready[h], k_d_ready[h]],
                    v=lambda k, h=h: v_d[:, k, h * P:(h + 1) * P], v_ready=lambda: m_vd,
                    out=mixed[:, t, 1024 + h * P:1024 + (h + 1) * P], out_free=h_in))
        pipeline(dsa_items, softmax_stages(b2), out_early, 0.9)
        out_early.finish()

        m_in2 = turn_and_split(mixed, 8, None, xT_hi, xT_lo, dsa_items[-1]["done"], xT_read, 8)
        run(straight("w_out", range(4), 8, xT_hi, xT_lo, m_in2, add_to_x(x_ready), k0=8))
        xT_read = stream.used[stream.at - 1]
        mixed_ready = [m_in, m_in2]
        block_free = [m_in, m_in2, select_ready, dsa_items[-1]["done"]]
        scope.close()

        scope = ExitStack()
        mT_hi = sbuf("mT_hi", [P, DK, TOK], F32R, scope)
        mT_lo = sbuf("mT_lo", [P, DK, TOK], F32R, scope)
        mem = sbuf("mem", [P, TT, D], F32, scope)
        kxT = sbuf("kxT", [P, 4, TOK], F32, scope)
        qxT = sbuf("qxT", [P, 4, TOK], F32, scope)
        v_x = sbuf("v_x", [P, TT, 512], F32, scope)
        o_x = sbuf("o_x", [P, TT, 512], F32, scope)
        h_x = sbuf("h_x", [P, TT, D], F32, scope)
        b3 = softmax_buffers(scope, "a3_", TOK)
        mem_in = load(others_in, mem[:, :, :], dram["mem"].rearrange("(t p) d -> p t d", p=P), "mem_landed",
                      block_free)
        n_mem = rms_scaled(mem, h_x, D, mem_in, block_free, 2)
        mem_T = turn_and_split(h_x, DK, "mem", mT_hi, mT_lo, n_mem, block_free)
        kx_ready, qx_ready, vx_ready = {}, {}, []
        run(turned("w_kx", range(2), DK, mT_hi, mT_lo, mem_T, evict_tiles(kxT, kx_ready, block_free)))
        h_done = rms_scaled(x, h_x, D, x_ready[:], mem_T, 0)
        h_in = turn_and_split(h_x, DK, "cross", xT_hi, xT_lo, h_done, xT_read)
        run(turned("w_qx", range(2), DK, xT_hi, xT_lo, h_in, evict_tiles(qxT, qx_ready, block_free, P ** -0.5)))
        xT_read = stream.used[stream.at - 1]
        act.program.append(lambda e: e.preload_act_table_set(EXPS))
        values = Filler(straight("w_vx", [0], DK, mT_hi, mT_lo, mem_T,
                                 copy_out(lambda c, t: v_x[:, t, :], vx_ready, block_free)))
        x_items = []
        for h in range(4):
            for t in range(TT):
                x_items.append(dict(
                    W=TOK, width=P, kind="open",
                    scores=lambda e, bank, t=t, h=h: e.matmul(
                        bank[:, 0:TOK], qxT[:, h, t * P:(t + 1) * P], kxT[:, h, :], start=True, stop=True),
                    ready=lambda h=h: [qx_ready[h], kx_ready[h]],
                    v=lambda k, h=h: v_x[:, k, h * P:(h + 1) * P], v_ready=lambda: vx_ready,
                    out=o_x[:, t, h * P:(h + 1) * P], out_free=block_free))
        value_of_head = values_stage(b3)

        def values_late(item, i):
            values.finish()
            value_of_head(item, i)

        pipeline(x_items, softmax_stages(b3, values_late), values, 3)
        mem_read = stream.used[stream.at - 1]
        o_in = turn_and_split(o_x, 4, None, xT_hi, xT_lo, x_items[-1]["done"], xT_read)
        run(straight("w_ox", range(4), 4, xT_hi, xT_lo, o_in, add_to_x(x_ready)))
        xT_read = stream.used[stream.at - 1]
        block_free = [o_in, mem_read, h_in, x_items[-1]["done"]]
        scope.close()

        scope = ExitStack()
        block_free = mlp(phases2, None, "w_up2", "w_down2", x_ready, "mlp", block_free, xT_read, scope, "2")
        scope.close()

        assert stream.at == len(plan)
        scope = ExitStack()
        g_final = sbuf("g_final", [P, D], F32, scope)
        result = sbuf("result", [P, TT, D], F32, scope)
        g_in = load(others_in, g_final[:, :], bass.AP(tensor=dram["final_gain"].tensor, offset=0, ap=[[0, P], [1, D]]),
                    "final_gain_landed", block_free)
        norm = rms_scaled(x, result, D, x_ready[:], block_free, 0)
        stored = ctx.enter_context(nc.semaphore("stored"))
        for t in range(TT):
            done = dve.do(lambda e, t=t: e.tensor_tensor(result[:, t, :], result[:, t, :], g_final[:, :], ALU.mult),
                          norm[t], g_in)
            others_in.wait(done)
            others_in.program.append(lambda e, t=t: e.dma_start(out_dram[t * P:(t + 1) * P, :], result[:, t, :])
                                     .then_inc(stored, 16))
        others_in.wait((stored, 16 * TT))
        scope.close()

        block = ctx.enter_context(nc.Block())

        @block.sync
        def _(e):
            weights_in.run(e)

        @block.gpsimd
        def _(e):
            others_in.run(e)

        @block.scalar
        def _(e):
            act.run(e)

        @block.vector
        def _(e):
            dve.run(e)

        @block.tensor
        def _(e):
            pe.run(e)


def lay_turned(w):
    k, c = w.shape
    per = min(4, k // P)
    return np.ascontiguousarray(w.reshape(k // P // per, per, P, c // TURNED_COLS, TURNED_COLS).transpose(3, 0, 2, 1, 4))


def lay_straight(w, width=STRAIGHT_COLS):
    k, c = w.shape
    return np.ascontiguousarray(w.reshape(k // P // 2, 2, P, c // width, width).transpose(3, 0, 2, 1, 4))


def lay_gain(g):
    return g.reshape(-1, P).T


def constants():
    i = np.arange(P)
    q = P + i[:, None]
    k = np.arange(TOK)[None, :]
    mask = np.where(k // CHUNK <= q // CHUNK, 0.0, NEG)
    parts = {
        "ident": np.eye(P), "flip": np.eye(P)[::-1],
        "after": i[:, None] > i[None, :],
        "causal": i[:, None] < i[None, :],
        "ones": np.ones((P, P)),
        "mask": mask, "blocked": -mask,
        "dist": np.where(mask == 0.0, -np.abs(q - k), NEG),
        "half": np.full((P, 1), 0.5), "eighth": np.full((P, 1), 0.125), "less_eighth": np.full((P, 1), -0.125),
        "freq": np.broadcast_to(np.float32(500000.0) ** (-np.arange(32, dtype=np.float32) / np.float32(32)), (P, 32)),
    }
    return np.ascontiguousarray(np.concatenate([parts[n].astype(np.float32) for n, _ in CONSTS], axis=1))


def kernel(**inputs):
    import concourse.bacc as bacc
    from concourse.bass_utils import run_bass_kernel_spmd

    i = {k: np.asarray(v) for k, v in inputs.items()}
    qkv, w_in = i["w_qkv"][0], i["w_in_2"][0]
    qb = i["w_qb_2"][0].reshape(512, 8, 192)
    kvb = i["w_kvb_2"][0].reshape(256, 8, 256)
    gains = {
        "attn": i["attn_norm"][0], "ffn": i["ffn_norm"][0],
        "y1": np.concatenate([np.tile(i["diff_subln"][0], NH), i["sb_norm"][0].ravel(), i["ch_norm"][0].ravel()]),
        "conv0": i["conv_w"][0, 0], "conv1": i["conv_w"][0, 1], "conv2": i["conv_w"][0, 2], "convb": i["conv_b"][0],
        "mix": i["g_mix_2"][0], "cq": i["g_cq_2"][0], "ckv": i["g_ckv_2"][0], "cross": i["g_cross_2"][0],
        "mem": i["g_mem_2"][0], "mlp": i["g_mlp_2"][0],
    }
    arrays = {
        "x": i["x"][0], "mem": i["mem_2"][0],
        "consts": constants(),
        "gains": np.concatenate([lay_gain(gains[n]) for n, _ in GAINS], axis=1),
        "lambdas": np.concatenate([i["lambda_q1"], i["lambda_k1"], i["lambda_q2"], i["lambda_k2"]]),
        "rel_rev": i["rel_bias"][0][:, ::-1],
        "positions": i["positions_2"][0].reshape(TT, P).T,
        "final_gain_1": i["final_norm"], "final_gain": i["g_final_2"],
        "w_qk": lay_turned(np.concatenate([qkv[:, 0:2048], qkv[:, 3072:4096], qkv[:, 4608:5632]], axis=1)),
        "w_v": lay_straight(np.concatenate([qkv[:, 2048:3072], qkv[:, 4096:4608], qkv[:, 5632:6144]], axis=1)),
        "w_o": lay_straight(i["w_o"][0]),
        "w_gate": lay_turned(i["w_gate"][0]), "w_up1": lay_turned(i["w_up"][0]),
        "w_down1": lay_straight(i["w_down"][0]),
        "w_tail": lay_straight(np.concatenate([w_in[:, C_KV:Q_D], w_in[:, K_IDX:]], axis=1), TAIL),
        "w_in": lay_straight(np.concatenate([w_in[:, Q_IDX:K_IDX], w_in[:, Q_D:Q_IDX], w_in[:, C_Q:C_KV]], axis=1)),
        "w_qnope": lay_turned(qb[:, :, 0:P].reshape(512, 1024)),
        "w_qrope": lay_straight(qb[:, :, P:].reshape(512, 512)),
        "w_knope": lay_turned(kvb[:, :, 0:P].reshape(256, 1024)),
        "w_vmla": lay_straight(kvb[:, :, P:].reshape(256, 1024)),
        "w_out": lay_straight(i["w_out_2"][0]),
        "w_qx": lay_turned(i["w_q_cross_2"][0]), "w_kx": lay_turned(i["w_k_cross_2"][0]),
        "w_vx": lay_straight(i["w_v_cross_2"][0]), "w_ox": lay_straight(i["w_o_cross_2"][0]),
        "w_up2": lay_turned(i["w_up_2"][0]), "w_down2": lay_straight(i["w_down_2"][0]),
    }
    nc = bacc.Bacc("TRN2", target_bir_lowering=False, num_devices=1)
    arrays = {f"in_{n}": np.ascontiguousarray(a) for n, a in arrays.items()}
    dram = {n[3:]: nc.dram_tensor(n, a.shape, mybir.dt.from_np(a.dtype), kind="ExternalInput").ap()
            for n, a in arrays.items()}
    out = nc.dram_tensor("out", (TOK, D), F32, kind="ExternalOutput").ap()
    build_program(nc, dram, out)
    r = run_bass_kernel_spmd(nc, [arrays], core_ids=[0])
    return r.results[0]["out"].reshape(1, TOK, D)
```

```python
from contextlib import ExitStack

import numpy as np
import concourse.bass as bass
from concourse import mybir

F32 = mybir.dt.float32
F32R = mybir.dt.float32r
I32 = mybir.dt.int32
ALU = mybir.AluOpType
ACT = mybir.ActivationFunctionType
AX_X = mybir.AxisListType.X

P = 128
TOK = 256
TT = TOK // P
D = 2048
DK = D // P
CHUNK = 64
F1 = 5632
F2 = 8192
HD = 64
NH = 8
MIX = 2048
N_REL = 192
IDX_HEADS = 16
TOPK = 64
NEG = -1.0e30
TAKEN = -3.0e38
PHASE = 16
TURNED_COLS = 256
STRAIGHT_COLS = 512
SUMS = 96
UNIT = 1024
RAW_SLOTS = 4
SPLIT_SLOTS = 4
EXPS = "natural_log_exp_and_others"
ROOTS = "sqrt_and_others"

C_Q, C_KV, K_ROPE, Q_D, K_D, V_D, Q_IDX, K_IDX, W_IDX = 0, 512, 768, 832, 1856, 2880, 3904, 4928, 4992
TAIL = 256 + 64 + 64 + 16

CONSTS = [("ident", P), ("flip", P), ("after", P), ("causal", P), ("ones", P),
          ("mask", TOK), ("blocked", TOK), ("dist", TOK), ("freq", 32), ("half", 1), ("eighth", 1), ("less_eighth", 1)]
GAINS = [("attn", 16), ("y1", 16), ("ffn", 16), ("conv0", 44), ("conv1", 44), ("conv2", 44), ("convb", 44),
         ("mix", 16), ("cq", 4), ("ckv", 2), ("cross", 16), ("mem", 16), ("mlp", 16)]


def columns_of(table):
    at, out = 0, {}
    for name, width in table:
        out[name] = (at, at + width)
        at += width
    return out, at


class Engine:

    def __init__(self, semaphore):
        self.semaphore, self.count, self.program, self.reached = semaphore, 0, [], {}

    def wait(self, *marks):
        for mark in flat(marks):
            semaphore, value = mark
            if self.reached.get(semaphore.name, 0) < value:
                self.reached[semaphore.name] = value
                self.program.append(lambda e, s=semaphore, v=value: e.wait_ge(s, v))

    def do(self, issue, *marks):
        self.wait(*marks)
        self.count += 1
        self.program.append(lambda e: issue(e).then_inc(self.semaphore, 1))
        return (self.semaphore, self.count)

    def run(self, e):
        for step in self.program:
            step(e)


def flat(marks):
    for m in marks:
        if m is None:
            continue
        if isinstance(m, list):
            yield from flat(m)
        else:
            yield m


class Banks:

    def __init__(self, banks):
        self.banks, self.free, self.at = banks, [None] * len(banks), 0

    def take(self):
        n = self.at % len(self.banks)
        self.at += 1
        return n, self.banks[n]


class Slots:

    def __init__(self, views):
        self.views, self.free = views, [None] * len(views)

    def of(self, i):
        return i % len(self.views), self.views[i % len(self.views)]


def build_program(nc, dram, out_dram):
    const_at, n_const = columns_of(CONSTS)
    gain_at, n_gain = columns_of(GAINS)

    ctx = ExitStack()
    with ctx:
        def sbuf(name, shape, dt=F32, scope=ctx):
            return scope.enter_context(nc.sbuf_tensor(name, shape, dt))

        raw_w = sbuf("raw_w", [P, RAW_SLOTS, UNIT])
        hi_w = sbuf("hi_w", [P, SPLIT_SLOTS, UNIT], F32R)
        lo_w = sbuf("lo_w", [P, SPLIT_SLOTS, UNIT], F32R)
        x = sbuf("x", [P, TT, D])
        xT = sbuf("xT", [P, DK, 2, TOK], F32R)
        xT_hi, xT_lo = xT[:, :, 0, :], xT[:, :, 1, :]
        consts = sbuf("consts", [P, n_const])
        gains = sbuf("gains", [P, n_gain])
        stats = sbuf("stats", [P, 192])
        banks = [ctx.enter_context(nc.psum_tensor(f"bank{i}", [P, 512], F32)) for i in range(8)]

        pe = Engine(ctx.enter_context(nc.semaphore("pe_done")))
        act = Engine(ctx.enter_context(nc.semaphore("act_done")))
        dve = Engine(ctx.enter_context(nc.semaphore("dve_done")))
        weights_in = Engine(None)
        others_in = Engine(None)
        raw_landed = [ctx.enter_context(nc.semaphore(f"raw_landed{i}")) for i in range(RAW_SLOTS)]

        def const(name):
            a, b = const_at[name]
            return consts[:, a:b]

        def gain(name, k):
            a = gain_at[name][0]
            return gains[:, a + k:a + k + 1]

        def load(queue, dst, src, name, *marks):
            landed = ctx.enter_context(nc.semaphore(name))
            queue.wait(*marks)
            queue.program.append(lambda e: e.dma_start(dst, src).then_inc(landed, 16))
            return (landed, 16)

        gemm_banks = Banks(banks[0:4])
        work_banks = Banks(banks[4:8])

        x_in = [[load(weights_in, x[:, t, a:a + D // 2], dram["x"][t * P:(t + 1) * P, a:a + D // 2],
                      f"x_landed{t}{a}") for a in (0, D // 2)] for t in range(TT)]
        consts_in = load(weights_in, consts[:, :], dram["consts"], "consts_landed")
        gains_in = load(weights_in, gains[:, :], dram["gains"], "gains_landed")

        def units_turned(name, groups, kts):
            per = min(4, kts)
            return [(name, g, u) for g in groups for u in range(kts // per)]

        def units_straight(name, chunks, kts, k0=0):
            return [(name, c, k0 // 2 + u) for c in chunks for u in range(kts // 2)]

        phases1 = [(a, min(a + PHASE, F1 // P)) for a in range(0, F1 // P, PHASE)]
        phases2 = [(a, min(a + PHASE, F2 // P)) for a in range(0, F2 // P, PHASE)]

        def mlp_units(phases, ups, down):
            out = []
            for n, (a, b) in enumerate(phases):
                for pair in range(a // 2, b // 2):
                    for name in ups:
                        out += units_turned(name, [pair], DK)
                if n:
                    out += units_straight(down, range(4), phases[n - 1][1] - phases[n - 1][0], phases[n - 1][0])
            return out + units_straight(down, range(4), phases[-1][1] - phases[-1][0], phases[-1][0])

        QKV_ORDER = [("w_qk", [0, 1, 4, 5]), ("w_v", [0]), ("w_qk", [2, 3, 6, 7]), ("w_v", [1]),
                     ("w_qk", [8, 9, 10, 11]), ("w_v", [2]), ("w_qk", [12, 13, 14, 15]), ("w_v", [3])]
        plan = []
        for name, parts in QKV_ORDER:
            plan += (units_turned if name == "w_qk" else units_straight)(name, parts, DK)
        plan += units_straight("w_o", range(4), 12) + units_straight("w_o", range(4), 4, 12)
        plan += mlp_units(phases1, ["w_gate", "w_up1"], "w_down1")
        plan += units_straight("w_tail", [0], DK) + units_straight("w_in", [8, 0, 1], DK)
        plan += units_turned("w_qnope", range(4), 4) + units_straight("w_qrope", [0], 4)
        plan += units_turned("w_knope", range(4), 2) + units_straight("w_vmla", range(2), 2)
        plan += units_straight("w_in", range(2, 8), DK)
        plan += units_straight("w_out", range(4), 8) + units_straight("w_out", range(4), 8, 8)
        plan += units_turned("w_kx", range(2), DK) + units_turned("w_qx", range(2), DK)
        plan += units_straight("w_vx", [0], DK) + units_straight("w_ox", range(4), 4)
        plan += mlp_units(phases2, ["w_up2"], "w_down2")

        def unit_source(u):
            name, part, k = plan[u]
            return dram[name][part, k].rearrange("p k c -> p (k c)")

        class WeightStream:

            def __init__(self):
                self.loaded = self.split_up_to = self.at = 0
                self.split_done = {}
                self.used = {}
                for _ in range(RAW_SLOTS):
                    self.load()
                for _ in range(SPLIT_SLOTS - 1):
                    self.split()

            def load(self):
                u = self.loaded
                if u >= len(plan):
                    return
                self.loaded += 1
                slot, src = u % RAW_SLOTS, unit_source(u)
                weights_in.wait(self.split_done.get(u - RAW_SLOTS))
                weights_in.program.append(
                    lambda e: e.dma_start(raw_w[:, slot, 0:src.shape[1]], src).then_inc(raw_landed[slot], 16))

            def split(self):
                u = self.split_up_to
                if u >= len(plan):
                    return
                self.split_up_to += 1
                n = unit_source(u).shape[1]
                raw = raw_w[:, u % RAW_SLOTS, 0:n]
                hi, lo = hi_w[:, u % SPLIT_SLOTS, 0:n], lo_w[:, u % SPLIT_SLOTS, 0:n]
                landed = (raw_landed[u % RAW_SLOTS], 16 * (u // RAW_SLOTS + 1))
                free = self.used.get(u - SPLIT_SLOTS)
                hi_done = act.do(lambda e: e.activation(hi, raw, ACT.Copy), landed, free)
                lo_done = dve.do(lambda e: e.tensor_tensor(lo, raw, hi.bitcast(F32), ALU.subtract), hi_done)
                self.split_done[u] = [lo_done, hi_done]
                self.load()

            def take(self, name, part, k):
                assert plan[self.at] == (name, part, k), (plan[self.at], name, part, k)
                self.split()
                u, n = self.at, unit_source(self.at).shape[1]
                return hi_w[:, u % SPLIT_SLOTS, 0:n], lo_w[:, u % SPLIT_SLOTS, 0:n], self.split_done[u][0]

            def release(self, mark):
                self.used[self.at] = mark
                self.at += 1

        def turned(name, groups, kts, both, in_ready, evict):
            per = min(4, kts)
            for g in groups:
                pair = [gemm_banks.take() for _ in range(2)]
                for u in range(kts // per):
                    w_hi, w_lo, w_ready = stream.take(name, g, u)

                    def issue(e, c, u=u, w_hi=w_hi, w_lo=w_lo, pair=pair):
                        o = pair[c][1]
                        for k in range(per):
                            kt = u * per + k
                            cols_k = slice(k * TURNED_COLS + c * P, k * TURNED_COLS + (c + 1) * P)
                            e.matmul(o[:, :], w_hi[:, cols_k], both[:, kt].rearrange("p h t -> p (h t)"),
                                     start=(kt == 0), stop=False, skip_group_check=True)
                            last = e.matmul(o[:, 0:TOK], w_lo[:, cols_k], both[:, kt, 0, :],
                                            start=False, stop=(kt == kts - 1), skip_group_check=True)
                        return last

                    ready = [in_ready[u * per + k] for k in range(per)]
                    free = [gemm_banks.free[n] for n, _ in pair] if u == 0 else None
                    marks = [pe.do(lambda e, c=c, issue=issue: issue(e, c), w_ready, ready, free) for c in range(2)]
                    stream.release(marks[-1])
                    if u < kts // per - 1:
                        yield
                for c, (n, bank) in enumerate(pair):
                    gemm_banks.free[n] = evict(2 * g + c, bank, marks[c])
                yield

        def summed(out, bank, ready, free=None, scale=1.0):
            lo = act.do(lambda e: e.activation(out, bank[:, TOK:2 * TOK], ACT.Copy, scale=scale), ready, free)
            return dve.do(lambda e: e.scalar_tensor_tensor(out, bank[:, 0:TOK], scale, out, ALU.mult, ALU.add), lo)

        def straight(name, chunks, kts, in_hi, in_lo, in_ready, evict, width=STRAIGHT_COLS, k0=0, in0=None):
            in0 = k0 if in0 is None else in0
            for c in chunks:
                pair = [gemm_banks.take() for _ in range(TT)]
                for u in range(kts // 2):
                    w_hi, w_lo, w_ready = stream.take(name, c, k0 // 2 + u)

                    def issue(e, t, u=u, w_hi=w_hi, w_lo=w_lo, pair=pair):
                        rows = slice(t * P, (t + 1) * P)
                        for k in range(2):
                            kt = u * 2 + k
                            cols_k = slice(k * width, (k + 1) * width)
                            passes = [(in_hi, w_hi), (in_hi, w_lo), (in_lo, w_hi)]
                            for i, (v, w) in enumerate(passes):
                                last = e.matmul(pair[t][1][:, 0:width], v[:, in0 + kt, rows], w[:, cols_k],
                                                start=(kt == 0 and i == 0),
                                                stop=(kt == kts - 1 and i == 2))
                        return last

                    ready = [in_ready[in0 + u * 2 + k] for k in range(2)]
                    free = [gemm_banks.free[n] for n, _ in pair] if u == 0 else None
                    marks = [pe.do(lambda e, t=t, issue=issue: issue(e, t), w_ready, ready, free) for t in range(TT)]
                    stream.release(marks[-1])
                    if u < kts // 2 - 1:
                        yield
                for t, (n, bank) in enumerate(pair):
                    gemm_banks.free[n] = evict(c, t, bank, marks[t])
                yield

        class Filler:

            def __init__(self, *products):
                self.left = (None for product in products for _ in product)

            def advance(self, units):
                for _ in range(units):
                    next(self.left, None)

            def until(self, have):
                while not have():
                    next(self.left)

            def finish(self):
                for _ in self.left:
                    pass

        def run(product):
            for _ in product:
                pass

        def inverse_root(v, width, ready):
            r, t = stats[:, 64:64 + width], stats[:, 128:128 + width]
            b = act.do(lambda e: e.activation(r, v, ACT.Sqrt), ready)
            b = dve.do(lambda e: e.reciprocal(r, r), b)
            c = dve.do(lambda e: e.scalar_tensor_tensor(t, r, -0.5, v, ALU.mult, ALU.mult), b)
            c = dve.do(lambda e: e.tensor_tensor(t, t, r, ALU.mult), c)
            return dve.do(lambda e: e.scalar_tensor_tensor(v, t, 1.5, r, ALU.add, ALU.mult), c)

        def mean_plus_eps(view, n, eps, ready):
            return dve.do(lambda e: e.tensor_scalar(view, view, 1.0 / n, eps, ALU.mult, ALU.add), ready)

        def fine_exp(quarters, rest, out, ready, out_free=None):
            a = act.do(lambda e: e.activation(out, quarters, ACT.Exp, bias=const("eighth"), scale=0.25),
                       ready, out_free)
            b = act.do(lambda e: e.activation(rest, rest, ACT.Exp, bias=const("less_eighth"), scale=0.25))
            return [a, b]

        def rms_scaled(src, dst, n, ready, dst_free, stat):
            marks = []
            for t in range(TT):
                ss = stats[:, stat + t:stat + t + 1]
                marks.append(act.do(lambda e, t=t, ss=ss: e.activation(dst[:, t, :], src[:, t, :], ACT.Square,
                                                                       accum_out=ss), ready, dst_free))
            ss = stats[:, stat:stat + TT]
            scale = inverse_root(ss, TT, mean_plus_eps(ss, n, 1e-6, marks))
            return [dve.do(lambda e, t=t: e.tensor_scalar(dst[:, t, :], src[:, t, :],
                                                          stats[:, stat + t:stat + t + 1], None, ALU.mult),
                           scale) for t in range(TT)]

        def turn_and_split(src, n_kt, gain_name, dst_hi, dst_lo, ready, dst_free, kt0=0, src0=None):
            src0 = kt0 if src0 is None else src0
            done = [None] * (kt0 + n_kt)
            for pair in range(n_kt // 2):
                n, bank = work_banks.take()

                def issue(e, pair=pair, bank=bank):
                    for k in range(2):
                        for t in range(TT):
                            kt = src0 + pair * 2 + k
                            last = e.transpose(bank[:, k * TOK + t * P:k * TOK + (t + 1) * P],
                                               src[:, t, kt * P:(kt + 1) * P], const("ident"))
                    return last

                turned_mark = pe.do(issue, ready, work_banks.free[n], consts_in)
                his = []
                for k in range(2):
                    kt = pair * 2 + k
                    half, hi = bank[:, k * TOK:(k + 1) * TOK], dst_hi[:, kt0 + kt, :]
                    scale = gain(gain_name, src0 + kt) if gain_name else 1.0
                    his.append(act.do(lambda e, hi=hi, half=half, scale=scale:
                                      e.activation(hi, half, ACT.Copy, scale=scale),
                                      turned_mark, dst_free, gains_in))
                for k in range(2):
                    kt = pair * 2 + k
                    half, hi, lo = bank[:, k * TOK:(k + 1) * TOK], dst_hi[:, kt0 + kt, :], dst_lo[:, kt0 + kt, :]
                    scale = gain(gain_name, src0 + kt) if gain_name else 1.0
                    done[kt0 + kt] = dve.do(lambda e, hi=hi, half=half, lo=lo, scale=scale:
                                            e.scalar_tensor_tensor(lo, half, scale, hi.bitcast(F32),
                                                                   ALU.mult, ALU.subtract),
                                            his, dst_free, gains_in)
                work_banks.free[n] = done[kt0 + pair * 2 + 1]
            return done

        def square_sum(src, col, ready):
            n, bank = work_banks.take()
            work_banks.free[n] = act.do(lambda e: e.activation(bank[:, 0:src.shape[1]], src, ACT.Square,
                                                               accum_out=stats[:, col:col + 1]),
                                        ready, work_banks.free[n])
            return work_banks.free[n]

        def add_to_x(x_ready, squared=None, gained=None):
            def evict(c, t, bank, mark):
                cols = slice(c * STRAIGHT_COLS, (c + 1) * STRAIGHT_COLS)
                here = x[:, t, cols]
                if gained is None:
                    done = dve.do(lambda e: e.tensor_tensor(here, bank[:, :], here, ALU.add), mark, x_ready[:])
                    x_ready.append(done)
                    if squared is not None:
                        squared.append(square_sum(here, SUMS + 4 * t + c, done))
                    return done
                g, g_in, buffer, buffer_free, both = gained
                total = buffer[:, t, cols]
                done = dve.do(lambda e: e.tensor_tensor(total, bank[:, :], here, ALU.add),
                              mark, x_ready[:], buffer_free)
                times_g = dve.do(lambda e: e.tensor_tensor(here, total, g[:, cols], ALU.mult), done, g_in)
                x_ready.append(times_g)
                squared.append(square_sum(total, SUMS + 4 * t + c, done))
                if both:
                    squared.append(square_sum(here, SUMS + 8 + 4 * t + c, times_g))
                return done
            return evict

        def token_scales(squared, both=False):
            rows = 2 * TT if both else TT
            v, v_gained = stats[:, 0:TT], stats[:, TT:2 * TT]
            sums = stats[:, SUMS:SUMS + 4 * rows].rearrange("p (r c) -> p r c", c=4)
            a = dve.do(lambda e: e.tensor_reduce(stats[:, 0:rows], sums, AX_X, ALU.add), squared)
            a = mean_plus_eps(v, D, 1e-6, a)
            if both:
                eps_v = stats[:, 128:128 + TT]
                a = dve.do(lambda e: e.tensor_scalar(eps_v, v, 1e-6, None, ALU.mult), a)
                a = dve.do(lambda e: e.scalar_tensor_tensor(v_gained, v_gained, 1.0 / D, eps_v, ALU.mult, ALU.add), a)
            return inverse_root(stats[:, 0:rows], rows, a)

        def normed_turned(dst, col, gain_name, scale_ready, dst_free, xT_free, marks):
            def scaled(piece):
                cols = slice(512 * piece, 512 * piece + 512)
                a = dve.do(lambda e: e.tensor_scalar(dst[:, 0, cols], x[:, 0, cols], stats[:, col:col + 1], None,
                                                     ALU.mult), scale_ready, dst_free)
                b = act.do(lambda e: e.activation(dst[:, 1, cols], x[:, 1, cols], ACT.Copy,
                                                  scale=stats[:, col + 1:col + 2]), scale_ready, dst_free)
                return [a, b]

            ahead = scaled(0)
            for piece in range(4):
                here, ahead = ahead, scaled(piece + 1) if piece < 3 else None
                kt0 = 4 * piece
                marks[kt0:kt0 + 4] = turn_and_split(dst, 4, gain_name, xT_hi, xT_lo, here, xT_free, kt0)[kt0:]
                yield

        def lead(pieces, product, units):
            next(pieces, None)
            for _ in pieces:
                for _ in range(units):
                    next(product, None)

        FILL = None

        def pipeline(items, stages, filler=None, rate=0.0):
            due = 0.0
            for s in range(len(items) + max(stage[0] for stage in stages if stage)):
                for stage in stages:
                    if stage is FILL:
                        due += rate
                        if filler and due >= 1:
                            filler.advance(int(due))
                            due -= int(due)
                    elif 0 <= s - stage[0] < len(items):
                        stage[1](items[s - stage[0]], s - stage[0])

        def softmax_buffers(scope, prefix, wide):
            b = {}
            for name, depth, width in (("s", 3, wide), ("p", 3, wide), ("pT", 2, TOK)):
                t = sbuf(prefix + name, [P, depth, width], F32, scope)
                b[name] = Slots([t[:, i, :] for i in range(depth)])
            small = sbuf(prefix + "small", [P, 4, 8], F32, scope)
            b["small"] = Slots([small[:, i, :] for i in range(4)])
            return b

        def turn_stage(b):
            def stage(item, i):
                kts, weights = item["W"] // P, item["p"]
                n, bank = work_banks.take()

                def turn(e):
                    for k in range(kts):
                        last = e.transpose(bank[:, k * P:(k + 1) * P], weights[:, k * P:(k + 1) * P], const("ident"))
                    return last

                mark = pe.do(turn, item["p_ready"], work_banks.free[n])
                b["p"].free[item["p_slot"]] = mark
                slot, pT = b["pT"].of(i)
                copied = act.do(lambda e: e.activation(pT[:, 0:kts * P], bank[:, 0:kts * P], ACT.Copy),
                                mark, b["pT"].free[slot])
                work_banks.free[n] = copied
                item["pT"], item["pT_ready"], item["pT_slot"] = pT, copied, slot
            return stage

        def values_stage(b):
            def stage(item, i):
                kts, pT = item["W"] // P, item["pT"]
                n, bank = work_banks.take()
                wide = item["width"]

                def issue(e):
                    for k in range(kts):
                        last = e.matmul(bank[:, 0:wide], pT[:, k * P:(k + 1) * P], item["v"](k),
                                        start=(k == 0), stop=(k == kts - 1))
                    return last

                mark = pe.do(issue, item["pT_ready"], item["v_ready"](), work_banks.free[n])
                b["pT"].free[item["pT_slot"]] = mark
                scale = item["scale_out"]
                done = act.do(lambda e: e.activation(item["out"], bank[:, 0:wide], ACT.Copy, scale=scale),
                              mark, item["scale_ready"], item.get("out_free"))
                if "ss" in item:
                    slot, junk = b["s"].of(i)
                    done = act.do(lambda e: e.activation(junk[:, 0:wide], bank[:, 0:wide], ACT.Square,
                                                         scale=scale, accum_out=item["ss"]), b["s"].free[slot])
                    b["s"].free[slot] = [b["s"].free[slot], done]
                b["small"].free[item["small_slot"]] = done
                work_banks.free[n] = done
                item["done"] = done
            return stage

        def softmax_stages(b, values=None):
            def scores(item, i):
                n, bank = work_banks.take()
                mark = pe.do(lambda e: item["scores"](e, bank), item["ready"](), work_banks.free[n])
                item["bank"], item["bank_n"], item["mark"] = bank, n, mark

            def soft(item, i):
                W, bank = item["W"], item["bank"]
                slot, s = b["s"].of(i)
                p_slot, p = b["p"].of(i)
                m_slot, small = b["small"].of(i)
                free = [b["s"].free[slot], b["small"].free[m_slot]]
                if item["kind"] == "fine":
                    m = dve.do(lambda e: e.tensor_tensor_reduce(s[:, 0:W], bank[:, 0:W], item["mask"], 1.0, TAKEN,
                                                                ALU.add, ALU.max, small[:, 0:1]),
                               item["mark"], item["mask_ready"], free)
                    work_banks.free[item["bank_n"]] = m
                    quarters = p.bitcast(I32)
                    q = dve.do(lambda e: e.tensor_scalar(quarters[:, 0:W], s[:, 0:W], small[:, 0:1], -0.5,
                                                         ALU.subtract, ALU.add), m, b["p"].free[p_slot])
                    q = dve.do(lambda e: e.scalar_tensor_tensor(s[:, 0:W], s[:, 0:W], small[:, 0:1],
                                                                quarters[:, 0:W], ALU.subtract, ALU.subtract), q)
                    ex = q
                elif item["kind"] == "masked":
                    m = dve.do(lambda e: e.tensor_tensor_reduce(s[:, 0:W], bank[:, 0:W], item["mask"], 1.0, -TAKEN,
                                                                ALU.add, ALU.min, small[:, 0:1]),
                               item["mark"], item["mask_ready"], free)
                    work_banks.free[item["bank_n"]] = m
                    ex = act.do(lambda e: e.activation(p[:, 0:W], s[:, 0:W], ACT.Exp, bias=small[:, 0:1], scale=-1.0,
                                                       accum_out=small[:, 1:2]), m, b["p"].free[p_slot])
                else:
                    m = dve.do(lambda e: e.tensor_reduce(small[:, 0:1], bank[:, 0:W], AX_X, ALU.max, negate=True),
                               item["mark"], free)
                    ex = act.do(lambda e: e.activation(p[:, 0:W], bank[:, 0:W], ACT.Exp, bias=small[:, 0:1],
                                                       accum_out=small[:, 1:2]), m, b["p"].free[p_slot])
                    work_banks.free[item["bank_n"]] = ex
                b["s"].free[slot] = ex
                item["s"], item["s_slot"] = s, slot
                item["p"], item["p_slot"], item["p_ready"] = p, p_slot, ex
                item["small"], item["small_slot"] = small, m_slot

            def fine(item, i):
                W, s, p = item["W"], item["s"], item["p"]
                if item["kind"] == "fine":
                    item["p_ready"] = fine_exp(p.bitcast(I32)[:, 0:W], s[:, 0:W], p[:, 0:W], item["p_ready"])

            def total(item, i):
                W, s, p, small = item["W"], item["s"], item["p"], item["small"]
                if item["kind"] == "fine":
                    item["p_ready"] = b["s"].free[item["s_slot"]] = dve.do(lambda e: e.tensor_tensor_reduce(
                        p[:, 0:W], p[:, 0:W], s[:, 0:W], 1.0, 0.0, ALU.mult, ALU.add, small[:, 1:2]),
                        item["p_ready"])
                item["scale_out"] = small[:, 2:3]
                item["scale_ready"] = dve.do(lambda e: e.reciprocal(small[:, 2:3], small[:, 1:2]), item["p_ready"])

            return [(4, values or values_stage(b)), (3, turn_stage(b)), (2, fine), (1, soft), (2, total), FILL,
                    (0, scores)]

        scope = ExitStack()
        qkT = sbuf("qkT", [P, 32, TOK], F32, scope)
        v1 = sbuf("v1", [P, TT, D], F32, scope)
        y1 = sbuf("y1", [P, TT, D], F32, scope)
        rel = sbuf("rel", [P, NH, TOK], F32, scope)
        lams = sbuf("lams", [P, 4, HD], F32, scope)
        b1 = softmax_buffers(scope, "a1_", 2 * TOK)
        act.program.append(lambda e: e.preload_act_table_set(ROOTS))
        x_squares = [act.do(lambda e, t=t, c=c: e.activation(
            banks[4 * t + c][:, :], x[:, t, 512 * c:512 * c + 512], ACT.Square,
            accum_out=stats[:, SUMS + 4 * t + c:SUMS + 4 * t + c + 1]), x_in[t][c // 2])
            for t in range(TT) for c in range(4)]
        gemm_banks.free, work_banks.free = x_squares[:4], x_squares[4:]
        h_in = [None] * DK
        h_scale = token_scales(x_squares)
        h_pieces = normed_turned(y1, 0, "attn", h_scale, None, None, h_in)
        next(h_pieces)
        stream = WeightStream()

        Q_SCALE = HD ** -0.5

        ext = nc.dram_tensor("rel_ext", (NH, 384), F32, kind="Internal").ap()
        ext_sb = v1[0:NH, 1, 0:384]
        table_in = load(others_in, ext_sb[:, 127:319], dram["rel_rev"], "rel_table_landed")
        far = dve.do(lambda e: e.tensor_copy(ext_sb[:, 0:127], ext_sb[:, 127:128].to_broadcast([NH, 127])), table_in)
        near = dve.do(lambda e: e.tensor_copy(ext_sb[:, 319:384], ext_sb[:, 318:319].to_broadcast([NH, 65])))
        ext_done = load(others_in, ext, ext_sb, "rel_ext_landed", near)
        hankel_src = bass.AP(tensor=ext.tensor, offset=0, ap=[[1, P], [384, NH], [1, TOK]])
        hankel = v1[:, 0, :].rearrange("p (h k) -> p h k", h=NH)
        hankel_in = load(others_in, hankel, hankel_src, "hankel_landed", ext_done)
        lams_in = load(others_in, lams[:, :, :], bass.AP(tensor=dram["lambdas"].tensor, offset=0,
                                                         ap=[[0, P], [HD, 4], [1, HD]]), "lams_landed")


        qk_ready = {}

        def evict_qk(tile, bank, mark):
            scale = 1.0
            if tile < 8 or 24 <= tile < 28:
                scale = 4 * Q_SCALE
            elif 16 <= tile < 20:
                scale = Q_SCALE
            qk_ready[tile] = summed(qkT[:, tile, :], bank, mark, scale=scale)
            return qk_ready[tile]

        v_ready = {}

        def evict_v(c, t, bank, mark):
            done = act.do(lambda e: e.activation(v1[:, t, c * 512:(c + 1) * 512], bank[:, :], ACT.Copy),
                          mark, hankel_read)
            v_ready[c, t] = done
            return done

        qkv = Filler(*(
            turned(name, parts, DK, xT, h_in, evict_qk) if name == "w_qk" else
            straight(name, parts, DK, xT_hi, xT_lo, h_in, evict_v) for name, parts in QKV_ORDER))

        for _ in h_pieces:
            qkv.advance(1)

        dots = [dve.do(lambda e, j=j: e.tensor_tensor_reduce(lams[:, 2 * j, :], lams[:, 2 * j, :], lams[:, 2 * j + 1, :],
                                                             1.0, 0.0, ALU.mult, ALU.add, stats[:, 8 + j:9 + j]),
                       lams_in) for j in range(2)]
        lam_x, lam_n = stats[:, 8:10], stats[:, 12:14]
        m = dve.do(lambda e: e.tensor_scalar(lam_n.bitcast(I32), lam_x, 4.0, -0.5, ALU.mult, ALU.add), dots)
        m = dve.do(lambda e: e.scalar_tensor_tensor(lam_x, lam_x, 4.0, lam_n.bitcast(I32), ALU.mult, ALU.subtract), m)
        lam_e = fine_exp(lam_n.bitcast(I32), lam_x, lam_n, [m, consts_in])
        m = dve.do(lambda e: e.tensor_tensor(lam_x, lam_x, lam_n, ALU.mult), lam_e)
        lam_d = dve.do(lambda e: e.tensor_tensor(stats[:, 10:11], stats[:, 9:10], stats[:, 8:9], ALU.subtract), m)
        neg_lam = stats[:, 11:12]
        neg_lam_ready = dve.do(lambda e: e.tensor_scalar(neg_lam, stats[:, 10:11], -0.2, None, ALU.add), lam_d)

        rel_ready = []
        for h in range(NH):
            n, bank = work_banks.take()
            mark = pe.do(lambda e, h=h, bank=bank: e.matmul(bank[:, 0:TOK], const("flip"), hankel[:, h, :],
                                                            start=True, stop=True),
                         hankel_in, consts_in, work_banks.free[n])
            done = dve.do(lambda e, h=h, bank=bank: e.scalar_tensor_tensor(
                rel[:, h, :], bank[:, 0:TOK], 4.0, const("mask"), ALU.mult, ALU.add), mark)
            work_banks.free[n] = done
            rel_ready.append(done)
        hankel_read = mark

        ss1 = stats[:, 16:64]

        def head_ss(branch, t, h):
            col = 16 * branch + 8 * t + h
            return ss1[:, col:col + 1]

        act.program.append(lambda e: e.preload_act_table_set(EXPS))

        def token_tile(t):
            return (P, P) if t == 0 else (TOK, 0)

        scaled_dist = sbuf("scaled_dist", [P, 2, TOK], F32, scope)
        dists = Slots([scaled_dist[:, j, :] for j in range(2)])
        dists.ready = [None, None]

        def diff_scores(item, i):
            t, h, W = item["t"], item["h"], item["W"]
            item["banks"] = []
            n_dist, dist = dists.of(h)
            if t == 0:
                dists.ready[n_dist] = act.do(
                    lambda e: e.activation(dist, const("dist"), ACT.Copy, scale=4 * 2.0 ** -(h + 1)),
                    consts_in, dists.free[n_dist])
            qkv.until(lambda: h in qk_ready and 8 + h in qk_ready)
            for c in range(2):
                n, bank = work_banks.take()
                rows = slice(c * 64, (c + 1) * 64)
                mark = pe.do(lambda e, rows=rows, bank=bank: e.matmul(
                    bank[:, 0:W], qkT[rows, h, t * P:(t + 1) * P], qkT[rows, 8 + h, 0:W], start=True, stop=True),
                    qk_ready[h], qk_ready[8 + h], work_banks.free[n])
                item["banks"].append((n, bank, mark))

        def diff_soft(item, i):
            h, W, m0 = item["h"], item["W"], item["m0"]
            slot, s = b1["s"].of(i)
            p_slot, p = b1["p"].of(i)
            m_slot, small = b1["small"].of(i)
            n_dist, dist = dists.of(h)
            maxima = []
            for c, (n, bank, mark) in enumerate(item["banks"]):
                a = dve.do(lambda e, c=c, bank=bank: e.tensor_tensor_reduce(
                    s[:, c * W:(c + 1) * W], bank[:, 0:W], dist[:, m0:m0 + W], 1.0, TAKEN,
                    ALU.add, ALU.max, small[:, c:c + 1]),
                    mark, dists.ready[n_dist], b1["s"].free[slot], b1["small"].free[m_slot])
                work_banks.free[n] = a
                maxima.append(a)
            dists.free[n_dist] = a
            quarters = p.bitcast(I32)
            rests = []
            for c in range(2):
                part = slice(c * W, (c + 1) * W)
                q = dve.do(lambda e, part=part, c=c: e.tensor_scalar(quarters[:, part], s[:, part], small[:, c:c + 1],
                                                                     -0.5, ALU.subtract, ALU.add),
                           maxima[c], b1["p"].free[p_slot])
                rests.append(dve.do(lambda e, part=part, c=c: e.scalar_tensor_tensor(
                    s[:, part], s[:, part], small[:, c:c + 1], quarters[:, part], ALU.subtract, ALU.subtract), q))
            item.update(s=s, s_slot=slot, p=p, p_slot=p_slot, small=small, small_slot=m_slot, rests=rests)

        def diff_exp(item, i):
            W, s, p = item["W"], item["s"], item["p"]
            item["exps"] = fine_exp(p.bitcast(I32)[:, 0:2 * W], s[:, 0:2 * W], p[:, 0:2 * W], item["rests"])

        def diff_combine(item, i):
            W, s, p, small = item["W"], item["s"], item["p"], item["small"]
            exps = [dve.do(lambda e, part=slice(c * W, (c + 1) * W), c=c: e.tensor_tensor_reduce(
                p[:, part], p[:, part], s[:, part], 1.0, 0.0, ALU.mult, ALU.add, small[:, 2 + c:3 + c]), item["exps"])
                for c in range(2)]
            b1["s"].free[item["s_slot"]] = exps[-1]
            r = dve.do(lambda e: e.reciprocal(small[:, 4:6], small[:, 2:4]), exps)
            ratio = dve.do(lambda e: e.scalar_tensor_tensor(small[:, 6:7], small[:, 5:6], neg_lam, small[:, 2:3],
                                                            ALU.mult, ALU.mult), r, neg_lam_ready)
            item["p_ready"] = dve.do(lambda e: e.scalar_tensor_tensor(
                p[:, 0:W], p[:, W:2 * W], small[:, 6:7], p[:, 0:W], ALU.mult, ALU.add), ratio)
            item["scale_out"], item["scale_ready"] = small[:, 4:5], r

        def diff_v_ready(h):
            qkv.until(lambda: (h // 4, 1) in v_ready)
            return [v_ready[h // 4, k] for k in range(TT)]

        diff_items = []
        for h in range(NH):
            for t in range(TT):
                W, m0 = token_tile(t)
                diff_items.append(dict(
                    t=t, h=h, W=W, m0=m0, width=2 * HD, out=y1[:, t, h * P:(h + 1) * P],
                    ss=head_ss(0, t, h), v=lambda k, h=h: v1[:, k, h * P:(h + 1) * P],
                    v_ready=lambda h=h: diff_v_ready(h), out_free=h_in))
        qkv.until(lambda: (0, 1) in v_ready)
        pipeline(diff_items, [(4, values_stage(b1)), (3, turn_stage(b1)), (2, diff_exp), (1, diff_soft),
                              (2, diff_combine), FILL,
                              (0, diff_scores)], qkv, 2)

        def head_norm(branches, ready):
            cols = slice(16 * branches[0], 16 * branches[-1] + 16)
            dims = {0: (2 * HD, 1e-5), 1: (HD, 1e-6), 2: (HD, 1e-6)}
            a = [mean_plus_eps(ss1[:, 16 * b:16 * b + 16], *dims[b], ready) for b in branches]
            a = inverse_root(ss1[:, cols], 16 * len(branches), a)
            if 0 in branches:
                a = dve.do(lambda e: e.tensor_scalar(ss1[:, 0:16], ss1[:, 0:16], 0.8, None, ALU.mult), a)
            marks = []
            for b in branches:
                c0, w = (0, 2 * HD) if b == 0 else (1024 + 512 * (b - 1), HD)
                for t in range(TT):
                    view = y1[:, t, c0:c0 + 8 * w].rearrange("p (h c) -> p h c", c=w)
                    scale = ss1[:, 16 * b + 8 * t:16 * b + 8 * t + 8].unsqueeze(2).to_broadcast([P, 8, w])
                    marks.append(dve.do(lambda e, view=view, scale=scale: e.tensor_tensor(view, view, scale,
                                                                                          ALU.mult), a))
            return marks

        early_diff = head_norm([0], diff_items[-1]["done"])

        SBW = 384
        half_tanh = qkT[:, 0:12, :].rearrange("p a t -> p (a t)")
        diff_read = diff_items[-1]["banks"][1][2]
        sb_items = [dict(h=h, tile=h // 2, rows=slice(64 * (h % 2), 64 * (h % 2) + 64), c0=1024 + h * HD)
                    for h in range(NH)]

        def sb_scores(item, i):
            tile, rows = item["tile"], item["rows"]
            n, bank = work_banks.take()

            def issue(e):
                e.matmul(bank[:, 0:TOK], qkT[rows, 20 + tile, 0:P], qkT[rows, 16 + tile, :], start=True, stop=True)
                return e.matmul(bank[:, TOK:SBW], qkT[rows, 20 + tile, P:TOK], qkT[rows, 16 + tile, P:TOK],
                                start=True, stop=True)

            qkv.until(lambda: 20 + tile in qk_ready and 16 + tile in qk_ready)
            item["z"] = (n, bank, pe.do(issue, qk_ready[20 + tile], qk_ready[16 + tile], work_banks.free[n]))

        def sb_tanh(item, i):
            n, z, mark = item["z"]
            item["tanh"] = half_tanh[:, i * SBW:(i + 1) * SBW]
            item["tanh_ready"] = act.do(lambda e: e.activation(item["tanh"], z[:, 0:SBW], ACT.Tanh, scale=0.5),
                                        mark, diff_read)
            work_banks.free[n] = item["tanh_ready"]

        pipeline(sb_items, [(1, sb_tanh), FILL, (0, sb_scores)], qkv, .5)
        act.program.append(lambda e: e.preload_act_table_set(EXPS))

        def sb_softplus(item, i):
            n, z, mark = item["z"]
            slot, l = b1["s"].of(i)
            p_slot, d = b1["p"].of(i)
            l, d = l[:, 0:SBW], d[:, 0:SBW]
            th = item["tanh"]
            a = act.do(lambda e: e.activation(l, th, ACT.Abs), item["tanh_ready"], b1["s"].free[slot])
            a = act.do(lambda e: e.activation(l, l, ACT.Ln, bias=const("half"), scale=0.5), a)
            a = dve.do(lambda e: e.scalar_tensor_tensor(l, z[:, 0:SBW], 0.0, l, ALU.max, ALU.subtract), a, mark)
            item["d_ready"] = dve.do(lambda e: e.tensor_tensor(d, z[:, 0:SBW], l, ALU.subtract),
                                     a, b1["p"].free[p_slot])
            work_banks.free[n] = item["d_ready"]
            diagonal = l.rearrange("p (b q) -> p b q", b=3)[:, 0:3:2, :]
            item["l_ready"] = dve.do(lambda e: e.tensor_tensor(
                diagonal, diagonal, const("causal").unsqueeze(1).to_broadcast([P, 2, P]), ALU.mult),
                item["d_ready"])
            item["l"], item["d"], item["slot"], item["p_slot"] = l, d, slot, p_slot

        def sb_suffix(item, i):
            l, d = item["l"], item["d"]
            n, bank = work_banks.take()

            def issue(e):
                e.matmul(bank[:, 0:TOK], const("after"), l[:, 0:TOK], start=True, stop=True, skip_group_check=True)
                e.matmul(bank[:, P:TOK], const("ones"), l[:, TOK:SBW], start=False, stop=True,
                         skip_group_check=True)
                return e.matmul(bank[:, TOK:SBW], const("after"), l[:, TOK:SBW], start=False, stop=True,
                                skip_group_check=True)

            mark = pe.do(issue, item["l_ready"], work_banks.free[n])
            a = dve.do(lambda e: e.tensor_tensor(d, d, bank[:, 0:SBW], ALU.subtract), mark, item["d_ready"])
            work_banks.free[n] = a
            quarters = l.bitcast(I32)
            a = dve.do(lambda e: e.tensor_scalar(quarters, d, 4.0, -0.5, ALU.mult, ALU.add), a)
            a = dve.do(lambda e: e.scalar_tensor_tensor(d, d, 4.0, quarters, ALU.mult, ALU.subtract), a)
            a = fine_exp(quarters, d, l, a)
            a = dve.do(lambda e: e.tensor_tensor(d, d, l, ALU.mult), a)
            b1["s"].free[item["slot"]] = a
            diagonal = d.rearrange("p (b q) -> p b q", b=3)[:, 0:3:2, :]
            item["a_ready"] = dve.do(lambda e: e.tensor_tensor(
                diagonal, diagonal, const("causal").unsqueeze(1).to_broadcast([P, 2, P]), ALU.mult), a)

        def sb_values(item, i):
            d, c0 = item["d"], item["c0"]
            n, bank = work_banks.take()

            def issue(e):
                e.matmul(bank[:, 0:HD], d[:, 0:P], v1[:, 0, c0:c0 + HD], start=True, stop=True)
                e.matmul(bank[:, HD:2 * HD], d[:, P:TOK], v1[:, 0, c0:c0 + HD], start=True, stop=False)
                return e.matmul(bank[:, HD:2 * HD], d[:, TOK:SBW], v1[:, 1, c0:c0 + HD], start=False, stop=True)

            mark = pe.do(issue, item["a_ready"], [v_ready[2, k] for k in range(TT)], work_banks.free[n])
            slot, junk = b1["pT"].of(i)
            done = act.do(lambda e: e.activation(y1[:, :, c0:c0 + HD],
                                                 bank[:, 0:2 * HD].rearrange("p (t c) -> p t c", t=2), ACT.Copy), mark)
            for t in range(TT):
                ss = head_ss(1, t, item["h"])
                done = act.do(lambda e, t=t, ss=ss: e.activation(
                    junk[:, 0:HD], bank[:, t * HD:(t + 1) * HD], ACT.Square, accum_out=ss),
                    b1["pT"].free[slot], done)
            b1["pT"].free[slot] = done
            b1["p"].free[item["p_slot"]] = mark
            work_banks.free[n] = done
            item["done"] = done

        pipeline(sb_items, [(3, sb_values), (2, sb_suffix), (1, sb_softplus), FILL, (0, sb_scores)], qkv, 2.4)
        early_sb = head_norm([1], sb_items[-1]["done"])
        qkv.finish()
        xT_read = stream.used[stream.at - 1]

        x_ready = []
        y_in = [None] * 12
        out_early = Filler(straight("w_o", range(4), 12, xT_hi, xT_lo, y_in, add_to_x(x_ready)))
        for kt, ready in ((0, early_diff), (4, early_diff), (8, early_sb)):
            y_in[kt:kt + 4] = turn_and_split(y1, 4, "y1", xT_hi, xT_lo, ready, xT_read, kt)[kt:]
            if kt:
                out_early.advance(1)
        act.program.append(lambda e: e.preload_act_table_set(EXPS))

        band_items = []
        for h in range(NH):
            for t in range(TT):
                W, m0 = token_tile(t)
                tile, rows = h // 2, slice(64 * (h % 2), 64 * (h % 2) + 64)
                c0 = 1536 + h * HD
                band_items.append(dict(
                    W=W, width=HD, kind="fine", mask=rel[:, h, m0:m0 + W], mask_ready=rel_ready[h],
                    scores=lambda e, bank, t=t, W=W, tile=tile, rows=rows: e.matmul(
                        bank[:, 0:W], qkT[rows, 24 + tile, t * P:(t + 1) * P], qkT[rows, 28 + tile, 0:W],
                        start=True, stop=True),
                    ready=lambda tile=tile: [qk_ready[24 + tile], qk_ready[28 + tile]],
                    v=lambda k, c0=c0: v1[:, k, c0:c0 + HD], v_ready=lambda: [v_ready[3, k] for k in range(TT)],
                    out=y1[:, t, c0:c0 + HD], ss=head_ss(2, t, h)))
        pipeline(band_items, softmax_stages(b1), out_early, 1.0)

        late = head_norm([2], band_items[-1]["done"])
        out_early.advance(2)
        y_in2 = turn_and_split(y1, 4, "y1", xT_hi, xT_lo, late, xT_read, 12)
        out_early.finish()
        x_squared = []
        run(straight("w_o", range(4), 4, xT_hi, xT_lo, y_in2, add_to_x(x_ready, x_squared), k0=12))
        xT_read = stream.used[stream.at - 1]
        scope.close()
        block_free = [y_in, y_in2, late, hankel_read]

        def mlp(phases, gate, up, down, x_ready, x_squared, gain_name, dst_free, xT_read, end_gain, both, scope, tag):
            act_hi = sbuf(f"act_hi{tag}", [P, 2, PHASE, TOK], F32R, scope)
            act_lo = sbuf(f"act_lo{tag}", [P, 2, PHASE, TOK], F32R, scope)
            h_nat = sbuf(f"h_nat{tag}", [P, TT, D], F32, scope)
            steps = sbuf(f"steps{tag}", [P, D], F32, scope)
            conv, prod = (steps[:, a:a + 1024].rearrange("p (s c t) -> p s c t", s=2, c=2) for a in (0, 1024))
            prod_free = [None, None]
            product = sbuf(f"product{tag}", [P, 2, TOK], F32, scope)
            product_free = [None, None]
            h_in = [None] * DK
            h_pieces = normed_turned(h_nat, 0, gain_name, token_scales(x_squared), dst_free, xT_read, h_in)
            acts_ready = {}
            down_read = {}

            def split_act(pair, src, ready):
                n, a = pair // (PHASE // 2), 2 * pair % PHASE
                hi, lo = act_hi[:, n % 2, a:a + 2, :], act_lo[:, n % 2, a:a + 2, :]
                free = down_read.get(n - 2)
                h = act.do(lambda e: e.activation(hi, src, ACT.Copy), ready, free)
                l = dve.do(lambda e: e.tensor_tensor(lo, src, hi.bitcast(F32), ALU.subtract), h, free)
                acts_ready[n, a] = acts_ready[n, a + 1] = [h, l]
                return [h, l]

            def gate_pair(pair):
                slot = pair % 2
                cv, pr = conv[:, slot], prod[:, slot]
                state = {}

                def evict_gate(tile, bank, mark):
                    c = tile % 2
                    here, out = product[:, c, :], cv[:, c, :]
                    done = summed(here, bank, mark, product_free[c])
                    a = act.do(lambda e: e.activation(out, here, ACT.Identity, bias=gain("convb", tile),
                                                      scale=gain("conv2", tile)), done, prod_free[slot])
                    for shift, tap in ((1, "conv1"), (2, "conv0")):
                        a = dve.do(lambda e, shift=shift, tap=tap: e.scalar_tensor_tensor(
                            out[:, shift:TOK], here[:, 0:TOK - shift], gain(tap, tile), out[:, shift:TOK],
                            ALU.mult, ALU.add), a)
                    product_free[c] = state[c] = a
                    if c:
                        th = act.do(lambda e: e.activation(pr, cv, ACT.Tanh, scale=0.5), state[0], state[1],
                                    prod_free[slot])
                        state["silu2"] = dve.do(lambda e: e.scalar_tensor_tensor(pr, pr, 1.0, cv, ALU.add, ALU.mult), th)
                    return done

                def evict_up(tile, bank, mark):
                    c = tile % 2
                    done = summed(product[:, c, :], bank, mark, product_free[c])
                    product_free[c] = done
                    if c:
                        m = dve.do(lambda e: e.scalar_tensor_tensor(pr, pr, 0.5, product[:, :, :], ALU.mult, ALU.mult),
                                   state["silu2"], done)
                        product_free[:] = [m, m]
                        prod_free[slot] = split_act(pair, pr, m)
                    return done

                first = turned(gate, [pair], DK, xT, h_in, evict_gate)
                lead(h_pieces, first, 1)
                run(first)
                run(turned(up, [pair], DK, xT, h_in, evict_up))

            def square_pair(pair):
                slot = pair % 2
                cv, pr = conv[:, slot], prod[:, slot]

                def evict(tile, bank, mark):
                    c = tile % 2
                    done = summed(cv[:, c, :], bank, mark, prod_free[slot])
                    if c:
                        m = dve.do(lambda e: e.scalar_tensor_tensor(pr, cv, 0.0, cv, ALU.max, ALU.mult), done)
                        prod_free[slot] = split_act(pair, pr, m)
                    return done

                first = turned(up, [pair], DK, xT, h_in, evict)
                lead(h_pieces, first, 1)
                run(first)

            def down_phase(n, **last):
                a, b = phases[n]
                ready = [acts_ready[n, k] for k in range(b - a)]
                run(straight(down, range(4), b - a, act_hi[:, n % 2], act_lo[:, n % 2], ready, add_to_x(x_ready, **last),
                             k0=a, in0=0))
                down_read[n] = stream.used[stream.at - 1]

            for n, (a, b) in enumerate(phases):
                for pair in range(a // 2, b // 2):
                    (gate_pair if gate else square_pair)(pair)
                if n:
                    down_phase(n - 1)
            g_in = load(others_in, steps[:, :], bass.AP(tensor=dram[end_gain].tensor, offset=0, ap=[[0, P], [1, D]]),
                        f"{end_gain}_landed", prod_free)
            act.program.append(lambda e: e.preload_act_table_set(ROOTS))
            squared = []
            down_phase(len(phases) - 1, squared=squared, gained=(steps, g_in, h_nat, h_in, both))
            return [x_ready[-1], down_read[len(phases) - 1], squared], squared

        scope = ExitStack()
        block_free, x_squared = mlp(phases1, "w_gate", "w_up1", "w_down1", x_ready, x_squared, "ffn", block_free,
                                    xT_read, "final_gain_1", True, scope, "1")
        xT_read = stream.used[stream.at - 1]
        scope.close()

        scope = ExitStack()
        mixed = sbuf("mixed", [P, TT, MIX], F32, scope)
        q_idxT = sbuf("q_idxT", [P, 8, TOK], F32, scope)
        k_idxT = sbuf("k_idxT", [P, TOK], F32, scope)
        q_dT = sbuf("q_dT", [P, 8, TOK], F32, scope)
        k_dT = q_idxT
        tail = sbuf("tail", [P, TT, TAIL], F32, scope)
        c_q = sbuf("c_q", [P, TT, 512], F32, scope)
        staging = sbuf("staging", [P, TT, 1024], F32, scope)
        q_nT = sbuf("q_nT", [P, 8, TOK], F32, scope)
        k_nT = sbuf("k_nT", [P, 8, TOK], F32, scope)
        v_m = sbuf("v_m", [P, TT, 1024], F32, scope)
        q_rT = sbuf("q_rT", [P, 4, TOK], F32, scope)
        k_dup = sbuf("k_dup", [P, TT, P], F32, scope)
        cos = sbuf("cos", [P, TT, 32], F32, scope)
        sin = sbuf("sin", [P, TT, 32], F32, scope)
        angle = sbuf("angle", [P, TT, 32], F32, scope)
        rope_tmp = [sbuf(f"rope_tmp{i}", [P, TOK], F32, scope) for i in range(3)]
        pos = sbuf("pos", [P, TT], I32, scope)
        posf = sbuf("posf", [P, TT], F32, scope)
        index = sbuf("index", [P, 384], F32, scope)
        top8 = sbuf("top8", [P, TT, 8], F32, scope)
        krT = sbuf("krT", [P, TOK], F32, scope)
        b2 = softmax_buffers(scope, "a2_", TOK)
        low_rank = ExitStack()
        cT = sbuf("cT", [P, 6, 2, TOK], F32R, low_rank)
        cT_hi, cT_lo = cT[:, :, 0, :], cT[:, :, 1, :]
        low_rank.close()
        v_d = sbuf("v_d", [P, TT, 1024], F32, scope)

        pos_in = load(others_in, pos[:, :], dram["positions"], "pos_landed", block_free)

        def rope(view, heads, half, ready):
            step = 32 // half
            shape = [P, heads, half]
            ends = []
            t1, t2, t3 = (r[:, 0:heads * half].rearrange("p (h f) -> p h f", h=heads) for r in rope_tmp)
            for t in range(TT):
                x1, x2 = view[:, t, :, 0:half], view[:, t, :, half:2 * half]
                co = cos[:, t, 0:32:step].unsqueeze(1).to_broadcast(shape)
                si = sin[:, t, 0:32:step].unsqueeze(1).to_broadcast(shape)
                before = [rope.done, trig_ready, ready]
                a = dve.do(lambda e, x1=x1, co=co: e.tensor_tensor(t1, x1, co, ALU.mult), before)
                b = dve.do(lambda e, x2=x2, si=si: e.tensor_tensor(t2, x2, si, ALU.mult))
                c = dve.do(lambda e, x1=x1, si=si: e.tensor_tensor(t3, x1, si, ALU.mult))
                d = dve.do(lambda e, x2=x2, co=co: e.tensor_tensor(x2, x2, co, ALU.mult), b)
                a = dve.do(lambda e, x1=x1: e.tensor_tensor(x1, t1, t2, ALU.subtract), c)
                rope.done = dve.do(lambda e, x2=x2: e.tensor_tensor(x2, x2, t3, ALU.add), d)
                ends += [a, rope.done]
            return ends

        def turn_tiles(src, tiles, dst, ready, scale=1.0, free=None):
            marks = {}
            for pair in range((tiles + 1) // 2):
                n, bank = work_banks.take()
                here = range(2 * pair, min(2 * pair + 2, tiles))

                def issue(e, bank=bank, here=here):
                    for j, tile in enumerate(here):
                        for t in range(TT):
                            last = e.transpose(bank[:, j * TOK + t * P:j * TOK + (t + 1) * P],
                                               src[:, t, tile * P:(tile + 1) * P], const("ident"))
                    return last

                mark = pe.do(issue, ready, work_banks.free[n])
                w = len(here)
                done = act.do(lambda e, bank=bank, here=here, w=w: e.activation(
                    dst[:, here[0]:here[0] + w, :], bank[:, 0:w * TOK].rearrange("p (c t) -> p c t", c=w),
                    ACT.Copy, scale=scale), mark, free)
                work_banks.free[n] = done
                for tile in here:
                    marks[tile] = done
            turn_tiles.read = mark
            return marks

        def copy_out(dst, marks, free=None):
            def evict(c, t, bank, mark):
                view = dst(c, t)
                done = act.do(lambda e: e.activation(view, bank[:, 0:view.shape[1]], ACT.Copy), mark, free)
                marks.append(done)
                return done
            return evict

        h_in = [None] * DK
        h_pieces = normed_turned(mixed, TT, "mix", token_scales(x_squared, True), block_free, xT_read, h_in)
        tail_done = []
        product = straight("w_tail", [0], DK, xT_hi, xT_lo, h_in,
                           copy_out(lambda c, t: tail[:, t, :], tail_done, block_free), width=TAIL)
        lead(h_pieces, product, 2)
        run(product)
        x_ready = [dve.do(lambda e, t=t: e.tensor_scalar(x[:, t, :], x[:, t, :], stats[:, t:t + 1], None, ALU.mult),
                          h_in) for t in range(TT)]

        TWO_PI = (6.28125, 1.9350051879882812e-03, 3.0198694e-07)
        ROUND = 12582912.0
        a = dve.do(lambda e: e.tensor_copy(posf[:, :], pos[:, :]), pos_in, block_free)
        ang_ready = [dve.do(lambda e, t=t: e.tensor_scalar(angle[:, t, :], const("freq"), posf[:, t:t + 1], None,
                                                           ALU.mult), a) for t in range(TT)]
        trig_ready = []
        for dst, quarter in ((sin, 0.0), (cos, 0.25)):
            turns = rope_tmp[0][:, 0:64].rearrange("p (t f) -> p t f", t=TT)
            m = dve.do(lambda e, quarter=quarter: e.tensor_scalar(turns, angle[:, :, :], 0.15915494309189535, quarter,
                                                                  ALU.mult, ALU.add), ang_ready, trig_ready)
            m = dve.do(lambda e: e.tensor_scalar(turns, turns, ROUND, None, ALU.add), m)
            m = dve.do(lambda e: e.tensor_scalar(turns, turns, -ROUND, None, ALU.add), m)
            src = angle[:, :, :]
            for part in TWO_PI:
                m = dve.do(lambda e, src=src, part=part, dst=dst: e.scalar_tensor_tensor(
                    dst[:, :, :], turns, -part, src, ALU.mult, ALU.add), m)
                src = dst[:, :, :]
            if quarter:
                m = dve.do(lambda e: e.tensor_scalar(dst[:, :, :], dst[:, :, :], 1.5707963267948966, None, ALU.add), m)
            m = dve.do(lambda e, dst=dst: e.tensor_scalar(dst[:, :, :], dst[:, :, :], 3.1415925, -3.1415925,
                                                          ALU.min, ALU.max), m)
            trig_ready.append(act.do(lambda e, dst=dst: e.activation(dst[:, :, :], dst[:, :, :], ACT.Sin), m))

        rope.done = trig_ready

        k_r, k_i, w_i = (tail[:, :, a:b] for a, b in ((256, 320), (320, 384), (384, 400)))

        def project(chunks, buf, marks, free):
            return straight("w_in", chunks, DK, xT_hi, xT_lo, h_in,
                            copy_out(lambda c, t: buf[:, t, (c - chunks[0]) * 512:(c - chunks[0] + 1) * 512],
                                     marks, free))

        def rotated_key(src, half, free):
            done = rope(src.unsqueeze(2), 1, half, tail_done)
            return [dve.do(lambda e, j=j: e.tensor_copy(k_dup[:, :, j * 64:(j + 1) * 64], src), done, free)
                    for j in range(2)]

        m_cq, m_qi = [], []
        low = Filler(project([8], c_q, m_cq, block_free))
        key = rotated_key(k_i, 8, None)
        low_kv = k_nT[:, 0:2, :]
        c_kv = tail[:, :, 0:256]
        low.advance(3)
        k_idx_ready = turn_tiles(k_dup, 1, k_idxT[:, :].unsqueeze(1), key)[0]
        key = rotated_key(k_r, 32, turn_tiles.read)
        n_ckv = rms_scaled(c_kv, low_kv, 256, tail_done, block_free, 4)
        w_idx_ready = dve.do(lambda e: e.tensor_scalar(w_i, w_i, IDX_HEADS ** -0.5, None, ALU.mult), tail_done)
        low.advance(3)
        kr_ready = turn_tiles(k_dup, 1, krT[:, :].unsqueeze(1), key)[0]
        ckv_in = turn_and_split(low_kv, 2, "ckv", cT_hi, cT_lo, n_ckv, block_free, 4, 0)
        low.finish()
        low_q = q_nT[:, 0:4, :].rearrange("p (t a) c -> p t (a c)", t=TT)
        q_idx = Filler(project([0, 1], staging, m_qi, block_free))
        q_idx.advance(2)
        n_cq = rms_scaled(c_q, low_q, 512, m_cq, block_free, 2)
        q_idx.advance(3)
        cq_in = turn_and_split(low_q, 4, "cq", cT_hi, cT_lo, n_cq, block_free)
        q_idx.finish()

        index_of = (index[:, 0:P], index[:, P:384])
        relus = Slots([rope_tmp[i][:, 0:TOK] for i in range(3)])
        index_ready = [None, None]
        q_idx_ready = {}
        idx_items = [dict(h=h, t=t) for h in range(IDX_HEADS) for t in range(TT)]

        def idx_scores(item, i):
            h, t = item["h"], item["t"]
            W, _ = token_tile(t)
            rows = slice(64 * (h % 2), 64 * (h % 2) + 64)
            n, bank = work_banks.take()
            mark = pe.do(lambda e: e.matmul(bank[:, 0:W], q_idxT[rows, h // 2, t * P:(t + 1) * P], k_idxT[rows, 0:W],
                                            start=True, stop=True),
                         q_idx_ready[h // 2], k_idx_ready, work_banks.free[n])
            slot, r = relus.of(i)
            relu = act.do(lambda e: e.activation(r[:, 0:W], bank[:, 0:W], ACT.Relu, scale=64 ** -0.5),
                          mark, relus.free[slot])
            work_banks.free[n] = relu
            item["r"], item["relu"], item["slot"], item["mark"] = r, relu, slot, mark

        def idx_add(item, i):
            h, t, r = item["h"], item["t"], item["r"]
            W, _ = token_tile(t)
            w = tail[:, t, 384 + h:385 + h]
            if h == 0:
                a = dve.do(lambda e: e.tensor_scalar(index_of[t], r[:, 0:W], w, None, ALU.mult),
                           item["relu"], w_idx_ready, block_free)
            else:
                a = dve.do(lambda e: e.scalar_tensor_tensor(index_of[t], r[:, 0:W], w, index_of[t],
                                                            ALU.mult, ALU.add), item["relu"], index_ready[t])
            index_ready[t] = a
            relus.free[item["slot"]] = item["added"] = a

        q_ready2, k_ready2 = {}, {}

        def evict_tiles(dst, marks, free, scale=1.0):
            def evict(tile, bank, mark):
                marks[tile] = summed(dst[:, tile, :], bank, mark, free, scale)
                return marks[tile]
            return evict

        m_qr, m_vm = [], []
        q_rope = c_q
        ckv_hi, ckv_lo = cT_hi[:, 4:6, :], cT_lo[:, 4:6, :]
        expand = Filler(
            turned("w_qnope", range(4), 4, cT, cq_in, evict_tiles(q_nT, q_ready2, cq_in, -192 ** -0.5)),
            straight("w_qrope", [0], 4, cT_hi, cT_lo, cq_in, copy_out(lambda c, t: q_rope[:, t, :], m_qr, n_cq)),
            turned("w_knope", range(4), 2, cT[:, 4:6], ckv_in[4:6], evict_tiles(k_nT, k_ready2, ckv_in)),
            straight("w_vmla", range(2), 2, ckv_hi, ckv_lo, ckv_in[4:6],
                     copy_out(lambda c, t: v_m[:, t, c * 512:(c + 1) * 512], m_vm, block_free)))
        r = rope(staging[:, :, :].rearrange("p t (h d) -> p t h d", d=64), IDX_HEADS, 8, m_qi)
        relus.free = [rope.done] * 3
        expand.advance(3)
        q_idx_ready.update(turn_tiles(staging, 8, q_idxT, r))
        staging_free = turn_tiles.read
        pipeline(idx_items, [(1, idx_add), FILL, (0, idx_scores)], expand, 0.25)
        expand.finish()
        expanded = stream.used[stream.at - 1]
        r = rope(q_rope[:, :, :].rearrange("p t (h d) -> p t h d", d=64), 8, 32, [m_qr, idx_items[-1]["added"]])
        m_qd, m_kd, m_vd = [], [], []
        rest = Filler(project([2, 3], staging, m_qd, staging_free))
        rest.advance(3)
        q_r_ready = turn_tiles(q_rope, 4, q_rT, r, -192 ** -0.5, block_free)

        for t in range(TT):
            W, m0 = token_tile(t)
            index_ready[t] = dve.do(lambda e, t=t, m0=m0, W=W: e.tensor_tensor(
                index_of[t], index_of[t], const("mask")[:, m0:m0 + W], ALU.add), index_ready[t])

        def select_round():
            best = [dve.do(lambda e, t=t: e.max(top8[:, t, :], index_of[t]), index_ready[t]) for t in range(TT)]
            for t in range(TT):
                index_ready[t] = dve.do(lambda e, t=t: e.match_replace(index_of[t], top8[:, t, :], index_of[t],
                                                                       TAKEN), best[t])

        for _ in range(TOPK // 8):
            select_round()
            rest.advance(1)
        rest.finish()
        select_ready = [dve.do(lambda e, t=t: e.tensor_scalar(index_of[t], index_of[t], TAKEN / 2, -NEG,
                                                              ALU.is_ge, ALU.mult), index_ready[t])
                        for t in range(TT)]
        r = rope(staging[:, :, :].rearrange("p t (h d) -> p t h d", d=P), 8, 16, m_qd)
        k_d_ready = {}
        rotated = []

        def rotate_k_d():
            rotated.extend(rope(staging[:, :, :].rearrange("p t (h d) -> p t h d", d=P), 8, 16, m_kd))
            yield

        def turn_k_d():
            k_d_ready.update(turn_tiles(staging, 8, k_dT, rotated, free=idx_items[-1]["mark"]))
            yield

        staging_read = []
        rest = Filler(project([4, 5], staging, m_kd, staging_read), rotate_k_d(),
                      project([6], v_d[:, :, 0:512], m_vd, [block_free, expanded]), turn_k_d(),
                      project([7], v_d[:, :, 512:1024], m_vd, [block_free, expanded]))
        rest.advance(3)
        q_d_ready = turn_tiles(staging, 8, q_dT, r, -P ** -0.5)
        staging_read.append(turn_tiles.read)
        act.program.append(lambda e: e.preload_act_table_set(EXPS))

        mla_items = []
        for h in range(NH):
            for t in range(TT):
                W, m0 = token_tile(t)
                rows = slice(64 * (h % 2), 64 * (h % 2) + 64)

                def scores(e, bank, t=t, W=W, h=h, rows=rows):
                    e.matmul(bank[:, 0:W], q_nT[:, h, t * P:(t + 1) * P], k_nT[:, h, 0:W], start=True, stop=False)
                    return e.matmul(bank[:, 0:W], q_rT[rows, h // 2, t * P:(t + 1) * P], krT[rows, 0:W],
                                    start=False, stop=True)

                mla_items.append(dict(
                    W=W, width=P, kind="masked", mask=const("blocked")[:, m0:m0 + W], mask_ready=None,
                    scores=scores, ready=lambda h=h: [q_ready2[h], k_ready2[h], q_r_ready[h // 2], kr_ready],
                    v=lambda k, h=h: v_m[:, k, h * P:(h + 1) * P], v_ready=lambda: m_vm,
                    out=mixed[:, t, h * P:(h + 1) * P], out_free=h_in))
        pipeline(mla_items, softmax_stages(b2), rest, 1.5)
        rest.finish()
        xT_read = stream.used[stream.at - 1]
        m_in = turn_and_split(mixed, 8, None, xT_hi, xT_lo, mla_items[-1]["done"], xT_read)
        out_early = Filler(straight("w_out", range(4), 8, xT_hi, xT_lo, m_in, add_to_x(x_ready)))

        dsa_items = []
        for h in range(NH):
            for t in range(TT):
                W, _ = token_tile(t)
                dsa_items.append(dict(
                    W=W, width=P, kind="masked", mask=index_of[t], mask_ready=select_ready[t],
                    scores=lambda e, bank, t=t, W=W, h=h: e.matmul(
                        bank[:, 0:W], q_dT[:, h, t * P:(t + 1) * P], k_dT[:, h, 0:W], start=True, stop=True),
                    ready=lambda h=h: [q_d_ready[h], k_d_ready[h]],
                    v=lambda k, h=h: v_d[:, k, h * P:(h + 1) * P], v_ready=lambda: m_vd,
                    out=mixed[:, t, 1024 + h * P:1024 + (h + 1) * P], out_free=h_in))
        pipeline(dsa_items, softmax_stages(b2), out_early, 0.65)
        out_early.advance(1)

        m_in2 = turn_and_split(mixed, 8, None, xT_hi, xT_lo, dsa_items[-1]["done"], xT_read, 8)
        out_early.finish()
        x_squared = []
        out_late = Filler(straight("w_out", range(4), 8, xT_hi, xT_lo, m_in2, add_to_x(x_ready, x_squared), k0=8))
        block_free = [m_in, m_in2, select_ready, dsa_items[-1]["done"]]
        scope.close()

        scope = ExitStack()
        mT = sbuf("mT", [P, DK, 2, TOK], F32R, scope)
        mT_hi, mT_lo = mT[:, :, 0, :], mT[:, :, 1, :]
        mem = sbuf("mem", [P, TT, D], F32, scope)
        kxT = sbuf("kxT", [P, 4, TOK], F32, scope)
        qxT = sbuf("qxT", [P, 4, TOK], F32, scope)
        v_x = sbuf("v_x", [P, TT, 512], F32, scope)
        o_x = sbuf("o_x", [P, TT, 512], F32, scope)
        h_x = sbuf("h_x", [P, TT, D], F32, scope)
        b3 = softmax_buffers(scope, "a3_", TOK)
        mem_in = load(others_in, mem[:, :, :], dram["mem"].rearrange("(t p) d -> p t d", p=P), "mem_landed",
                      block_free)
        out_late.advance(8)
        act.program.append(lambda e: e.preload_act_table_set(ROOTS))
        n_mem = rms_scaled(mem, h_x, D, mem_in, block_free, 2)
        out_late.advance(3)
        mem_T = []
        for kt in range(0, DK, 4):
            mem_T += turn_and_split(h_x, 4, "mem", mT_hi, mT_lo, n_mem, block_free, kt)[kt:]
            out_late.advance(1)
        out_late.finish()
        xT_read = stream.used[stream.at - 1]
        kx_ready, qx_ready, vx_ready = {}, {}, []
        h_in = [None] * DK
        h_pieces = normed_turned(h_x, 0, "cross", token_scales(x_squared), mem_T, xT_read, h_in)
        product = turned("w_kx", range(2), DK, mT, mem_T, evict_tiles(kxT, kx_ready, block_free))
        for _ in range(2):
            next(product)
        lead(h_pieces, product, 1)
        run(product)
        run(turned("w_qx", range(2), DK, xT, h_in, evict_tiles(qxT, qx_ready, block_free, P ** -0.5)))
        xT_read = stream.used[stream.at - 1]
        act.program.append(lambda e: e.preload_act_table_set(EXPS))
        values = Filler(straight("w_vx", [0], DK, mT_hi, mT_lo, mem_T,
                                 copy_out(lambda c, t: v_x[:, t, :], vx_ready, block_free)))
        x_items = []
        for h in range(4):
            for t in range(TT):
                x_items.append(dict(
                    W=TOK, width=P, kind="open",
                    scores=lambda e, bank, t=t, h=h: e.matmul(
                        bank[:, 0:TOK], qxT[:, h, t * P:(t + 1) * P], kxT[:, h, :], start=True, stop=True),
                    ready=lambda h=h: [qx_ready[h], kx_ready[h]],
                    v=lambda k, h=h: v_x[:, k, h * P:(h + 1) * P], v_ready=lambda: vx_ready,
                    out=o_x[:, t, h * P:(h + 1) * P], out_free=block_free))
        value_of_head = values_stage(b3)

        def values_late(item, i):
            values.finish()
            value_of_head(item, i)

        pipeline(x_items, softmax_stages(b3, values_late), values, 3)
        mem_read = stream.used[stream.at - 1]
        o_in = turn_and_split(o_x, 4, None, xT_hi, xT_lo, x_items[-1]["done"], xT_read)
        act.program.append(lambda e: e.preload_act_table_set(ROOTS))
        x_squared = []
        run(straight("w_ox", range(4), 4, xT_hi, xT_lo, o_in, add_to_x(x_ready, x_squared)))
        xT_read = stream.used[stream.at - 1]
        block_free = [o_in, mem_read, h_in, x_items[-1]["done"]]
        scope.close()

        scope = ExitStack()
        block_free, x_squared = mlp(phases2, None, "w_up2", "w_down2", x_ready, x_squared, "mlp", block_free,
                                    xT_read, "final_gain", False, scope, "2")
        scope.close()

        assert stream.at == len(plan)
        scale = token_scales(x_squared)
        stored = ctx.enter_context(nc.semaphore("stored"))
        half = D // 2
        for c in range(2):
            cols = slice(c * half, (c + 1) * half)
            ends = [dve.do(lambda e, cols=cols: e.tensor_scalar(x[:, 0, cols], x[:, 0, cols], stats[:, 0:1], None,
                                                                ALU.mult), scale),
                    act.do(lambda e, cols=cols: e.activation(x[:, 1, cols], x[:, 1, cols], ACT.Copy,
                                                             scale=stats[:, 1:2]), scale)]
            for t in range(TT):
                weights_in.wait(ends[t])
                weights_in.program.append(lambda e, t=t, cols=cols: e.dma_start(
                    out_dram[t * P:(t + 1) * P, cols], x[:, t, cols]).then_inc(stored, 16))
        weights_in.wait((stored, 16 * 2 * TT))

        block = ctx.enter_context(nc.Block())

        @block.sync
        def _(e):
            weights_in.run(e)

        @block.gpsimd
        def _(e):
            others_in.run(e)

        @block.scalar
        def _(e):
            act.run(e)

        @block.vector
        def _(e):
            dve.run(e)

        @block.tensor
        def _(e):
            pe.run(e)


def lay_turned(w):
    k, c = w.shape
    per = min(4, k // P)
    return np.ascontiguousarray(w.reshape(k // P // per, per, P, c // TURNED_COLS, TURNED_COLS).transpose(3, 0, 2, 1, 4))


def lay_straight(w, width=STRAIGHT_COLS):
    k, c = w.shape
    return np.ascontiguousarray(w.reshape(k // P // 2, 2, P, c // width, width).transpose(3, 0, 2, 1, 4))


def lay_gain(g):
    return g.reshape(-1, P).T


def constants():
    i = np.arange(P)
    q = P + i[:, None]
    k = np.arange(TOK)[None, :]
    mask = np.where(k // CHUNK <= q // CHUNK, 0.0, NEG)
    parts = {
        "ident": np.eye(P), "flip": np.eye(P)[::-1],
        "after": i[:, None] > i[None, :],
        "causal": i[:, None] < i[None, :],
        "ones": np.ones((P, P)),
        "mask": mask, "blocked": -mask,
        "dist": np.where(mask == 0.0, -np.abs(q - k), NEG),
        "half": np.full((P, 1), 0.5), "eighth": np.full((P, 1), 0.125), "less_eighth": np.full((P, 1), -0.125),
        "freq": np.broadcast_to(np.float32(500000.0) ** (-np.arange(32, dtype=np.float32) / np.float32(32)), (P, 32)),
    }
    return np.ascontiguousarray(np.concatenate([parts[n].astype(np.float32) for n, _ in CONSTS], axis=1))


def kernel(**inputs):
    import concourse.bacc as bacc
    from concourse.bass_utils import run_bass_kernel_spmd

    i = {k: np.asarray(v) for k, v in inputs.items()}
    qkv, w_in = i["w_qkv"][0], i["w_in_2"][0]
    qb = i["w_qb_2"][0].reshape(512, 8, 192)
    kvb = i["w_kvb_2"][0].reshape(256, 8, 256)
    gains = {
        "attn": i["attn_norm"][0], "ffn": i["ffn_norm"][0],
        "y1": np.concatenate([np.tile(i["diff_subln"][0], NH), i["sb_norm"][0].ravel(), i["ch_norm"][0].ravel()]),
        "conv0": i["conv_w"][0, 0], "conv1": i["conv_w"][0, 1], "conv2": i["conv_w"][0, 2], "convb": i["conv_b"][0],
        "mix": i["g_mix_2"][0], "cq": i["g_cq_2"][0], "ckv": i["g_ckv_2"][0], "cross": i["g_cross_2"][0],
        "mem": i["g_mem_2"][0], "mlp": i["g_mlp_2"][0],
    }
    arrays = {
        "x": i["x"][0], "mem": i["mem_2"][0],
        "consts": constants(),
        "gains": np.concatenate([lay_gain(gains[n]) for n, _ in GAINS], axis=1),
        "lambdas": np.concatenate([i["lambda_q1"], i["lambda_k1"], i["lambda_q2"], i["lambda_k2"]]),
        "rel_rev": i["rel_bias"][0][:, ::-1],
        "positions": i["positions_2"][0].reshape(TT, P).T,
        "final_gain_1": i["final_norm"], "final_gain": i["g_final_2"],
        "w_qk": lay_turned(np.concatenate([qkv[:, 0:2048], qkv[:, 3072:4096], qkv[:, 4608:5632]], axis=1)),
        "w_v": lay_straight(np.concatenate([qkv[:, 2048:3072], qkv[:, 4096:4608], qkv[:, 5632:6144]], axis=1)),
        "w_o": lay_straight(i["w_o"][0]),
        "w_gate": lay_turned(i["w_gate"][0]), "w_up1": lay_turned(i["w_up"][0]),
        "w_down1": lay_straight(i["w_down"][0]),
        "w_tail": lay_straight(np.concatenate([w_in[:, C_KV:Q_D], w_in[:, K_IDX:]], axis=1), TAIL),
        "w_in": lay_straight(np.concatenate([w_in[:, Q_IDX:K_IDX], w_in[:, Q_D:Q_IDX], w_in[:, C_Q:C_KV]], axis=1)),
        "w_qnope": lay_turned(qb[:, :, 0:P].reshape(512, 1024)),
        "w_qrope": lay_straight(qb[:, :, P:].reshape(512, 512)),
        "w_knope": lay_turned(kvb[:, :, 0:P].reshape(256, 1024)),
        "w_vmla": lay_straight(kvb[:, :, P:].reshape(256, 1024)),
        "w_out": lay_straight(i["w_out_2"][0]),
        "w_qx": lay_turned(i["w_q_cross_2"][0]), "w_kx": lay_turned(i["w_k_cross_2"][0]),
        "w_vx": lay_straight(i["w_v_cross_2"][0]), "w_ox": lay_straight(i["w_o_cross_2"][0]),
        "w_up2": lay_turned(i["w_up_2"][0]), "w_down2": lay_straight(i["w_down_2"][0]),
    }
    nc = bacc.Bacc("TRN2", target_bir_lowering=False, num_devices=1)
    arrays = {f"in_{n}": np.ascontiguousarray(a) for n, a in arrays.items()}
    dram = {n[3:]: nc.dram_tensor(n, a.shape, mybir.dt.from_np(a.dtype), kind="ExternalInput").ap()
            for n, a in arrays.items()}
    out = nc.dram_tensor("out", (TOK, D), F32, kind="ExternalOutput").ap()
    build_program(nc, dram, out)
    r = run_bass_kernel_spmd(nc, [arrays], core_ids=[0])
    return r.results[0]["out"].reshape(1, TOK, D)
```
